# Optimizing a Trainium2 kernel written in Bass

```python
import jax, jax.numpy as jnp
from jax import lax
import numpy as np

D_MODEL = 1024
BATCH = 1
SEQ = 2048
DEPTH = 1

GRID_W = 64
CTX_LEN = 256
RWKV_HEADS = 8
RWKV_HEAD_DIM = 64
D_RWKV = RWKV_HEADS * RWKV_HEAD_DIM
W_RANK = 64
A_RANK = 64
G_RANK = 128
GN_EPS = 64e-5
CHUNK = 128
SG_GROUPS = 4
SG_GROUP_DIM = 128
D_SG = SG_GROUPS * SG_GROUP_DIM
P_A = 3 * D_RWKV + 2 * W_RANK + 2 * A_RANK + G_RANK
W_IN_COLS = P_A + 2 * D_SG + 2 * D_MODEL
RWKV_SPLITS = (D_RWKV, 2 * D_RWKV, 3 * D_RWKV, 3 * D_RWKV + 2 * W_RANK, 3 * D_RWKV + 2 * W_RANK + 2 * A_RANK)
N_GROUPS = 4
EXPERTS_PER_GROUP = 8
N_EXPERTS = N_GROUPS * EXPERTS_PER_GROUP
TOP_K_IN_GROUP = 2
D_EXPERT = 512
MOE_BLOCK = 128
NORM_EPS = 1e-6

kernel_name = "hybrid_rwkv7_chunkgmlp_hmoe_dit"

def rms_norm(x, g):
    xf = x.astype(jnp.float32)
    y = xf * lax.rsqrt(jnp.mean(xf * xf, axis=-1, keepdims=True) + NORM_EPS)
    return (y * g).astype(x.dtype)

def layer_norm(x, w, b):
    xf = x.astype(jnp.float32)
    mu = jnp.mean(xf, axis=-1, keepdims=True)
    var = jnp.mean((xf - mu) ** 2, axis=-1, keepdims=True)
    return ((xf - mu) * lax.rsqrt(var + 1e-5) * w + b).astype(x.dtype)

def modulate(h, shift, scale):
    return h * (1.0 + scale[:, None, :]) + shift[:, None, :]

def grid_shift(z, rows):
    B, L, C = z.shape
    zq = z.reshape(B, rows, GRID_W, C // 4, 4)
    left = jnp.pad(zq[:, :, :-1, :, 0], ((0, 0), (0, 0), (1, 0), (0, 0)))
    right = jnp.pad(zq[:, :, 1:, :, 1], ((0, 0), (0, 0), (0, 1), (0, 0)))
    up = jnp.pad(zq[:, :-1, :, :, 2], ((0, 0), (1, 0), (0, 0), (0, 0)))
    down = jnp.pad(zq[:, 1:, :, :, 3], ((0, 0), (0, 1), (0, 0), (0, 0)))
    return jnp.stack([left, right, up, down], axis=-1).reshape(B, L, C)

def seq_shift(z):
    B, L, C = z.shape
    zq = z.reshape(B, L, C // 2, 2)
    prev = jnp.pad(zq[:, :-1, :, 0], ((0, 0), (1, 0), (0, 0)))
    nxt = jnp.pad(zq[:, 1:, :, 1], ((0, 0), (0, 1), (0, 0)))
    return jnp.stack([prev, nxt], axis=-1).reshape(B, L, C)

def dir_major(t_fwd, t_bwd):
    B, L, _ = t_fwd.shape
    t = jnp.stack([t_fwd, jnp.flip(t_bwd, axis=1)], axis=0).astype(jnp.float32)
    return jnp.transpose(t.reshape(2, B, L, RWKV_HEADS, RWKV_HEAD_DIM), (2, 0, 1, 3, 4))

def rwkv_prepare(zA, w0, w_up, a0, a_up, g_up, k_k, k_a):
    B, L, _ = zA.shape
    r, k, v, wd, ad, gd = jnp.split(zA, RWKV_SPLITS, axis=-1)
    wd = jnp.tanh(wd).reshape(B, L, 2, W_RANK)
    ad = ad.reshape(B, L, 2, A_RANK)
    w = -jax.nn.softplus(-(w0 + jnp.einsum('bldr,drc->bldc', wd, w_up))) - 0.5
    decay = jnp.exp(-jnp.exp(w.astype(jnp.float32)))
    a = jax.nn.sigmoid(a0 + jnp.einsum('bldr,drc->bldc', ad, a_up))
    g = jax.nn.sigmoid(gd) @ g_up
    kk = (k * k_k).astype(jnp.float32).reshape(B, L, RWKV_HEADS, RWKV_HEAD_DIM)
    kk = kk / jnp.maximum(jnp.sqrt(jnp.sum(kk * kk, axis=-1, keepdims=True)), 1e-12)
    kk = kk.reshape(B, L, D_RWKV)
    k_dir = k[:, :, None, :] * (1.0 + (a - 1.0) * k_a)
    a32 = a.astype(jnp.float32)
    scan_in = (dir_major(r, r),
               dir_major(decay[:, :, 0], decay[:, :, 1]),
               dir_major(k_dir[:, :, 0], k_dir[:, :, 1]),
               dir_major(v, v),
               dir_major(kk, kk),
               dir_major(kk * a32[:, :, 0], kk * a32[:, :, 1]))
    return scan_in, r, k, v, g

def rwkv_step(S, inp):
    r, w, k, v, kk, kka = inp
    sa = jnp.einsum('dbhvk,dbhk->dbhv', S, kk)
    S = S * w[..., None, :] - sa[..., :, None] * kka[..., None, :] + v[..., :, None] * k[..., None, :]
    y = jnp.einsum('dbhvk,dbhk->dbhv', S, r)
    return S, y

def rwkv_scan(scan_in, S0):
    S_fin, ys = lax.scan(rwkv_step, S0, scan_in)
    y = ys[:, 0] + jnp.flip(ys[:, 1], axis=0)
    return S_fin, jnp.transpose(y, (1, 0, 2, 3))

def rwkv_output(y, r, k, v, g, r_k, ln_w, ln_b):
    B, L, H, N = y.shape
    mu = jnp.mean(y, axis=-1, keepdims=True)
    var = jnp.mean((y - mu) ** 2, axis=-1, keepdims=True)
    yn = ((y - mu) * lax.rsqrt(var + GN_EPS)).reshape(B, L, D_RWKV) * ln_w + ln_b
    rh = r.reshape(B, L, H, N)
    kh = k.reshape(B, L, H, N)
    vh = v.reshape(B, L, H, N)
    bonus = (jnp.sum(rh * kh * r_k, axis=-1, keepdims=True) * vh).reshape(B, L, D_RWKV)
    return (yn.astype(r.dtype) + bonus) * g

def chunk_gating(zB, ln_w, ln_b, sg_w, sg_b):
    B, L, _ = zB.shape
    u, v = jnp.split(jax.nn.gelu(zB), 2, axis=-1)
    v = layer_norm(v, ln_w, ln_b).reshape(B, L // CHUNK, CHUNK, SG_GROUPS, SG_GROUP_DIM)
    s = jnp.einsum('gpq,bnqgc->bnpgc', sg_w, v) + jnp.transpose(sg_b)[:, :, None]
    return u * s.reshape(B, L, D_SG)

def mixer_stream(h, shift_fn, S0, need_output, params):
    (w_in, mu, w0, w_up, a0, a_up, g_up, k_k, k_a, r_k, ln_w, ln_b,
     w_branch_a, sg_ln_w, sg_ln_b, sg_w, sg_b, w_branch_b, w_out) = params
    z = h @ (w_in if need_output else w_in[:, :P_A])
    zA = z[..., :P_A]
    zA = zA + mu * (shift_fn(zA) - zA)
    scan_in, r, k, v, g = rwkv_prepare(zA, w0, w_up, a0, a_up, g_up, k_k, k_a)
    S_fin, y = rwkv_scan(scan_in, S0)
    if not need_output:
        return None, S_fin
    zB = z[..., P_A:P_A + 2 * D_SG]
    gate_a, gate_b = jnp.split(jax.nn.sigmoid(z[..., P_A + 2 * D_SG:]), 2, axis=-1)
    y_a = rwkv_output(y, r, k, v, g, r_k, ln_w, ln_b) @ w_branch_a
    y_b = chunk_gating(zB, sg_ln_w, sg_ln_b, sg_w, sg_b) @ w_branch_b
    return (gate_a * y_a + gate_b * y_b) @ w_out, S_fin

def hier_moe(h, grp_w, grp_b, exp_w, exp_b, w_gate, w_up, w_down):
    B, L, D = h.shape
    T = B * L
    xt = h.reshape(T, D)
    tok = jnp.arange(T)
    grp_logits = (xt @ grp_w + grp_b).astype(jnp.float32)
    grp = jnp.argmax(grp_logits, axis=-1)
    p_grp = jax.nn.softmax(grp_logits, axis=-1)[tok, grp]
    exp_logits = (xt @ exp_w + exp_b).astype(jnp.float32).reshape(T, N_GROUPS, EXPERTS_PER_GROUP)
    top_val, top_idx = lax.top_k(exp_logits[tok, grp], TOP_K_IN_GROUP)
    top_w = jax.nn.softmax(top_val, axis=-1) * p_grp[:, None]
    expert = grp[:, None] * EXPERTS_PER_GROUP + top_idx
    A = T * TOP_K_IN_GROUP
    flat_e = expert.reshape(A).astype(jnp.int32)
    flat_tok = jnp.repeat(tok, TOP_K_IN_GROUP).astype(jnp.int32)
    flat_w = top_w.reshape(A)
    order = jnp.argsort(flat_e)
    e_s, tok_s, w_s = flat_e[order], flat_tok[order], flat_w[order]
    counts = jax.ops.segment_sum(jnp.ones((A,), jnp.int32), flat_e, num_segments=N_EXPERTS)
    start = jnp.cumsum(counts) - counts
    padded = ((counts + MOE_BLOCK - 1) // MOE_BLOCK) * MOE_BLOCK
    pend = jnp.cumsum(padded)
    pstart = pend - padded
    dest = pstart[e_s] + (jnp.arange(A, dtype=jnp.int32) - start[e_s])
    P = ((A + MOE_BLOCK - 1) // MOE_BLOCK) * MOE_BLOCK + N_EXPERTS * MOE_BLOCK
    n_blocks = P // MOE_BLOCK
    row_tok = jnp.full((P,), T, jnp.int32).at[dest].set(tok_s)
    row_w = jnp.zeros((P,), jnp.float32).at[dest].set(w_s)
    block_expert = jnp.minimum(jnp.searchsorted(pend, jnp.arange(n_blocks) * MOE_BLOCK, side='right'),
                               N_EXPERTS - 1)
    x_pad = jnp.concatenate([xt, jnp.zeros((1, D), xt.dtype)], axis=0)
    rows = x_pad[row_tok].reshape(n_blocks, MOE_BLOCK, D)

    def expert_block(args):
        xb, e = args
        hb = jax.nn.silu(xb @ w_gate[e]) * (xb @ w_up[e])
        return hb @ w_down[e]

    out = lax.map(expert_block, (rows, block_expert)).reshape(P, D)
    out = out * row_w[:, None].astype(out.dtype)
    y = jax.ops.segment_sum(out, row_tok, num_segments=T + 1)[:T]
    return y.reshape(B, L, D)

def setup_inputs(seed: int = 0) -> dict:
    key = jax.random.key(seed)
    ks = jax.random.split(key, 40)
    f32 = jnp.float32

    def nrm(k, shape, scale):
        return scale * jax.random.normal(k, shape, f32)

    Dp = DEPTH
    return {
        "x": nrm(ks[0], (BATCH, SEQ, D_MODEL), 1.0),
        "c": nrm(ks[1], (BATCH, D_MODEL), 1.0),
        "ctx": nrm(ks[2], (BATCH, CTX_LEN, D_MODEL), 1.0),
        "c_ctx": nrm(ks[3], (D_MODEL,), 1.0),
        "ada_w": nrm(ks[4], (Dp, D_MODEL, 6 * D_MODEL), 0.5 * D_MODEL ** -0.5),
        "ada_b": nrm(ks[5], (Dp, 6 * D_MODEL), 0.01),
        "norm1_g": 1.0 + nrm(ks[6], (Dp, D_MODEL), 0.02),
        "norm2_g": 1.0 + nrm(ks[7], (Dp, D_MODEL), 0.02),
        "w_in": nrm(ks[8], (Dp, D_MODEL, W_IN_COLS), D_MODEL ** -0.5),
        "shift_mu": jax.random.uniform(ks[9], (Dp, P_A), f32, 0.2, 0.8),
        "rwkv_w0": jax.random.uniform(ks[10], (Dp, 2, D_RWKV), f32, -6.5, -1.5),
        "rwkv_w_up": nrm(ks[11], (Dp, 2, W_RANK, D_RWKV), 0.1),
        "rwkv_a0": nrm(ks[12], (Dp, 2, D_RWKV), 0.1),
        "rwkv_a_up": nrm(ks[13], (Dp, 2, A_RANK, D_RWKV), 0.1),
        "rwkv_g_up": nrm(ks[14], (Dp, G_RANK, D_RWKV), G_RANK ** -0.5),
        "rwkv_k_k": 0.85 + nrm(ks[15], (Dp, D_RWKV), 0.02),
        "rwkv_k_a": 1.0 + nrm(ks[16], (Dp, D_RWKV), 0.02),
        "rwkv_r_k": nrm(ks[17], (Dp, RWKV_HEADS, RWKV_HEAD_DIM), 0.1),
        "rwkv_ln_w": 1.0 + nrm(ks[18], (Dp, D_RWKV), 0.02),
        "rwkv_ln_b": nrm(ks[19], (Dp, D_RWKV), 0.01),
        "w_branch_a": nrm(ks[20], (Dp, D_RWKV, D_MODEL), D_RWKV ** -0.5),
        "sg_ln_w": 1.0 + nrm(ks[21], (Dp, D_SG), 0.02),
        "sg_ln_b": nrm(ks[22], (Dp, D_SG), 0.01),
        "sg_w": nrm(ks[23], (Dp, SG_GROUPS, CHUNK, CHUNK), CHUNK ** -0.5),
        "sg_b": 1.0 + nrm(ks[24], (Dp, SG_GROUPS, CHUNK), 0.02),
        "w_branch_b": nrm(ks[25], (Dp, D_SG, D_MODEL), D_SG ** -0.5),
        "w_out": nrm(ks[26], (Dp, D_MODEL, D_MODEL), D_MODEL ** -0.5),
        "moe_grp_w": nrm(ks[27], (Dp, D_MODEL, N_GROUPS), D_MODEL ** -0.5),
        "moe_grp_b": nrm(ks[28], (Dp, N_GROUPS), 0.01),
        "moe_exp_w": nrm(ks[29], (Dp, D_MODEL, N_EXPERTS), D_MODEL ** -0.5),
        "moe_exp_b": nrm(ks[30], (Dp, N_EXPERTS), 0.01),
        "moe_w_gate": nrm(ks[31], (Dp, N_EXPERTS, D_MODEL, D_EXPERT), D_MODEL ** -0.5),
        "moe_w_up": nrm(ks[32], (Dp, N_EXPERTS, D_MODEL, D_EXPERT), D_MODEL ** -0.5),
        "moe_w_down": nrm(ks[33], (Dp, N_EXPERTS, D_EXPERT, D_MODEL), D_EXPERT ** -0.5),
        "final_norm_g": 1.0 + nrm(ks[34], (D_MODEL,), 0.02),
    }

def reference(x, c, ctx, c_ctx, ada_w, ada_b, norm1_g, norm2_g, w_in, shift_mu,
              rwkv_w0, rwkv_w_up, rwkv_a0, rwkv_a_up, rwkv_g_up, rwkv_k_k, rwkv_k_a, rwkv_r_k,
              rwkv_ln_w, rwkv_ln_b, w_branch_a, sg_ln_w, sg_ln_b, sg_w, sg_b, w_branch_b, w_out,
              moe_grp_w, moe_grp_b, moe_exp_w, moe_exp_b, moe_w_gate, moe_w_up, moe_w_down,
              final_norm_g):
    rows = x.shape[1] // GRID_W
    lat_shift = lambda z: grid_shift(z, rows)
    xc = ctx
    for layer in range(DEPTH):
        need_ctx = layer + 1 < DEPTH
        params = (w_in[layer], shift_mu[layer], rwkv_w0[layer], rwkv_w_up[layer], rwkv_a0[layer],
                  rwkv_a_up[layer], rwkv_g_up[layer], rwkv_k_k[layer], rwkv_k_a[layer], rwkv_r_k[layer],
                  rwkv_ln_w[layer], rwkv_ln_b[layer], w_branch_a[layer], sg_ln_w[layer], sg_ln_b[layer],
                  sg_w[layer], sg_b[layer], w_branch_b[layer], w_out[layer])
        moe_params = (moe_grp_w[layer], moe_grp_b[layer], moe_exp_w[layer], moe_exp_b[layer],
                      moe_w_gate[layer], moe_w_up[layer], moe_w_down[layer])
        mod = jax.nn.silu(c) @ ada_w[layer] + ada_b[layer]
        mod_c = jax.nn.silu(c_ctx)[None] @ ada_w[layer] + ada_b[layer]
        sh1, sc1, gt1, sh2, sc2, gt2 = jnp.split(mod, 6, axis=-1)
        csh1, csc1, cgt1, csh2, csc2, cgt2 = jnp.split(mod_c, 6, axis=-1)
        h_c = modulate(rms_norm(xc, norm1_g[layer]), csh1, csc1)
        s0 = jnp.zeros((2, xc.shape[0], RWKV_HEADS, RWKV_HEAD_DIM, RWKV_HEAD_DIM), jnp.float32)
        out_c, s_ctx = mixer_stream(h_c, seq_shift, s0, need_ctx, params)
        h = modulate(rms_norm(x, norm1_g[layer]), sh1, sc1)
        out, _ = mixer_stream(h, lat_shift, s_ctx, True, params)
        x = x + gt1[:, None, :] * out
        h = modulate(rms_norm(x, norm2_g[layer]), sh2, sc2)
        x = x + gt2[:, None, :] * hier_moe(h, *moe_params)
        if need_ctx:
            xc = xc + cgt1[:, None, :] * out_c
            hc = modulate(rms_norm(xc, norm2_g[layer]), csh2, csc2)
            xc = xc + cgt2[:, None, :] * hier_moe(hc, *moe_params)
    return rms_norm(x, final_norm_g)


_drawn_inputs = setup_inputs


def setup_inputs(seed=0):
    import zlib

    import numpy as np

    out = dict(_drawn_inputs(seed))
    spreads = {}
    factors = {'ctx': 14.423,
     'c_ctx': 27.285,
     'ada_b': 4.39,
     'norm1_g': 6.426,
     'norm2_g': 17.843,
     'rwkv_w_up': 6.68,
     'rwkv_a0': 8.0,
     'rwkv_k_k': 200.0,
     'rwkv_k_a': 200.0,
     'rwkv_ln_w': 200.0,
     'rwkv_ln_b': 200.0,
     'sg_ln_w': 66.814,
     'sg_ln_b': 125.746,
     'sg_b': 52.392,
     'moe_grp_b': 200.0,
     'moe_exp_b': 108.266,
     'final_norm_g': 21.842}
    for name, (base, spread) in spreads.items():
        noise = np.random.default_rng([zlib.crc32(name.encode()), seed]).standard_normal(out[name].shape)
        drawn = base * np.exp(spread * noise) if base else spread * noise
        out[name] = __import__('jax').numpy.asarray(drawn.astype(out[name].dtype))
    for name, factor in factors.items():
        out[name] = (out[name] * factor).astype(out[name].dtype)
    return out
```

```python
from contextlib import ExitStack

import numpy as np

import concourse.bass as bass
from concourse import mybir

F32 = mybir.dt.float32
I32 = mybir.dt.int32
U32 = mybir.dt.uint32
ALU = mybir.AluOpType
ACT = mybir.ActivationFunctionType
AX = mybir.AxisListType
ds = bass.ds

P = 128
D = 1024
KD = D // P
SEQ = 2048
CTX = 256
ALL = CTX + SEQ
GRID_W = 64
HEAD = 64
D_RWKV = 512
PAIRS = D_RWKV // P
CHUNK = 64
NCTX = CTX // CHUNK
NLAT = SEQ // CHUNK
STEPS = NCTX + NLAT
UNITS = 2 * PAIRS
OPW = 5 * CHUNK + 1
P_A = 1920
MA = P_A // P
D_SG = 512
GROUPS_SG = D_SG // P
Z_U = P_A
Z_V = P_A + D_SG
Z_G = P_A + 2 * D_SG
Z_COLS = Z_G + 2 * D
N_GRP = 4
PER_GRP = 8
N_EXP = N_GRP * PER_GRP
D_EXP = 512
SLOTS_BLOCK = 128
N_BLOCKS = 2 * SEQ // SLOTS_BLOCK + N_EXP
TILES = SEQ // P
NORM_EPS = 1e-6
GN_EPS = 64e-5
KAPPA = float(np.exp(-0.5))

PC = {}
_at = 0
for _name, _n in (("ada_b", 48), ("norm1_g", 8), ("shift_mu", MA), ("rwkv_w0", 8), ("rwkv_a0", 8), ("rwkv_k_k", 4),
                  ("rwkv_k_a", 4), ("rwkv_r_k", 4), ("rwkv_ln_w", 4), ("rwkv_ln_b", 4)):
    PC[_name] = _at
    _at += _n
N_PC = _at


class Core:

    def __init__(self, nc, ctx, stage):
        self.nc, self.ctx, self.stage, self.sems = nc, ctx, stage, []
        ctx.callback(self.clear)

    def sb(self, name, shape, dt=F32):
        return self.ctx.enter_context(self.nc.sbuf_tensor(f"{self.stage}_{name}", shape, dt))

    def ps(self, name, shape, dt=F32):
        return self.ctx.enter_context(self.nc.psum_tensor(f"{self.stage}_{name}", shape, dt))

    def sem(self, name):
        self.sems.append(self.nc.alloc_semaphore(f"{self.stage}_{name}"))
        return self.sems[-1]

    def clear(self):
        if self.sems:
            self.nc.clear_and_free_semaphores(self.sems)
            self.nc.all_engine_barrier()


def modulation(nc, a, keep):
    with ExitStack() as ctx:
        c = Core(nc, ctx, "modulation")
        NB = 512
        w = [c.sb(f"ada_tile{b}", [P, KD, NB]) for b in range(2)]
        cc = c.sb("cond", [P, 2, KD])
        cs = c.sb("cond_silu", [P, KD, 2])
        bias = c.sb("ada_bias", [2, 6 * D])
        rows = c.sb("par_rows", [N_PC, P])
        acc = [c.ps(f"ada_acc{b}", [P, NB]) for b in range(2)]
        turn = c.ps("par_turn", [P, NB])
        turn2 = c.ps("mod_turn", [P, NB])
        cond_in, rows_in, w_in_, w_free = c.sem("cond_in"), c.sem("rows_in"), [c.sem(f"ada_w_in{b}") for b in range(2)], c.sem("ada_w_free")
        eye0, eye, silu_ok, acc_ok, mod_ok = c.sem("eye0"), c.sem("eye"), c.sem("silu_ok"), c.sem("acc_ok"), c.sem("mod_ok")
        turned, par_ok, cols_ok, z_ok = c.sem("turned"), c.sem("par_ok"), c.sem("cols_ok"), c.sem("zeroed")
        bias_in = c.sem("bias_in")
        block = ctx.enter_context(nc.Block())
        adaw = a["ada_w"][0].rearrange("(p k) n -> p k n", k=KD)

        @block.sync
        def _(sp):
            sp.dma_start(cc[:, 0, :], a["c"][0].rearrange("(p k) -> p k", k=KD)).then_inc(cond_in, 16)
            sp.dma_start(cc[:, 1, :], a["c_ctx"].rearrange("(p k) -> p k", k=KD)).then_inc(cond_in, 16)
            with sp.Fori(0, 6) as i:
                for b in range(2):
                    sp.wait_ge(w_free, i + 1)
                    sp.dma_start(w[b][:, :, :], adaw[:, :, ds(i * (2 * NB) + b * NB, NB)]).then_inc(w_in_[b], 16)

        @block.gpsimd
        def _(pool):
            for r in range(2):
                pool.dma_start(bias[r:r + 1, :], a["ada_b"]).then_inc(bias_in, 16)
            flat = {"ada_b": a["ada_b"][0], "norm1_g": a["norm1_g"][0], "shift_mu": a["shift_mu"][0],
                    "rwkv_w0": a["rwkv_w0"][0].rearrange("d c -> (d c)"), "rwkv_a0": a["rwkv_a0"][0].rearrange("d c -> (d c)"),
                    "rwkv_k_k": a["rwkv_k_k"][0], "rwkv_k_a": a["rwkv_k_a"][0],
                    "rwkv_r_k": a["rwkv_r_k"][0].rearrange("h k -> (h k)"),
                    "rwkv_ln_w": a["rwkv_ln_w"][0], "rwkv_ln_b": a["rwkv_ln_b"][0]}
            for name, at in PC.items():
                v = flat[name].rearrange("(r p) -> r p", p=P)
                pool.dma_start(rows[at:at + v.shape[0], :], v).then_inc(rows_in, 16)
            pool.memset(keep.ident[:, :], 0.0).then_inc(eye0, 1)
            pool.memset(keep.heads[:, :], 0.0).then_inc(eye0, 1)
            pool.memset(keep.head_of[:, :], 0.0).then_inc(eye0, 1)
            pool.memset(keep.restart[:, :], 1.0).then_inc(eye0, 1)
            pool.memset(keep.quarter[:, :, :], 0.0).then_inc(eye0, 1)
            pool.memset(keep.ones[:, :], 1.0).then_inc(eye, 1)
            pool.wait_ge(eye0, 5)
            pool.wait_ge(eye, 1)
            for h in range(2):
                pool.wait_ge(eye, h + 1)
                pool.memset(keep.heads[h * HEAD:(h + 1) * HEAD, h * HEAD:(h + 1) * HEAD], 1.0).then_inc(eye, 1)
            for h in range(2):
                pool.wait_ge(eye, h + 3)
                pool.memset(keep.head_of[h * HEAD:(h + 1) * HEAD, h:h + 1], 1.0).then_inc(eye, 1)
            pool.wait_ge(eye, 5)
            pool.memset(keep.restart[:, :].rearrange("p (c t) -> p c t", t=CHUNK)[:, :, 0:1], 0.0).then_inc(eye, 1)
            pool.affine_select(out=keep.ident[:, :], in_=keep.ident[:, :], compare_op=ALU.not_equal, fill=1.0, base=0,
                               pattern=[[-1, P]], channel_multiplier=1).then_inc(eye, 1)
            pool.affine_select(out=keep.quarter[:, :, :], in_=keep.quarter[:, :, :], compare_op=ALU.not_equal, fill=1.0,
                               base=0, pattern=[[-1, 4], [-4, 32]], channel_multiplier=1).then_inc(eye, 1)

        @block.scalar
        def _(act):
            act.wait_ge(cond_in, 32)
            for v in range(2):
                act.activation(cs[:, :, v], cc[:, v, :], ACT.Silu).then_inc(silu_ok, 1)

        @block.tensor
        def _(pe):
            pe.wait_ge(silu_ok, 2)
            with pe.Fori(0, 6) as i:
                for b in range(2):
                    pe.wait_ge(w_in_[b], i * 16 + 16)
                    pe.wait_ge(mod_ok, i * 2 + b + 1)
                    for k in range(KD):
                        mm = pe.matmul(acc[b][0:2, :], cs[:, k, :], w[b][:, k, :], start=k == 0, stop=k == KD - 1)
                    mm.then_inc(acc_ok, 1)
            pe.wait_ge(eye, 8)
            pe.wait_ge(rows_in, 16 * len(PC))
            pe.transpose(turn[:, 0:N_PC], rows[:, :], keep.ident[0:N_PC, 0:N_PC]).then_inc(turned, 1)
            pe.wait_ge(mod_ok, 14)
            for t in range(48):
                mm = pe.transpose(turn2[:, 2 * t:2 * t + 2], keep.mod[:, t * P:(t + 1) * P], keep.ident[0:2, 0:2])
            mm.then_inc(turned, 1)

        @block.vector
        def _(dve):
            dve.sem_inc(w_free, 1)
            dve.sem_inc(mod_ok, 2)
            dve.wait_ge(bias_in, 32)
            with dve.Fori(0, 6) as i:
                for b in range(2):
                    dve.wait_ge(acc_ok, i * 2 + b + 1)
                    dve.tensor_tensor(keep.mod[:, ds(i * (2 * NB) + b * NB, NB)], acc[b][0:2, :],
                                      bias[:, ds(i * (2 * NB) + b * NB, NB)], ALU.add).then_inc(mod_ok, 1)
                dve.sem_inc(w_free, 1)
            dve.wait_ge(eye, 8)
            dve.tensor_reduce(keep.dirq[:, :], keep.quarter[:, :, :], AX.X, ALU.add).then_inc(z_ok, 1)
            dve.wait_ge(turned, 1)
            dve.tensor_copy(keep.par[:, :], turn[:, 0:N_PC]).then_inc(par_ok, 1)
            dve.wait_ge(turned, 2)
            dve.tensor_copy(keep.modc[:, :, :], turn2[:, 0:96].rearrange("p (t v) -> p t v", v=2)).then_inc(par_ok, 1)
            dve.wait_ge(par_ok, 2)
            dve.wait_ge(z_ok, 1)
            for v in range(2):
                dve.scalar_tensor_tensor(keep.scale1[:, v, :], keep.modc[:, KD:2 * KD, v], 1.0,
                                         keep.par[:, PC["norm1_g"]:PC["norm1_g"] + KD], ALU.add, ALU.mult).then_inc(cols_ok, 1)
            mu = keep.par[:, PC["shift_mu"]:PC["shift_mu"] + MA]
            dve.tensor_scalar(keep.mu_rest[:, :], mu, -1.0, 1.0, ALU.mult, ALU.add).then_inc(cols_ok, 1)
            for q in range(4):
                dve.tensor_scalar(keep.mu_dir[:, q, :], mu, keep.dirq[:, q:q + 1], None, ALU.mult).then_inc(cols_ok, 1)
            dve.wait_ge(cols_ok, 7)
            for q in range(2):
                dve.tensor_tensor(keep.mu_dir[:, 4 + q, :], keep.mu_dir[:, q, :], keep.mu_dir[:, q + 2, :],
                                  ALU.add).then_inc(cols_ok, 1)
            ka = keep.par[:, PC["rwkv_k_a"]:PC["rwkv_k_a"] + PAIRS]
            dve.tensor_scalar(keep.ka_rest[:, :], ka, -1.0, 1.0, ALU.mult, ALU.add).then_inc(cols_ok, 1)


def normalise(nc, a, keep, hT):
    with ExitStack() as ctx:
        c = Core(nc, ctx, "normalise")
        xt = [c.sb(f"x_tile{b}", [P, D]) for b in range(2)]
        xn = [c.sb(f"x_normed{b}", [P, D]) for b in range(2)]
        sq = c.sb("x_squared", [P, D])
        ss = c.sb("sum_squares", [P, 2])
        rt = c.sb("root", [P, 2])
        rs = c.sb("rstd", [P, 2])
        eps = c.sb("eps", [P, 1])
        turn = [c.ps(f"x_turn{b}", [P, D]) for b in range(2)]
        x_in = [c.sem(f"x_in{b}") for b in range(2)]
        names = ("x_sq", "x_root", "x_rstd", "x_norm", "x_turned", "h_ok", "eps_ok")
        x_sq, x_root, x_rstd, x_norm, x_turned, h_ok, eps_ok = (c.sem(n) for n in names)
        block = ctx.enter_context(nc.Block())
        TC = CTX // P
        ctx_rows = a["ctx"][0]
        lat_rows = a["x"][0]

        @block.sync
        def _(sp):
            for b in range(TC):
                sp.dma_start(xt[b][:, :], ctx_rows[b * P:(b + 1) * P, :]).then_inc(x_in[b], 16)
            with sp.Fori(0, TILES // 2) as i:
                for b in range(2):
                    sp.wait_ge(x_norm, i * 2 + b + 1)
                    sp.dma_start(xt[b][:, :], lat_rows[ds(i * (2 * P) + b * P, P), :]).then_inc(x_in[b], 16)

        @block.scalar
        def _(act):
            def tile(n, b, loads):
                act.wait_ge(x_in[b], loads * 16)
                act.wait_ge(x_rstd, n + 1)
                act.activation(sq[:, :], xt[b][:, :], ACT.Square, accum_out=ss[:, b:b + 1]).then_inc(x_sq, 1)
                act.wait_ge(x_sq, n + 1)
                act.activation(rt[:, b:b + 1], ss[:, b:b + 1], ACT.Sqrt, bias=eps[:, :], scale=1.0 / D).then_inc(x_root, 1)
                act.wait_ge(x_rstd, n + 3)
                act.wait_ge(x_turned, n + 1)
                act.activation(xn[b][:, :], xt[b][:, :], ACT.Copy, scale=rs[:, b:b + 1]).then_inc(x_norm, 1)
            act.wait_ge(eps_ok, 1)
            for b in range(TC):
                tile(b, b, 1)
            with act.Fori(0, TILES // 2) as i:
                for b in range(2):
                    tile(i * 2 + b + TC, b, i + 2)

        @block.tensor
        def _(pe):
            pe.sem_inc(x_turned, 2)

            def tile(n, b):
                pe.wait_ge(x_norm, n + 1)
                pe.wait_ge(h_ok, n + 1)
                for k in range(KD):
                    mm = pe.transpose(turn[b][:, k * P:(k + 1) * P], xn[b][:, k * P:(k + 1) * P], keep.ident[:, :])
                mm.then_inc(x_turned, 1)
            for b in range(TC):
                tile(b, b)
            with pe.Fori(0, TILES // 2) as i:
                for b in range(2):
                    tile(i * 2 + b + TC, b)

        @block.vector
        def _(dve):
            dve.memset(eps[:, :], NORM_EPS).then_inc(eps_ok, 1)
            dve.sem_inc(x_rstd, 2)
            dve.sem_inc(h_ok, 2)

            def tile(n, b, v, col):
                dve.wait_ge(x_root, n + 1)
                dve.reciprocal(rs[:, b:b + 1], rt[:, b:b + 1]).then_inc(x_rstd, 1)
                dve.wait_ge(x_turned, n + 3)
                for k in range(KD):
                    ins = dve.tensor_scalar(hT[:, k, ds(col, P)], turn[b][:, k * P:(k + 1) * P], keep.scale1[:, v, k:k + 1],
                                            keep.modc[:, k, v:v + 1], ALU.mult, ALU.add)
                ins.then_inc(h_ok, 1)
            for b in range(TC):
                tile(b, b, 1, b * P)
            with dve.Fori(0, TILES // 2) as i:
                for b in range(2):
                    tile(i * 2 + b + TC, b, 0, i * (2 * P) + (b * P + CTX))


def project(nc, a, keep, hT, ZA, UU, GT):
    with ExitStack() as ctx:
        c = Core(nc, ctx, "project")
        NW = 3
        w = [c.sb(f"w_tile{b}", [P, KD, P]) for b in range(NW)]
        zr = [c.sb(f"z_raw{b}", [P, ALL]) for b in range(2)]
        zm = [c.sb(f"z_mixed{b}", [P, ALL]) for b in range(2)]
        NG = 5
        acc = [c.ps(f"z_acc{g}", [P, 512]) for g in range(NG)]
        w_ready = [c.sem(f"w_ready{b}") for b in range(NW)]
        names = ("z_done", "z_out", "mixed", "stored", "shift", "z_free")
        z_done, z_out, mixed, stored, shift, z_free = (c.sem(n) for n in names)
        block = ctx.enter_context(nc.Block())
        GC = [(0, CTX)] + [(CTX + 512 * g, 512) for g in range(4)]
        win = a["w_in"][0].rearrange("(k p) n -> p k n", p=P)
        REST = (D_SG + 2 * D) // P

        @block.sync
        def _(sp):
            def load(b, col):
                sp.dma_start(w[b][:, :, :], win[:, :, ds(col, P)]).then_inc(w_ready[b], 16)
            for b in range(NW):
                load(b, b * P)
            with sp.Fori(0, MA // NW - 1) as i:
                for b in range(NW):
                    sp.wait_ge(z_done, i * (NW * NG) + (b + 1) * NG)
                    load(b, i * (NW * P) + (NW + b) * P)
            tiles = 0
            for col, count in ((Z_U, D_SG // P), (Z_G, 2 * D // P)):
                with sp.Fori(0, count // 2) as i:
                    for b in range(2):
                        sp.wait_ge(z_done, i * 8 + (MA * NG + (tiles + b - 1) * 4))
                        load(b, i * (2 * P) + (col + b * P))
                tiles += count

        @block.tensor
        def _(pe):
            def tile(loads, b, g0, done):
                pe.wait_ge(w_ready[b], loads * 16)
                for g in range(g0, NG):
                    pe.wait_ge(z_out, done + (g - g0 + 1))
                    col, nt = GC[g]
                    for k in range(KD):
                        mm = pe.matmul(acc[g][:, 0:nt], w[b][:, k, :], hT[:, k, col:col + nt], start=k == 0, stop=k == KD - 1)
                    mm.then_inc(z_done, 1)
            with pe.Fori(0, MA // 3) as i:
                for b in range(3):
                    tile(i + 1, b, 0, i * 15 + b * 5)
            with pe.Fori(0, REST // 2) as i:
                for b in range(2):
                    tile(i + (MA // 3 + 1), b, 1, i * 8 + (MA * 5 + b * 4 + 1))

        @block.scalar
        def _(act):
            act.sem_inc(z_out, NG)

            def tile(n, b, g0, done, func):
                if g0 == 0:
                    act.wait_ge(mixed, n + 1)
                else:
                    act.wait_ge(z_free, n + 1)
                for g in range(g0, NG):
                    act.wait_ge(z_done, done + (g - g0 + 1))
                    col, nt = GC[g]
                    act.activation(zr[b][:, col:col + nt], acc[g][:, 0:nt], func).then_inc(z_out, 1)
            with act.Fori(0, (MA - 1) // 2) as i:
                for b in range(2):
                    tile(i * 2 + b, b, 0, i * 10 + b * 5, ACT.Copy)
            tile(MA - 1, 0, 0, (MA - 1) * 5, ACT.Copy)
            act.wait_ge(mixed, MA + 2)
            base = MA * 5
            with act.Fori(0, D_SG // P // 2) as i:
                for b in range(2):
                    tile(i * 2 + (MA + b), b, 1, i * 8 + (base + b * 4), ACT.Gelu_apprx_tanh)
            base += 4 * 4
            with act.Fori(0, 2 * D // P // 2) as i:
                for b in range(2):
                    tile(i * 2 + (MA + 4 + b), b, 1, i * 8 + (base + b * 4), ACT.Sigmoid)

        @block.vector
        def _(dve):
            dve.sem_inc(mixed, 2)

            def tile(n, b):
                z, m = zr[b], zm[b]
                mu = lambda q: keep.mu_dir[:, q, ds(n, 1)]
                dve.wait_ge(z_out, n * 5 + (NG + 5))
                dve.wait_ge(z_free, n + 1)
                dve.tensor_scalar(m[:, :], z[:, :], keep.mu_rest[:, ds(n, 1)], None, ALU.mult).then_inc(shift, 1)
                steps = []
                for q, (to, frm) in enumerate(((slice(1, GRID_W), slice(0, GRID_W - 1)), (slice(0, GRID_W - 1), slice(1, GRID_W)))):
                    mg = m[:, CTX:ALL].rearrange("p (r w) -> p r w", w=GRID_W)
                    zg = z[:, CTX:ALL].rearrange("p (r w) -> p r w", w=GRID_W)
                    steps.append((mg[:, :, to], zg[:, :, frm], q))
                steps.append((m[:, CTX + GRID_W:ALL], z[:, CTX:ALL - GRID_W], 2))
                steps.append((m[:, CTX:ALL - GRID_W], z[:, CTX + GRID_W:ALL], 3))
                steps.append((m[:, 1:CTX], z[:, 0:CTX - 1], 4))
                steps.append((m[:, 0:CTX - 1], z[:, 1:CTX], 5))
                for j, (to, frm, q) in enumerate(steps):
                    dve.wait_ge(shift, n * 6 + (j + 1))
                    ins = dve.scalar_tensor_tensor(to, frm, mu(q), to, ALU.mult, ALU.add)
                    ins.then_inc(mixed if j == 5 else shift, 1)
            with dve.Fori(0, (MA - 1) // 2) as i:
                for b in range(2):
                    tile(i * 2 + b, b)
            tile(MA - 1, 0)

        @block.gpsimd
        def _(pool):
            pool.sem_inc(z_free, 2)

            def store(n, dst, src):
                pool.dma_start(dst, src).then_inc(stored, 16)
                pool.wait_ge(stored, n * 16 + 16)
                pool.sem_inc(z_free, 1)
            with pool.Fori(0, (MA - 1) // 2) as i:
                for b in range(2):
                    pool.wait_ge(mixed, i * 2 + (b + 3))
                    store(i * 2 + b, ZA[ds(i * 2 + b, 1), :, :].rearrange("m p t -> (m p) t"), zm[b][:, :])
            pool.wait_ge(mixed, MA + 2)
            store(MA - 1, ZA[MA - 1], zm[0][:, :])
            base, tiles = NG + MA * 5, MA
            for dst, count in ((UU, D_SG // P), (GT, 2 * D // P)):
                with pool.Fori(0, count // 2) as i:
                    for b in range(2):
                        pool.wait_ge(z_out, i * 8 + (base + b * 4 + 4))
                        store(i * 2 + (tiles + b), dst[ds(i * 2 + b, 1), :, :].rearrange("m p t -> (m p) t"), zr[b][:, CTX:ALL])
                base, tiles = base + 4 * count, tiles + count


def spatial_gate(nc, a, keep, hT, UU, YB):
    with ExitStack() as ctx:
        c = Core(nc, ctx, "spatial_gate")
        wv = c.sb("w_v", [P, KD, D_SG])
        hs = [c.sb(f"h_tile{b}", [P, KD, P]) for b in range(2)]
        v = [c.sb(f"v_gelu{b}", [P, D_SG]) for b in range(2)]
        vn = [c.sb(f"v_normed{b}", [P, D_SG]) for b in range(2)]
        ut = [c.sb(f"u_tile{b}", [P, GROUPS_SG, P]) for b in range(2)]
        yb = [c.sb(f"yb_tile{b}", [P, GROUPS_SG, P]) for b in range(2)]
        lnw, lnb = c.sb("sg_ln_w_all", [P, D_SG]), c.sb("sg_ln_b_all", [P, D_SG])
        sgb = c.sb("sg_b_all", [P, GROUPS_SG * P])
        sgw, sgwT = c.sb("sg_w_rows", [P, GROUPS_SG, P]), c.sb("sg_w_turned", [P, GROUPS_SG, P])
        st, mv, rt, rs = c.sb("v_stats", [P, 2, 6]), c.sb("v_meanvar", [P, 2, 2]), c.sb("v_root", [P, 2]), c.sb("v_rstd", [P, 2])
        eps = c.sb("ln_eps", [P, 1])
        acc = [c.ps(f"v_acc{b}", [P, D_SG]) for b in range(2)]
        mix = [c.ps(f"mix_acc{b}", [P, GROUPS_SG * P]) for b in range(2)]
        turn = c.ps("sg_turn", [P, GROUPS_SG * P])
        u_in = [c.sem(f"u_in{b}") for b in range(2)]
        aggr_go = c.sem("aggr_go")
        yb_stored = [c.sem(f"yb_stored{b}") for b in range(2)]
        names = ("const_in", "h_copied", "v_acc_ok", "v_ok", "stats_ok", "mv_ok", "root_ok", "rstd_ok", "centred", "scaled", "vn_ok",
                 "mix_ok", "biased", "yb_ok", "sg_turned", "sg_ready", "eps_ok")
        (const_in, h_copied, v_acc_ok, v_ok, stats_ok, mv_ok, root_ok, rstd_ok, centred, scaled, vn_ok, mix_ok, biased, yb_ok,
         sg_turned, sg_ready, eps_ok) = (c.sem(n) for n in names)
        block = ctx.enter_context(nc.Block())
        win = a["w_in"][0].rearrange("(k p) n -> p k n", p=P)

        @block.sync
        def _(sp):
            sp.dma_start(wv[:, :, :], win[:, :, Z_V:Z_V + D_SG]).then_inc(const_in, 16)
            sp.dma_start(lnw[:, :], a["sg_ln_w"].to_broadcast([P, D_SG])).then_inc(const_in, 16)
            sp.dma_start(lnb[:, :], a["sg_ln_b"].to_broadcast([P, D_SG])).then_inc(const_in, 16)
            sp.dma_start(sgb[:, :], a["sg_b"].rearrange("o g p -> o (g p)").to_broadcast([P, GROUPS_SG * P])).then_inc(const_in, 16)
            sp.dma_start(sgw[:, :, :], a["sg_w"][0].rearrange("g p q -> p g q")).then_inc(const_in, 16)
            for b in range(2):
                sp.sem_inc(yb_stored[b], 16)
                sp.dma_start(ut[b][:, :, :], UU[:, :, b * P:(b + 1) * P].rearrange("m p t -> p m t")).then_inc(u_in[b], 16)
            def store(n, b, col):
                sp.wait_ge(yb_ok, n + 1)
                sp.dma_start(YB[:, :, ds(col, P)].rearrange("m p t -> p m t"), yb[b][:, :, :]).then_inc(yb_stored[b], 16)
            with sp.Fori(0, TILES // 2 - 1) as i:
                for b in range(2):
                    store(i * 2 + b, b, i * (2 * P) + b * P)
                    sp.dma_start(ut[b][:, :, :],
                                 UU[:, :, ds(i * (2 * P) + (2 + b) * P, P)].rearrange("m p t -> p m t")).then_inc(u_in[b], 16)
            for b in range(2):
                store(TILES - 2 + b, b, (TILES - 2 + b) * P)
            for b in range(2):
                sp.wait_ge(yb_stored[b], 16 * (TILES // 2 + 1))

        @block.gpsimd
        def _(pool):
            with pool.Fori(0, TILES // 2) as i:
                for b in range(2):
                    pool.wait_ge(v_acc_ok, i * 2 + b + 1)
                    pool.tensor_copy(hs[b][:, :, :], hT[:, :, ds(i * (2 * P) + (CTX + b * P), P)]).then_inc(h_copied, 1)

        @block.tensor
        def _(pe):
            pe.sem_inc(v_acc_ok, 2)
            pe.wait_ge(const_in, 80)
            for g in range(GROUPS_SG):
                mm = pe.transpose(turn[:, g * P:(g + 1) * P], sgw[:, g, :], keep.ident[:, :])
            mm.then_inc(sg_turned, 1)

            def values(n, b):
                pe.wait_ge(h_copied, n + 1)
                pe.wait_ge(v_ok, n + 1)
                for k in range(KD):
                    mm = pe.matmul(acc[b][:, :], hs[b][:, k, :], wv[:, k, :], start=k == 0, stop=k == KD - 1)
                mm.then_inc(v_acc_ok, 1)

            def mixing(n, b):
                pe.wait_ge(vn_ok, n + 1)
                pe.wait_ge(biased, n + 1)
                for g in range(GROUPS_SG):
                    mm = pe.matmul(mix[b][:, g * P:(g + 1) * P], vn[b][:, g * P:(g + 1) * P], sgwT[:, g, :], start=True, stop=True)
                mm.then_inc(mix_ok, 1)
            pe.wait_ge(sg_ready, 1)
            values(0, 0)
            with pe.Fori(0, TILES // 2 - 1) as i:
                values(i * 2 + 1, 1)
                mixing(i * 2, 0)
                values(i * 2 + 2, 0)
                mixing(i * 2 + 1, 1)
            values(TILES - 1, 1)
            mixing(TILES - 2, 0)
            mixing(TILES - 1, 1)

        @block.scalar
        def _(act):
            act.sem_inc(v_ok, 2)
            act.wait_ge(eps_ok, 1)
            with act.Fori(0, TILES // 2) as i:
                for b in range(2):
                    n = i * 2 + b
                    act.wait_ge(v_acc_ok, n + 3)
                    act.wait_ge(centred, n + 1)
                    act.activation(v[b][:, :], acc[b][:, :], ACT.Gelu_apprx_tanh).then_inc(v_ok, 1)
                    act.wait_ge(mv_ok, n + 1)
                    act.activation(rt[:, b:b + 1], mv[:, b, 1:2], ACT.Sqrt, bias=eps[:, :]).then_inc(root_ok, 1)

        @block.vector
        def _(dve):
            dve.memset(eps[:, :], 1e-5).then_inc(eps_ok, 1)
            dve.sem_inc(centred, 2)
            dve.sem_inc(biased, 2)
            dve.wait_ge(sg_turned, 1)
            dve.tensor_copy(sgwT[:, :, :].rearrange("p g q -> p (g q)"), turn[:, :]).then_inc(sg_ready, 1)
            dve.wait_ge(const_in, 80)
            with dve.Fori(0, TILES // 2) as i:
                for b in range(2):
                    n = i * 2 + b
                    dve.wait_ge(v_ok, n + 3)
                    dve.bn_stats(st[:, b, :], v[b][:, :]).then_inc(stats_ok, 1)
                    dve.wait_ge(stats_ok, n + 1)
                    dve.sem_inc(aggr_go, 1)
                    dve.bn_aggr(mv[:, b, :], st[:, b, :]).then_inc(mv_ok, 1)
                    dve.wait_ge(root_ok, n + 1)
                    dve.reciprocal(rs[:, b:b + 1], rt[:, b:b + 1]).then_inc(rstd_ok, 1)
                    dve.wait_ge(rstd_ok, n + 1)
                    dve.tensor_scalar(vn[b][:, :], v[b][:, :], mv[:, b, 0:1], rs[:, b:b + 1], ALU.subtract, ALU.mult).then_inc(centred, 1)
                    dve.wait_ge(centred, n + 3)
                    dve.tensor_tensor(vn[b][:, :], vn[b][:, :], lnw[:, :], ALU.mult).then_inc(scaled, 1)
                    dve.wait_ge(scaled, n + 1)
                    dve.tensor_tensor(vn[b][:, :], vn[b][:, :], lnb[:, :], ALU.add).then_inc(vn_ok, 1)
                    dve.wait_ge(mix_ok, n + 1)
                    dve.wait_ge(yb_stored[b], i * 16 + 16)
                    yf = yb[b][:, :, :].rearrange("p g t -> p (g t)")
                    dve.tensor_tensor(yf, mix[b][:, :], sgb[:, :], ALU.add).then_inc(biased, 1)
                    dve.wait_ge(biased, n + 3)
                    dve.wait_ge(u_in[b], i * 16 + 16)
                    dve.tensor_tensor(yf, yf, ut[b][:, :, :].rearrange("p g t -> p (g t)"), ALU.mult).then_inc(yb_ok, 1)


def prepare(nc, a, keep, ZA, OPS):
    with ExitStack() as ctx:
        c = Core(nc, ctx, "prepare")
        NT = 512

        def two(name, shape=(P, NT)):
            return [c.sb(f"{name}{b}", list(shape)) for b in range(2)]
        r, k, v, wd, ad, wu, au = two("r"), two("k"), two("v"), two("wd"), two("ad"), two("w_up", (P, P)), two("a_up", (P, P))
        th, kk, sq, nrm = two("wd_tanh"), two("kk"), two("kk_sq"), two("kk_norm")
        four = (P, 2, NT)
        sg, av, lc, y, q = two("decay_sig", four), two("a_gate", four), two("log_sum", four), two("log_mid", four), two("log_prev", four)
        pp = two("pair_par", (P, 8))
        half = two("half", (P, 2, NT // CHUNK))
        ea, er, eb, kd, kka = two("exp_a", four), two("exp_r", four), two("exp_b", four), two("k_dir", four), two("kk_a", four)
        ops = [[c.sb(f"ops{b}{d}", [P, NT // CHUNK, OPW]) for d in range(2)] for b in range(2)]
        argw = [c.ps(f"arg_w{d}", [P, NT]) for d in range(2)]
        arga = [c.ps(f"arg_a{d}", [P, NT]) for d in range(2)]
        ssum = c.ps("kk_sum", [P, NT])
        z_in = [c.sem(f"z_in{b}") for b in range(2)]
        stored = [c.sem(f"ops_stored{b}") for b in range(2)]
        names = ("tanh_ok", "args_ok", "sig_ok", "sums_ok", "kk1_ok", "sq_ok", "norm_ok", "root_ok", "scan_ok", "half_ok", "mid_ok",
                 "prev_ok", "exp_ok", "act_end", "floor_ok", "inv_ok", "kk_ok", "kdir1_ok", "kdir2_ok", "pool_end", "slot_ok", "dve_end",
                 "pe_end", "ops_free", "par_pair_ok")
        (tanh_ok, args_ok, sig_ok, sums_ok, kk1_ok, sq_ok, norm_ok, root_ok, scan_ok, half_ok, mid_ok, prev_ok, exp_ok, act_end,
         floor_ok, inv_ok, kk_ok, kdir1_ok, kdir2_ok, pool_end, slot_ok, dve_end, pe_end,
         ops_free, par_pair_ok) = (c.sem(n) for n in names)
        block = ctx.enter_context(nc.Block())

        def instances(eng, body):
            with eng.Fori(0, PAIRS // 2) as i:
                for b in range(2):
                    p = i * 2 + b
                    body(p, i, b, p, 0, CTX, 0)
            with eng.Fori(0, PAIRS) as p:
                with eng.Fori(0, 2) as s:
                    for b in range(2):
                        seg = s * 2 + b
                        body(p * 4 + seg + 4, p * 2 + s + 2, b, p, seg * NT + CTX, NT, seg * (NT // CHUNK) + NCTX)

        @block.sync
        def _(sp):
            def body(n, m, b, p, col, nt, chunk):
                for e in (dve_end, act_end, pool_end, pe_end):
                    sp.wait_ge(e, n + 1)
                for dst, tile in ((r, p), (k, p + PAIRS), (v, p + 2 * PAIRS), (wd, 3 * PAIRS), (ad, 3 * PAIRS + 1)):
                    sp.dma_start(dst[b][:, 0:nt], ZA[ds(tile, 1), :, ds(col, nt)].rearrange("m p t -> (m p) t")).then_inc(z_in[b], 16)
                sp.dma_start(wu[b][:, :], a["rwkv_w_up"][0].rearrange("d r c -> (d r) c")[:, ds(p * P, P)]).then_inc(z_in[b], 16)
                sp.dma_start(au[b][:, :], a["rwkv_a_up"][0].rearrange("d r c -> (d r) c")[:, ds(p * P, P)]).then_inc(z_in[b], 16)
            instances(sp, body)

        @block.tensor
        def _(pe):
            pe.sem_inc(pe_end, 2)

            def body(n, m, b, p, col, nt, chunk):
                pe.wait_ge(tanh_ok, n + 1)
                pe.wait_ge(sig_ok, n * 4 + 4)
                for d in range(2):
                    h = slice(HEAD * d, HEAD * d + HEAD)
                    pe.matmul(argw[d][:, 0:nt], wu[b][h, :], th[b][h, 0:nt], start=True, stop=True)
                    mm = pe.matmul(arga[d][:, 0:nt], au[b][h, :], ad[b][h, 0:nt], start=True, stop=True)
                mm.then_inc(args_ok, 1)
                pe.wait_ge(sq_ok, n + 1)
                pe.wait_ge(root_ok, n + 1)
                pe.matmul(ssum[:, 0:nt], keep.heads[:, :], sq[b][:, 0:nt], start=True, stop=True).then_inc(pe_end, 1)
            instances(pe, body)

        @block.scalar
        def _(act):
            act.sem_inc(sig_ok, 4)
            act.sem_inc(root_ok, 1)
            act.sem_inc(act_end, 2)

            def body(n, m, b, p, col, nt, chunk):
                act.wait_ge(z_in[b], m * 112 + 112)
                act.wait_ge(pe_end, n + 1)
                act.activation(th[b][:, 0:nt], wd[b][:, 0:nt], ACT.Tanh).then_inc(tanh_ok, 1)
                act.wait_ge(args_ok, n + 1)
                act.wait_ge(par_pair_ok, n * 2 + 2)
                act.wait_ge(dve_end, n + 1)
                act.wait_ge(pool_end, n + 1)
                for d in range(2):
                    act.activation(sg[b][:, d, 0:nt], argw[d][:, 0:nt], ACT.Sigmoid,
                                   bias=pp[b][:, d:d + 1]).then_inc(sig_ok, 1)
                    act.activation(av[b][:, d, 0:nt], arga[d][:, 0:nt], ACT.Sigmoid,
                                   bias=pp[b][:, 2 + d:3 + d]).then_inc(sig_ok, 1)
                act.wait_ge(sig_ok, n * 4 + 8)
                for d in range(2):
                    act.activation(kd[b][:, d, 0:nt], av[b][:, d, 0:nt], ACT.Identity, scale=pp[b][:, 5:6],
                                   bias=pp[b][:, 6:7]).then_inc(kdir1_ok, 1)
                act.wait_ge(kk1_ok, n + 1)
                act.activation(sq[b][:, 0:nt], kk[b][:, 0:nt], ACT.Square).then_inc(sq_ok, 1)
                act.wait_ge(pe_end, n + 3)
                act.activation(nrm[b][:, 0:nt], ssum[:, 0:nt], ACT.Sqrt).then_inc(root_ok, 1)
                act.wait_ge(ops_free, n + 1)
                for d in range(2):
                    act.wait_ge(prev_ok, n * 2 + (d + 1))
                    y_, q_ = y[b][:, d, 0:nt], q[b][:, d, 0:nt]
                    table = ((er, y_, -1), (ea, q_, -1), (eb, y_, 1)) if d == 0 else ((ea, y_, 1), (er, q_, 1), (eb, q_, -1))
                    for dst, src, sign in table:
                        act.activation(dst[b][:, d, 0:nt], src, ACT.Exp, scale=sign * KAPPA).then_inc(exp_ok, 1)
                    nch = nt // CHUNK
                    act.activation(ops[b][d][:, 0:nch, 5 * CHUNK], half[b][:, d, 0:nch], ACT.Exp, scale=-KAPPA).then_inc(exp_ok, 1)
                for d in range(2):
                    act.activation(ops[b][d][:, 0:nt // CHUNK, 4 * CHUNK:5 * CHUNK],
                                   v[b][:, 0:nt].rearrange("p (c t) -> p c t", t=CHUNK), ACT.Copy).then_inc(act_end if d else exp_ok, 1)
            instances(act, body)

        @block.gpsimd
        def _(pool):
            pool.sem_inc(pool_end, 2)
            pool.sem_inc(ops_free, 2)

            def body(n, m, b, p, col, nt, chunk):
                pool.wait_ge(sig_ok, n * 4 + 8)
                pool.wait_ge(z_in[b], m * 112 + 112)
                pool.wait_ge(dve_end, n + 1)
                for d in range(2):
                    pool.wait_ge(kdir1_ok, n * 2 + (d + 1))
                    pool.tensor_tensor(kd[b][:, d, 0:nt], kd[b][:, d, 0:nt], k[b][:, 0:nt], ALU.mult).then_inc(kdir2_ok, 1)
                pool.wait_ge(kk_ok, n + 1)
                for d in range(2):
                    pool.tensor_tensor(kka[b][:, d, 0:nt], kk[b][:, 0:nt], av[b][:, d, 0:nt],
                                       ALU.mult).then_inc(pool_end if d else kdir2_ok, 1)
                nch = nt // CHUNK
                pool.wait_ge(dve_end, n + 3)
                pool.wait_ge(act_end, n + 3)
                for d in range(2):
                    pool.dma_start(OPS[ds(chunk, nch), ds(p + PAIRS * d, 1), :, :].rearrange("s u p w -> p (s u) w"),
                                   ops[b][d][:, 0:nch, :]).then_inc(stored[b], 16)
                pool.wait_ge(stored[b], m * 32 + 32)
                pool.sem_inc(ops_free, 1)
            instances(pool, body)

        @block.vector
        def _(dve):
            dve.sem_inc(dve_end, 2)

            def body(n, m, b, p, col, nt, chunk):
                nch = nt // CHUNK
                by_chunk = lambda x: x.rearrange("p (c t) -> p c t", t=CHUNK)
                dve.wait_ge(z_in[b], m * 112 + 112)
                dve.wait_ge(pool_end, n + 1)
                dve.wait_ge(act_end, n + 1)
                dve.tensor_scalar(pp[b][:, 0:6], keep.par[:, PC["rwkv_w0"]:PC["rwkv_w0"] + 6 * PAIRS].rearrange(
                    "p (v q) -> p v q", q=PAIRS)[:, :, ds(p, 1)].rearrange("p v q -> p (v q)"), 1.0, None, ALU.mult).then_inc(par_pair_ok, 1)
                dve.tensor_scalar(pp[b][:, 6:7], keep.ka_rest[:, ds(p, 1)], 1.0, None, ALU.mult).then_inc(par_pair_ok, 1)
                dve.wait_ge(par_pair_ok, n * 2 + 2)
                dve.tensor_scalar(kk[b][:, 0:nt], k[b][:, 0:nt], pp[b][:, 4:5], None,
                                  ALU.mult).then_inc(kk1_ok, 1)
                dve.wait_ge(sig_ok, n * 4 + 8)
                for d in range(2):
                    dve.tensor_tensor_scan(lc[b][:, d, 0:nt], keep.restart[:, 0:nt], sg[b][:, d, 0:nt], 0.0, ALU.mult,
                                           ALU.add).then_inc(scan_ok, 1)
                for d in range(2):
                    dve.wait_ge(scan_ok, n * 2 + (d + 1))
                    dve.tensor_scalar(half[b][:, d, 0:nch], by_chunk(lc[b][:, d, 0:nt])[:, :, CHUNK - 1], 0.5, None,
                                      ALU.mult).then_inc(half_ok, 1)
                for d in range(2):
                    dve.wait_ge(half_ok, n * 2 + (d + 1))
                    dve.tensor_tensor(by_chunk(y[b][:, d, 0:nt]), by_chunk(lc[b][:, d, 0:nt]),
                                      half[b][:, d, 0:nch, None].to_broadcast([P, nch, CHUNK]), ALU.subtract).then_inc(mid_ok, 1)
                for d in range(2):
                    dve.wait_ge(mid_ok, n * 2 + (d + 1))
                    dve.tensor_tensor(q[b][:, d, 0:nt], y[b][:, d, 0:nt], sg[b][:, d, 0:nt], ALU.subtract).then_inc(prev_ok, 1)
                dve.wait_ge(root_ok, n + 2)
                dve.tensor_scalar(nrm[b][:, 0:nt], nrm[b][:, 0:nt], 1e-12, None, ALU.max).then_inc(floor_ok, 1)
                dve.wait_ge(floor_ok, n + 1)
                dve.reciprocal(nrm[b][:, 0:nt], nrm[b][:, 0:nt]).then_inc(inv_ok, 1)
                dve.wait_ge(inv_ok, n + 1)
                dve.tensor_tensor(kk[b][:, 0:nt], kk[b][:, 0:nt], nrm[b][:, 0:nt], ALU.mult).then_inc(kk_ok, 1)
                dve.wait_ge(kk_ok, n + 1)
                dve.wait_ge(ops_free, n + 1)
                for d in range(2):
                    dve.wait_ge(exp_ok, n * 9 + 4 * (d + 1))
                    if d == 0:
                        dve.wait_ge(pool_end, n + 3)
                    for s, (x, e) in enumerate(((kk[b][:, 0:nt], ea), (r[b][:, 0:nt], er), (kka[b][:, d, 0:nt], eb),
                                                (kd[b][:, d, 0:nt], eb))):
                        dve.tensor_tensor(ops[b][d][:, 0:nch, s * CHUNK:(s + 1) * CHUNK], by_chunk(x),
                                          by_chunk(e[b][:, d, 0:nt]), ALU.mult).then_inc(dve_end if (d, s) == (1, 3) else slot_ok, 1)
            instances(dve, body)


LEVELS = 5
N_MASKS = 4 + 1 + LEVELS


def scan_masks():
    s, t = np.arange(P)[:, None], np.arange(P)[None, :]
    same = s // CHUNK == t // CHUNK
    out = np.zeros((P, 2, N_MASKS, P), np.float32)
    for d in range(2):
        a, b = (s, t) if d == 0 else (t, s)
        for j in range(4):
            out[:, d, j] = same & ((a < b) if j % 2 == 0 else (a <= b))
        for lv in range(LEVELS + 1):
            w = 1 << lv
            out[:, d, 4 + lv] = (a // (2 * w) == b // (2 * w)) & (a // w < b // w)
        out[:, d, 4] *= -1
    return out


def scan(nc, a, keep, OPS, Y):
    with ExitStack() as ctx:
        c = Core(nc, ctx, "scan")
        U4 = PAIRS
        BD = U4 + 1
        masks = c.sb("masks", [P, 2, N_MASKS, P])

        def g2(name, shape):
            return [c.sb(f"{name}{g}", shape) for g in range(2)]

        def g2b(name, shape):
            return [[c.sb(f"{name}{g}{b}", shape) for b in range(2)] for g in range(2)]
        st, bd, yo, dh = g2b("staged", [P, U4, OPW]), g2b("diag", [P, U4, 5, P]), g2b("y_out", [P, U4, CHUNK]), g2b("decay", [P, U4])
        gm, tm, lv = g2("products", [P, U4, 4, P]), g2("by_token", [P, U4, 3, P]), g2("level_parts", [P, U4, LEVELS, P])
        T, TT, Z = g2("inv", [P, U4, P]), g2("inv_turned", [P, U4, P]), g2("level_prod", [P, U4, P])
        ru, uu, sp_, sn = g2("u_rhs", [P, U4, P]), g2("u", [P, U4, P]), g2b("state_mid", [P, U4, P]), g2("state", [P, U4, P])
        d2 = g2("decay_two", [P, U4])
        bank = [[c.ps(f"bank{g}{j}", [P, 512]) for j in range(4)] for g in range(2)]

        def s2(name):
            return [c.sem(f"{name}{g}") for g in range(2)]
        ops_in = [[c.sem(f"ops_in{g}{b}") for b in range(2)] for g in range(2)]
        y_stored = [[c.sem(f"y_stored{g}{b}") for b in range(2)] for g in range(2)]
        masks_in, zeroed = c.sem("masks_in"), c.sem("diag_zeroed")
        bd_ok, decay_ok, mid_ok, lv_ok = s2("diag_ok"), s2("decay_ok"), s2("state_mid_ok"), s2("levels_ok")
        tr_mm, g_mm, ru_mm, t0_mm, z_mm, p_mm = s2("turned"), s2("products_mm"), s2("u_rhs_mm"), s2("inv0_mm"), s2("z_mm"), s2("p_mm")
        u_mm, s_mm, y_mm = s2("u_mm"), s2("state_mm"), s2("y_mm")
        tm_ok, ru_ok, z_ok, u_ok, y_ok = s2("by_token_ok"), s2("u_rhs_ok"), s2("z_ok"), s2("u_ok"), s2("y_ok")
        gm_ok, pair_ok, tt0_ok, t0_ok, t_ok, tt_ok, sn_ok = (s2("products_ok"), s2("pairs_ok"), s2("inv0_turned_ok"), s2("inv0_ok"),
                                                             s2("inv_ok"), s2("inv_turned_ok"), s2("state_ok"))
        block = ctx.enter_context(nc.Block())

        def steps(eng, body):
            with eng.Fori(0, NCTX // 2) as i:
                for b in range(2):
                    body(i * 2 + b, i, b, (i * 2 + b, i * (-2) + (NCTX - 1 - b)))
            with eng.Fori(0, NLAT // 2) as i:
                for b in range(2):
                    body(i * 2 + (NCTX + b), i + NCTX // 2, b, (i * 2 + (NCTX + b), i * (-2) + (STEPS - 1 - b)))

        @block.sync
        def _(sp):
            sp.dma_start(masks[:, :, :, :], a["scan_masks"]).then_inc(masks_in, 16)

            def body(n, m, b, chunk):
                for g in range(2):
                    sp.wait_ge(bd_ok[g], n * BD + BD)
                    sp.dma_start(st[g][b][:, :, :],
                                 OPS[ds(chunk[g], 1), U4 * g:U4 * g + U4, :, :].rearrange("c u p w -> p (c u) w")).then_inc(ops_in[g][b], 16)
            steps(sp, body)

        @block.gpsimd
        def _(pool):
            for g in range(2):
                pool.sem_inc(bd_ok[g], 2 * BD)
                pool.memset(sn[g][:, :, :], 0.0).then_inc(zeroed, 1)
                pool.memset(dh[g][1][:, :], 1.0).then_inc(zeroed, 1)
            pool.wait_ge(zeroed, 4)
            pool.wait_ge(masks_in, 16)

            def body(n, m, b, chunk):
                for g in range(2):
                    pool.wait_ge(ops_in[g][b], m * 16 + 16)
                    pool.wait_ge(y_mm[g], n + 1)
                    for u in range(U4):
                        pool.tensor_tensor(bd[g][b][:, u, :, :].rearrange("p o (h t) -> p o h t", h=2),
                                           st[g][b][:, u, 0:5 * CHUNK].rearrange("p (o x t) -> p o x t", o=5, x=1).to_broadcast([P, 5, 2, CHUNK]),
                                           keep.head_of[:, None, :, None].to_broadcast([P, 5, 2, CHUNK]), ALU.mult).then_inc(bd_ok[g], 1)
                    pool.tensor_tensor(dh[g][b][:, :], st[g][b][:, :, 5 * CHUNK], keep.ones[:, 0:U4], ALU.mult).then_inc(bd_ok[g], 1)
                for g in range(2):
                    pool.wait_ge(bd_ok[g], n * BD + 3 * BD)
                    pool.tensor_tensor(d2[g][:, :], dh[g][b][:, :], dh[g][1 - b][:, :], ALU.mult).then_inc(decay_ok[g], 1)
                    pool.wait_ge(decay_ok[g], n + 1)
                    pool.wait_ge(sn_ok[g], n + 1)
                    pool.tensor_tensor(sp_[g][b][:, :, :], sn[g][:, :, :], d2[g][:, :, None].to_broadcast([P, U4, P]),
                                       ALU.mult).then_inc(mid_ok[g], 1)
                for g in range(2):
                    pool.wait_ge(gm_ok[g], n * 4 + 4)
                    pool.tensor_tensor(lv[g][:, :, :, :], gm[g][:, :, 0:1, :].to_broadcast([P, U4, LEVELS, P]),
                                       masks[:, g:g + 1, 5:5 + LEVELS, :].to_broadcast([P, U4, LEVELS, P]), ALU.mult).then_inc(lv_ok[g], 1)
            steps(pool, body)

        @block.tensor
        def _(pe):
            for g in range(2):
                pe.sem_inc(y_mm[g], 2)

            def body(n, m, b, chunk):
                def mm(g, j, u, lhsT, rhs, start=True, stop=True, w=P):
                    return pe.matmul(bank[g][j][:, u * w:(u + 1) * w], lhsT, rhs, start=start, stop=stop)
                for g in range(2):
                    pe.wait_ge(bd_ok[g], n * BD + 3 * BD)
                    for e in (u_ok, sn_ok, ru_ok):
                        pe.wait_ge(e[g], n + 1)
                    pe.wait_ge(y_ok[g], n * 2 + 2)
                    for u in range(U4):
                        for j in range(3):
                            x = pe.transpose(bank[g][u][:, j * P:(j + 1) * P], bd[g][b][:, u, 2 + j, :], keep.ident[:, :])
                        x.then_inc(tr_mm[g], 1)
                for g in range(2):
                    for u in range(U4):
                        pe.wait_ge(tm_ok[g], n * 4 + (u + 1))
                        ar = bd[g][b][:, u, 0:2, :]
                        for j in range(2):
                            x = pe.matmul(bank[g][u][:, j * 256:(j + 1) * 256], bd[g][b][:, u, 2 + j, :], ar, start=True, stop=True)
                        x.then_inc(g_mm[g], 1)
                for g in range(2):
                    pe.wait_ge(mid_ok[g], n + 1)
                    pe.wait_ge(gm_ok[g], n * 4 + 4)
                    for u in range(U4):
                        mm(g, 3, u, bd[g][b][:, u, 0, :], sp_[g][b][:, u, :], stop=False)
                        x = mm(g, 3, u, gm[g][:, u, 2, :], tm[g][:, u, 2, :], start=False)
                    x.then_inc(ru_mm[g], 1)
                for g in range(2):
                    pe.wait_ge(tt0_ok[g], n + 1)
                    for u in range(U4):
                        x = pe.transpose(bank[g][0][:, u * P:(u + 1) * P], TT[g][:, u, :], keep.ident[:, :])
                    x.then_inc(t0_mm[g], 1)
                for l in range(1, LEVELS + 1):
                    for g in range(2):
                        if l == 1:
                            pe.wait_ge(lv_ok[g], n + 1)
                            pe.wait_ge(t0_ok[g], n + 1)
                        else:
                            pe.wait_ge(t_ok[g], n * (LEVELS - 1) + (l - 1))
                        for u in range(U4):
                            x = mm(g, 0, u, lv[g][:, u, l - 1, :], T[g][:, u, :])
                        x.then_inc(z_mm[g], 1)
                    for g in range(2):
                        pe.wait_ge(z_ok[g], n * LEVELS + l)
                        if l > 1:
                            pe.wait_ge(tt_ok[g], n * LEVELS + (l - 1))
                        if l < LEVELS:
                            for u in range(U4):
                                mm(g, 1, u, TT[g][:, u, :], Z[g][:, u, :])
                        for u in range(U4):
                            x = mm(g, 2, u, Z[g][:, u, :], TT[g][:, u, :])
                        x.then_inc(p_mm[g], 1)
                for g in range(2):
                    pe.wait_ge(tt_ok[g], n * LEVELS + LEVELS)
                    pe.wait_ge(ru_ok[g], n + 2)
                    for u in range(U4):
                        x = mm(g, 0, u, TT[g][:, u, :], ru[g][:, u, :])
                    x.then_inc(u_mm[g], 1)
                for g in range(2):
                    pe.wait_ge(u_ok[g], n + 2)
                    for u in range(U4):
                        mm(g, 1, u, tm[g][:, u, 0, :], uu[g][:, u, :], stop=False)
                        x = mm(g, 1, u, tm[g][:, u, 1, :], tm[g][:, u, 2, :], start=False)
                    x.then_inc(s_mm[g], 1)
                for g in range(2):
                    for u in range(U4):
                        mm(g, 2, u, sp_[g][b][:, u, :], bd[g][b][:, u, 1, :], stop=False)
                        mm(g, 2, u, uu[g][:, u, :], gm[g][:, u, 1, :], start=False, stop=False)
                        x = mm(g, 2, u, tm[g][:, u, 2, :], gm[g][:, u, 3, :], start=False)
                    x.then_inc(y_mm[g], 1)
            steps(pe, body)

        @block.scalar
        def _(act):
            for g in range(2):
                act.sem_inc(u_ok[g], 1)
                act.sem_inc(ru_ok[g], 1)
                act.sem_inc(y_ok[g], 2)
                for b in range(2):
                    act.sem_inc(y_stored[g][b], 16)
            flat = lambda x: x.rearrange("p u t -> p (u t)")

            def body(n, m, b, chunk):
                for g in range(2):
                    for u in range(U4):
                        act.wait_ge(tr_mm[g], n * 4 + (u + 1))
                        act.activation(tm[g][:, u, :, :].rearrange("p o t -> p (o t)"), bank[g][u][:, 0:3 * P],
                                       ACT.Copy).then_inc(tm_ok[g], 1)
                for g in range(2):
                    act.wait_ge(ru_mm[g], n + 1)
                    act.activation(flat(ru[g][:, :, :]), bank[g][3][:, :], ACT.Copy).then_inc(ru_ok[g], 1)
                for l in range(1, LEVELS + 1):
                    for g in range(2):
                        act.wait_ge(z_mm[g], n * LEVELS + l)
                        act.activation(flat(Z[g][:, :, :]), bank[g][0][:, :], ACT.Copy).then_inc(z_ok[g], 1)
                for g in range(2):
                    act.wait_ge(u_mm[g], n + 1)
                    act.activation(flat(uu[g][:, :, :]), bank[g][0][:, :], ACT.Copy, scale=-1.0).then_inc(u_ok[g], 1)
                for g in range(2):
                    act.wait_ge(y_mm[g], n + 3)
                    act.wait_ge(y_stored[g][b], m * 16 + 16)
                    for h in range(2):
                        hp = slice(HEAD * h, HEAD * h + HEAD)
                        act.activation(yo[g][b][hp, :, :], bank[g][2][hp, :].rearrange("p (u t) -> p u t", t=P)[:, :, hp],
                                       ACT.Copy).then_inc(y_ok[g], 1)
                    act.wait_ge(y_ok[g], n * 2 + 4)
                    act.dma_start(Y[g, :, :, ds(chunk[g] * CHUNK, CHUNK)].rearrange("u p t -> p u t"),
                                  yo[g][b][:, :, :]).then_inc(y_stored[g][b], 16)
            steps(act, body)
            for g in range(2):
                for b in range(2):
                    act.wait_ge(y_stored[g][b], 16 + 16 * (STEPS // 2))

        @block.vector
        def _(dve):
            for g in range(2):
                dve.sem_inc(sn_ok[g], 1)
            dve.wait_ge(masks_in, 16)
            flat = lambda x: x.rearrange("p u t -> p (u t)")

            def body(n, m, b, chunk):
                for g in range(2):
                    for u in range(U4):
                        dve.wait_ge(g_mm[g], n * 4 + (u + 1))
                        dve.tensor_tensor(gm[g][:, u, :, :].rearrange("p o t -> p (o t)"), bank[g][u][:, :],
                                          masks[:, g, 0:4, :].rearrange("p o t -> p (o t)"), ALU.mult).then_inc(gm_ok[g], 1)
                    dve.wait_ge(gm_ok[g], n * 4 + 4)
                    dve.tensor_tensor(TT[g][:, :, :], gm[g][:, :, 0, :], masks[:, g, 4:5, :].to_broadcast([P, U4, P]),
                                      ALU.mult).then_inc(pair_ok[g], 1)
                    dve.wait_ge(pair_ok[g], n + 1)
                    dve.tensor_tensor(TT[g][:, :, :], TT[g][:, :, :], keep.ident[:, None, :].to_broadcast([P, U4, P]),
                                      ALU.add).then_inc(tt0_ok[g], 1)
                for g in range(2):
                    dve.wait_ge(t0_mm[g], n + 1)
                    dve.tensor_copy(flat(T[g][:, :, :]), bank[g][0][:, :]).then_inc(t0_ok[g], 1)
                for l in range(1, LEVELS + 1):
                    for g in range(2):
                        dve.wait_ge(p_mm[g], n * LEVELS + l)
                        if l < LEVELS:
                            dve.tensor_tensor(flat(T[g][:, :, :]), flat(T[g][:, :, :]), bank[g][1][:, :], ALU.subtract).then_inc(t_ok[g], 1)
                        dve.tensor_tensor(flat(TT[g][:, :, :]), flat(TT[g][:, :, :]), bank[g][2][:, :], ALU.subtract).then_inc(tt_ok[g], 1)
                for g in range(2):
                    dve.wait_ge(s_mm[g], n + 1)
                    dve.tensor_tensor(flat(sn[g][:, :, :]), flat(sp_[g][b][:, :, :]), bank[g][1][:, :], ALU.add).then_inc(sn_ok[g], 1)
            steps(dve, body)


def mixer_out(nc, a, keep, ZA, Y, YA):
    with ExitStack() as ctx:
        c = Core(nc, ctx, "mixer_out")
        NT = 512

        def two(name, shape=(P, NT)):
            return [c.sb(f"{name}{b}", list(shape)) for b in range(2)]
        yf, yr, r, k, v, gd, gu = two("y_fwd"), two("y_rev"), two("r"), two("k"), two("v"), two("gd"), two("g_up", (P, P))
        pp, rk, gs, yc, sq, rt, out = two("pair_par", (P, 4)), two("rk"), two("g_sig"), two("y_mid"), two("y_sq"), two("y_root"), two("ya")
        eps = c.sb("gn_eps", [P, 1])
        mean, bonus, gate, var = c.ps("mean", [P, NT]), c.ps("bonus", [P, NT]), c.ps("gate", [P, NT]), c.ps("var", [P, NT])
        y_in = [c.sem(f"y_in{b}") for b in range(2)]
        names = ("y_sum", "rk_ok", "g_sig_ok", "par_ok", "sums_mm", "mid_ok", "sq_ok", "var_mm", "root_ok", "inv_ok", "norm_ok", "affine_ok",
                 "bonus_ok", "added", "ya_ok", "stored", "ya_free", "eps_ok")
        (y_sum, rk_ok, g_sig_ok, par_ok, sums_mm, mid_ok, sq_ok, var_mm, root_ok, inv_ok, norm_ok, affine_ok, bonus_ok, added, ya_ok,
         stored, ya_free, eps_ok) = (c.sem(n) for n in names)
        block = ctx.enter_context(nc.Block())

        def instances(eng, body):
            with eng.Fori(0, PAIRS) as p:
                with eng.Fori(0, 2) as s:
                    for b in range(2):
                        body(p * 4 + s * 2 + b, p * 2 + s, b, p, s * (2 * NT) + b * NT)

        @block.sync
        def _(sp):
            def body(n, m, b, p, col):
                sp.wait_ge(ya_ok, n + 1)
                cols = ds(col + CTX, NT)
                for d, dst in enumerate((yf, yr)):
                    sp.dma_start(dst[b][:, :], Y[d, ds(p, 1), :, cols].rearrange("u p t -> (u p) t")).then_inc(y_in[b], 16)
                for dst, tile in ((r, p), (k, p + PAIRS), (v, p + 2 * PAIRS), (gd, MA - 1)):
                    sp.dma_start(dst[b][:, :], ZA[ds(tile, 1), :, cols].rearrange("m p t -> (m p) t")).then_inc(y_in[b], 16)
                sp.dma_start(gu[b][:, :], a["rwkv_g_up"][0][:, ds(p * P, P)]).then_inc(y_in[b], 16)
            instances(sp, body)

        @block.scalar
        def _(act):
            act.sem_inc(root_ok, 1)
            act.wait_ge(eps_ok, 1)

            def body(n, m, b, p, col):
                act.wait_ge(y_in[b], m * 112 + 112)
                act.activation(gs[b][:, :], gd[b][:, :], ACT.Sigmoid).then_inc(g_sig_ok, 1)
                act.wait_ge(mid_ok, n + 1)
                act.activation(sq[b][:, :], yc[b][:, :], ACT.Square).then_inc(sq_ok, 1)
                act.wait_ge(var_mm, n + 1)
                act.activation(rt[b][:, :], var[:, :], ACT.Sqrt, bias=eps[:, :], scale=1.0 / HEAD).then_inc(root_ok, 1)
            instances(act, body)

        @block.tensor
        def _(pe):
            def body(n, m, b, p, col):
                pe.wait_ge(y_sum, n + 1)
                pe.wait_ge(ya_ok, n + 2)
                pe.matmul(mean[:, :], keep.heads[:, :], yf[b][:, :], start=True, stop=True)
                pe.wait_ge(rk_ok, n + 1)
                pe.matmul(bonus[:, :], keep.heads[:, :], rk[b][:, :], start=True, stop=True)
                pe.wait_ge(g_sig_ok, n + 1)
                pe.matmul(gate[:, :], gu[b][:, :], gs[b][:, :], start=True, stop=True).then_inc(sums_mm, 1)
                pe.wait_ge(sq_ok, n + 1)
                pe.wait_ge(root_ok, n + 1)
                pe.matmul(var[:, :], keep.heads[:, :], sq[b][:, :], start=True, stop=True).then_inc(var_mm, 1)
            instances(pe, body)

        @block.vector
        def _(dve):
            dve.memset(eps[:, :], GN_EPS).then_inc(eps_ok, 1)
            dve.sem_inc(ya_ok, 2)

            def body(n, m, b, p, col):
                dve.wait_ge(y_in[b], m * 112 + 112)
                dve.tensor_scalar(pp[b][:, 0:3], keep.par[:, PC["rwkv_r_k"]:PC["rwkv_r_k"] + 3 * PAIRS].rearrange(
                    "p (v q) -> p v q", q=PAIRS)[:, :, ds(p, 1)].rearrange("p v q -> p (v q)"), 1.0, None, ALU.mult).then_inc(par_ok, 1)
                dve.tensor_tensor(yf[b][:, :], yf[b][:, :], yr[b][:, :], ALU.add).then_inc(y_sum, 1)
                dve.wait_ge(par_ok, n + 1)
                dve.scalar_tensor_tensor(rk[b][:, :], r[b][:, :], pp[b][:, 0:1], k[b][:, :], ALU.mult, ALU.mult).then_inc(rk_ok, 1)
                dve.wait_ge(sums_mm, n + 1)
                dve.scalar_tensor_tensor(yc[b][:, :], mean[:, :], -1.0 / HEAD, yf[b][:, :], ALU.mult, ALU.add).then_inc(mid_ok, 1)
                dve.tensor_tensor(v[b][:, :], v[b][:, :], bonus[:, :], ALU.mult).then_inc(bonus_ok, 1)
                dve.wait_ge(root_ok, n + 2)
                dve.reciprocal(rt[b][:, :], rt[b][:, :]).then_inc(inv_ok, 1)
                dve.wait_ge(inv_ok, n + 1)
                dve.tensor_tensor(yc[b][:, :], yc[b][:, :], rt[b][:, :], ALU.mult).then_inc(norm_ok, 1)
                dve.wait_ge(norm_ok, n + 1)
                dve.scalar_tensor_tensor(yc[b][:, :], yc[b][:, :], pp[b][:, 1:2], v[b][:, :], ALU.mult, ALU.add).then_inc(affine_ok, 1)
                dve.wait_ge(affine_ok, n + 1)
                dve.wait_ge(ya_free, n + 1)
                dve.scalar_tensor_tensor(out[b][:, :], yc[b][:, :], pp[b][:, 2:3], gate[:, :], ALU.add, ALU.mult).then_inc(ya_ok, 1)
            instances(dve, body)

        @block.gpsimd
        def _(pool):
            pool.sem_inc(ya_free, 2)

            def body(n, m, b, p, col):
                pool.wait_ge(ya_ok, n + 3)
                pool.dma_start(YA[ds(p, 1), :, ds(col, NT)].rearrange("m p t -> (m p) t"), out[b][:, :]).then_inc(stored, 16)
                pool.wait_ge(stored, n * 16 + 16)
                pool.sem_inc(ya_free, 1)
            instances(pool, body)


def merge(nc, a, keep, YA, YB, GT, merged):
    with ExitStack() as ctx:
        c = Core(nc, ctx, "merge")
        NT, K4 = 512, D_RWKV // P
        wa, wb = c.sb("w_branch_a", [P, K4, D]), c.sb("w_branch_b", [P, K4, D])
        ya = [c.sb(f"ya{b}", [P, K4, NT]) for b in range(2)]
        yb = [c.sb(f"yb{b}", [P, K4, NT]) for b in range(2)]
        ga = [c.sb(f"gate{j}", [P, 2, NT]) for j in range(2)]
        t = [c.sb(f"gated{j}", [P, 2, NT]) for j in range(2)]
        acc = [[c.ps(f"branch{j}{x}", [P, NT]) for x in range(2)] for j in range(2)]
        w_in_, y_in = c.sem("w_branch_in"), [c.sem(f"y_in{b}") for b in range(2)]
        g_in = [c.sem(f"gate_in{j}") for j in range(2)]
        mm_ok, gated, summed = c.sem("branch_mm"), c.sem("gated"), c.sem("summed")
        block = ctx.enter_context(nc.Block())

        @block.sync
        def _(sp):
            sp.dma_start(wa[:, :, :], a["w_branch_a"][0].rearrange("(k p) n -> p k n", p=P)).then_inc(w_in_, 16)
            sp.dma_start(wb[:, :, :], a["w_branch_b"][0].rearrange("(k p) n -> p k n", p=P)).then_inc(w_in_, 16)
            with sp.Fori(0, 2) as i:
                for b in range(2):
                    sp.wait_ge(summed, i * 16 + (8 * b + 8))
                    cols = ds(i * (2 * NT) + b * NT, NT)
                    for src, dst in ((YA, ya), (YB, yb)):
                        sp.dma_start(dst[b][:, :, :], src[:, :, cols].rearrange("m p t -> p m t")).then_inc(y_in[b], 16)
                    for m in range(KD):
                        j = m % 2
                        sp.wait_ge(summed, i * 16 + (8 * b + m + 15))
                        sp.dma_start(ga[j][:, :, :], GT.rearrange("(x m) p t -> m p x t", x=2)[m][:, :, cols]).then_inc(g_in[j], 16)

        @block.tensor
        def _(pe):
            pe.wait_ge(w_in_, 32)
            with pe.Fori(0, 2) as i:
                for b in range(2):
                    pe.wait_ge(y_in[b], i * 32 + 32)
                    for m in range(KD):
                        j = m % 2
                        pe.wait_ge(gated, i * 32 + (16 * b + 2 * m + 2))
                        for x, (w, y) in enumerate(((wa, ya), (wb, yb))):
                            for k in range(K4):
                                mm = pe.matmul(acc[j][x][:, :], w[:, k, m * P:(m + 1) * P], y[b][:, k, :], start=k == 0, stop=k == K4 - 1)
                        mm.then_inc(mm_ok, 1)

        @block.vector
        def _(dve):
            dve.sem_inc(gated, 4)
            dve.sem_inc(summed, 16)
            with dve.Fori(0, 2) as i:
                for b in range(2):
                    for m in range(KD):
                        j = m % 2
                        dve.wait_ge(mm_ok, i * 16 + (8 * b + m + 1))
                        dve.wait_ge(g_in[j], i * 128 + 16 * (4 * b + m // 2 + 1))
                        for x in range(2):
                            dve.tensor_tensor(t[j][:, x, :], ga[j][:, x, :], acc[j][x][:, :], ALU.mult).then_inc(gated, 1)
                        dve.wait_ge(gated, i * 32 + (16 * b + 2 * m + 6))
                        dve.tensor_tensor(merged[:, m, ds(i * (2 * NT) + b * NT, NT)], t[j][:, 0, :], t[j][:, 1, :],
                                          ALU.add).then_inc(summed, 1)


def row_of(pe, acc, keep, row, col):
    return pe.matmul(acc, keep.ones[0:1, 0:P], keep.mod[0:1, row * D + col:row * D + col + 512], start=True, stop=True)


def residual(nc, a, keep, merged, X2, H2):
    with ExitStack() as ctx:
        c = Core(nc, ctx, "residual")
        NR = N_GRP + N_EXP

        def two(name, shape):
            return [c.sb(f"{name}{b}", list(shape)) for b in range(2)]
        wo, wr = c.sb("w_out", [P, KD, D]), c.sb("w_router", [P, KD, NR])
        br, gt, sc, sh = c.sb("b_router", [P, NR]), c.sb("gt1_all", [P, D]), c.sb("scale2_all", [P, D]), c.sb("shift2_all", [P, D])
        ms, xt, x2, h2, hT = two("merged_tile", (P, KD, P)), two("x_tile", (P, D)), two("x2", (P, D)), two("h2", (P, D)), two("h2_turned", (P, KD, P))
        sq = c.sb("x2_sq", [P, D])
        ss, rt, rs, eps = c.sb("sum_sq", [P, 2]), c.sb("root", [P, 2]), c.sb("rstd", [P, 2]), c.sb("eps", [P, 1])
        acc = [[c.ps(f"out{b}{h}", [P, 512]) for h in range(2)] for b in range(2)]
        turn = [c.ps(f"h2_turn{h}", [P, 512]) for h in range(2)]
        lg = c.ps("logits", [P, NR])
        const_in, x_in = c.sem("const_in"), [c.sem(f"x_in{b}") for b in range(2)]
        r_in = c.sem("router_in")
        st = [c.sem(f"rows_stored{b}") for b in range(2)]
        names = ("rows_mm", "rows_ok", "copied", "out_mm", "gated", "x2_ok", "sq_ok", "root_ok", "rstd_ok", "normed", "scaled", "h2_ok",
                 "turn_mm", "turn_ok", "lg_mm", "lg_ok", "eps_ok")
        (rows_mm, rows_ok, copied, out_mm, gated, x2_ok, sq_ok, root_ok, rstd_ok, normed, scaled, h2_ok, turn_mm, turn_ok, lg_mm, lg_ok,
         eps_ok) = (c.sem(n) for n in names)
        block = ctx.enter_context(nc.Block())

        @block.sync
        def _(sp):
            sp.dma_start(wo[:, :, :], a["w_out"][0].rearrange("(k p) n -> p k n", p=P)).then_inc(const_in, 16)
            sp.dma_start(wr[:, :, 0:N_GRP], a["moe_grp_w"][0].rearrange("(k p) n -> p k n", p=P)).then_inc(const_in, 16)
            sp.dma_start(wr[:, :, N_GRP:NR], a["moe_exp_w"][0].rearrange("(k p) n -> p k n", p=P)).then_inc(const_in, 16)
            sp.dma_start(br[:, 0:N_GRP], a["moe_grp_b"].to_broadcast([P, N_GRP])).then_inc(const_in, 16)
            sp.dma_start(br[:, N_GRP:NR], a["moe_exp_b"].to_broadcast([P, N_EXP])).then_inc(const_in, 16)
            sp.dma_start(sq[:, :], a["norm2_g"].to_broadcast([P, D])).then_inc(const_in, 16)
            for b in range(2):
                sp.sem_inc(st[b], 32)
            with sp.Fori(0, TILES // 2) as i:
                for b in range(2):
                    rows = ds(i * (2 * P) + b * P, P)
                    n = i * 2 + b
                    sp.wait_ge(x2_ok, n * 2 + 2)
                    sp.dma_start(xt[b][:, :], a["x"][0][rows, :]).then_inc(x_in[b], 16)
                    sp.wait_ge(x2_ok, n * 2 + 6)
                    sp.dma_start(X2[rows, :], x2[b][:, :]).then_inc(st[b], 16)
                    sp.wait_ge(h2_ok, n + 1)
                    sp.dma_start(H2[rows, :], h2[b][:, :]).then_inc(st[b], 16)
            for b in range(2):
                sp.wait_ge(st[b], 32 + 32 * (TILES // 2))

        @block.gpsimd
        def _(pool):
            with pool.Fori(0, TILES // 2) as i:
                for b in range(2):
                    pool.wait_ge(out_mm, i * 2 + b + 1)
                    pool.tensor_copy(ms[b][:, :, :], merged[:, :, ds(i * (2 * P) + b * P, P)]).then_inc(copied, 1)

        @block.tensor
        def _(pe):
            pe.sem_inc(out_mm, 2)
            for j, row in enumerate((2, 4, 3)):
                for h in range(2):
                    if j == 2:
                        pe.wait_ge(rows_ok, 2)
                    mm = row_of(pe, acc[j % 2][h][:, :], keep, row, h * 512)
                mm.then_inc(rows_mm, 1)
            pe.wait_ge(const_in, 96)
            pe.wait_ge(rows_ok, 7)

            def out(n, b):
                pe.wait_ge(copied, n + 1)
                pe.wait_ge(gated, n * 2 + 2)
                for h in range(2):
                    for k in range(KD):
                        mm = pe.matmul(acc[b][h][:, :], ms[b][:, k, :], wo[:, k, h * 512:(h + 1) * 512], start=k == 0, stop=k == KD - 1)
                mm.then_inc(out_mm, 1)

            def router(n, b):
                pe.wait_ge(h2_ok, n + 1)
                pe.wait_ge(turn_ok, n * 2 + 2)
                for k in range(KD):
                    mm = pe.transpose(turn[k // 4][:, (k % 4) * P:(k % 4 + 1) * P], h2[b][:, k * P:(k + 1) * P], keep.ident[:, :])
                mm.then_inc(turn_mm, 1)
                pe.wait_ge(turn_ok, n * 2 + 4)
                pe.wait_ge(lg_ok, n + 1)
                for k in range(KD):
                    mm = pe.matmul(lg[:, :], hT[b][:, k, :], wr[:, k, :], start=k == 0, stop=k == KD - 1)
                mm.then_inc(lg_mm, 1)
            out(0, 0)
            with pe.Fori(0, TILES // 2 - 1) as i:
                out(i * 2 + 1, 1)
                router(i * 2, 0)
                out(i * 2 + 2, 0)
                router(i * 2 + 1, 1)
            out(TILES - 1, 1)
            router(TILES - 2, 0)
            router(TILES - 1, 1)

        @block.scalar
        def _(act):
            act.sem_inc(turn_ok, 2)
            act.wait_ge(eps_ok, 1)
            act.wait_ge(rows_ok, 7)
            with act.Fori(0, TILES // 2) as i:
                for b in range(2):
                    n = i * 2 + b
                    act.wait_ge(x2_ok, n * 2 + 6)
                    act.activation(sq[:, :], x2[b][:, :], ACT.Square, accum_out=ss[:, b:b + 1]).then_inc(sq_ok, 1)
                    act.wait_ge(sq_ok, n + 1)
                    act.activation(rt[:, b:b + 1], ss[:, b:b + 1], ACT.Sqrt, bias=eps[:, :], scale=1.0 / D).then_inc(root_ok, 1)
                    act.wait_ge(rstd_ok, n + 1)
                    act.wait_ge(st[b], i * 32 + 32)
                    act.wait_ge(turn_mm, n + 1)
                    act.activation(h2[b][:, :], x2[b][:, :], ACT.Copy, scale=rs[:, b:b + 1]).then_inc(normed, 1)
                    act.wait_ge(turn_mm, n + 3)
                    for h in range(2):
                        act.activation(hT[b][:, 4 * h:4 * h + 4, :].rearrange("p k t -> p (k t)"), turn[h][:, :], ACT.Copy).then_inc(turn_ok, 1)

        @block.vector
        def _(dve):
            dve.memset(eps[:, :], NORM_EPS).then_inc(eps_ok, 1)
            dve.sem_inc(gated, 4)
            dve.sem_inc(x2_ok, 4)
            dve.sem_inc(lg_ok, 1)
            dve.sem_inc(turn_mm, 2)
            for j, dst in enumerate((gt, sc, sh)):
                dve.wait_ge(rows_mm, j + 1)
                for h in range(2):
                    dve.tensor_copy(dst[:, h * 512:(h + 1) * 512], acc[j % 2][h][:, :]).then_inc(rows_ok, 1)
            dve.wait_ge(const_in, 96)
            dve.wait_ge(rows_ok, 4)
            dve.scalar_tensor_tensor(sc[:, :], sc[:, :], 1.0, sq[:, :], ALU.add, ALU.mult).then_inc(rows_ok, 1)
            dve.wait_ge(rows_ok, 7)

            def first(n, i, b):
                dve.wait_ge(out_mm, n + 3)
                dve.wait_ge(x_in[b], i * 16 + 16)
                dve.wait_ge(st[b], i * 32 + 32)
                for h in range(2):
                    cols = slice(h * 512, (h + 1) * 512)
                    dve.tensor_tensor(x2[b][:, cols], acc[b][h][:, :], gt[:, cols], ALU.mult).then_inc(gated, 1)
                for h in range(2):
                    cols = slice(h * 512, (h + 1) * 512)
                    dve.wait_ge(gated, n * 2 + (5 + h))
                    dve.tensor_tensor(x2[b][:, cols], x2[b][:, cols], xt[b][:, cols], ALU.add).then_inc(x2_ok, 1)
                dve.wait_ge(root_ok, n + 1)
                dve.reciprocal(rs[:, b:b + 1], rt[:, b:b + 1]).then_inc(rstd_ok, 1)
                dve.wait_ge(normed, n + 1)
                dve.tensor_tensor(h2[b][:, :], h2[b][:, :], sc[:, :], ALU.mult).then_inc(scaled, 1)
                dve.wait_ge(scaled, n + 1)
                dve.tensor_tensor(h2[b][:, :], h2[b][:, :], sh[:, :], ALU.add).then_inc(h2_ok, 1)

            def second(n):
                dve.wait_ge(lg_mm, n + 1)
                dve.tensor_tensor(keep.logits[:, ds(n, 1), :].rearrange("p n e -> p (n e)"), lg[:, :], br[:, :], ALU.add).then_inc(lg_ok, 1)
            first(0, 0, 0)
            with dve.Fori(0, TILES // 2 - 1) as i:
                second(i * 2)
                first(i * 2 + 1, i, 1)
                second(i * 2 + 1)
                first(i * 2 + 2, i + 1, 0)
            second(TILES - 2)
            first(TILES - 1, TILES // 2 - 1, 1)
            second(TILES - 1)


def routing(nc, a, keep, ROWTOK):
    with ExitStack() as ctx:
        c = Core(nc, ctx, "routing")
        G, E, N, T16 = N_GRP, PER_GRP, N_EXP, TILES
        BIG = 1e30

        g3, gm, gi, goh = c.sb("grp_tmp", [P, T16, G]), c.sb("grp_max", [P, T16]), c.sb("grp_first", [P, T16]), c.sb("grp_hot", [P, T16, G])
        ge, pg = c.sb("grp_exp", [P, T16, G]), c.sb("p_grp", [P, T16])
        mix, sel, s3 = c.sb("grp_logits", [P, T16, G, E]), c.sb("selected", [P, T16, E]), c.sb("sel_tmp", [P, T16, E])
        v = [c.sb(f"top{j}", [P, T16]) for j in range(2)]
        vi = c.sb("top_first", [P, T16])
        hot = [c.sb(f"hot{j}", [P, T16, E]) for j in range(2)]
        M = [c.sb(f"mask{j}", [P, T16, G, E]) for j in range(3)]
        big4, big8 = c.sb("iota_grp", [P, G]), c.sb("iota_exp", [P, E])
        iota16, iota64, tok = c.sb("iota_blocks", [P, TILES]), c.sb("iota_all_blocks", [P, N_BLOCKS]), c.sb("token", [P, T16])
        tri = c.sb("before", [P, P])
        dv, e1 = c.sb("v_diff", [P, T16]), c.sb("v_exp", [P, T16])
        base, tot, slot = c.sb("tile_base", [P, T16, N]), c.sb("tile_total", [P, T16, N]), c.sb("slot_of", [P, T16, N])
        cnt, cmp1, nb, pend, pst = (c.sb("count", [P, N]), c.sb("count_cmp", [P, N, TILES]), c.sb("n_blocks", [P, N]), c.sb("end_block", [P, N]),
                                    c.sb("first_slot", [P, N]))
        cmp2, be, pr = c.sb("block_cmp", [P, N_BLOCKS, N]), c.sb("block_exp", [P, N_BLOCKS]), c.sb("prod", [P, T16, N])
        dest = [c.sb(f"dest{j}", [P, T16]) for j in range(2)]
        zero, rows = c.sb("zero_rows", [N_BLOCKS, P]), c.sb("slot_rows", [N_BLOCKS, P])
        cum, total, turn = c.ps("cum", [P, T16 * N]), c.ps("total", [P, T16 * N]), c.ps("slot_turn", [P, N_BLOCKS])
        iota_ok, chain, act_ok, hot_mm, dest_ok = c.sem("iota_ok"), c.sem("chain"), c.sem("act_ok"), c.sem("hot_mm"), c.sem("dest_ok")
        tri0, zero_out, scattered, rows_in, turned, split_ok = (c.sem("tri0"), c.sem("zero_out"), c.sem("scattered"), c.sem("rows_in"),
                                                               c.sem("turned"), c.sem("hot_ok"))
        masks_ok = c.sem("masks_ok")
        block = ctx.enter_context(nc.Block())
        LG, LE = keep.logits[:, :, 0:G], keep.logits[:, :, G:G + N].rearrange("p t (g e) -> p t g e", g=G)
        flat = lambda x: x.rearrange("p t g e -> p (t g e)")
        by_exp = lambda x: x.rearrange("p t g e -> p t (g e)")

        @block.gpsimd
        def _(pool):
            pool.memset(tri[:, :], 1.0).then_inc(tri0, 1)
            pool.memset(zero[:, :], 0.0).then_inc(tri0, 1)
            pool.iota(big4[:, :], pattern=[[1, G]], base=0, channel_multiplier=0, allow_small_or_imprecise_dtypes=True).then_inc(iota_ok, 1)
            pool.iota(big8[:, :], pattern=[[1, E]], base=0, channel_multiplier=0, allow_small_or_imprecise_dtypes=True).then_inc(iota_ok, 1)
            pool.iota(iota16[:, :], pattern=[[SLOTS_BLOCK, TILES]], base=0, channel_multiplier=0,
                      allow_small_or_imprecise_dtypes=True).then_inc(iota_ok, 1)
            pool.iota(iota64[:, :], pattern=[[1, N_BLOCKS]], base=0, channel_multiplier=0,
                      allow_small_or_imprecise_dtypes=True).then_inc(iota_ok, 1)
            pool.iota(tok[:, :], pattern=[[P, T16]], base=0, channel_multiplier=1, allow_small_or_imprecise_dtypes=True).then_inc(iota_ok, 1)
            pool.wait_ge(tri0, 2)
            pool.affine_select(out=tri[:, :], in_=tri[:, :], compare_op=ALU.is_gt, fill=0.0, base=0, pattern=[[1, P]],
                               channel_multiplier=-1).then_inc(iota_ok, 1)
            pool.dma_start(ROWTOK.rearrange("(b p) o -> b (p o)", p=P), zero[:, :]).then_inc(zero_out, 16)
            pool.wait_ge(zero_out, 16)
            pool.wait_ge(dest_ok, 2)
            for j in range(2):
                for t in range(T16):
                    pool.indirect_dma_start(out=ROWTOK, out_offset=bass.IndirectOffsetOnAxis(ap=keep.dest[j][:, t:t + 1], axis=0),
                                            in_=tok[:, t:t + 1], in_offset=None).then_inc(scattered, 16)
            pool.wait_ge(scattered, 16 * 2 * T16)
            pool.dma_start(rows[:, :], ROWTOK.rearrange("(b p) o -> b (p o)", p=P)).then_inc(rows_in, 16)

        @block.scalar
        def _(act):
            act.wait_ge(split_ok, 1)
            act.activation(ge[:, :, :], g3[:, :, :], ACT.Exp).then_inc(act_ok, 1)
            act.wait_ge(split_ok, 2)
            act.activation(e1[:, :], dv[:, :], ACT.Exp).then_inc(act_ok, 1)

        @block.tensor
        def _(pe):
            pe.wait_ge(iota_ok, 6)
            pe.wait_ge(masks_ok, 1)
            pe.matmul(cum[:, :], tri[:, :], flat(M[2][:, :, :, :]), start=True, stop=True)
            pe.matmul(total[:, :], keep.ones[:, 0:P], flat(M[2][:, :, :, :]), start=True, stop=True).then_inc(hot_mm, 1)
            pe.wait_ge(rows_in, 16)
            pe.transpose(turn[:, :], rows[:, :], keep.ident[0:N_BLOCKS, 0:N_BLOCKS]).then_inc(turned, 1)

        @block.vector
        def _(dve):
            done = [0]

            def link(ins):
                done[0] += 1
                ins.then_inc(chain, 1)
                dve.wait_ge(chain, done[0])

            bt = lambda x, n: x[:, :, None].to_broadcast([P, T16, n])

            def first_of(dst_hot, vals, top, iota, first, tmp, n):
                link(dve.tensor_tensor(tmp, vals, bt(top, n), ALU.is_lt))
                link(dve.scalar_tensor_tensor(tmp, tmp, BIG, iota[:, None, :].to_broadcast([P, T16, n]), ALU.mult, ALU.add))
                link(dve.tensor_reduce(first, tmp, AX.X, ALU.min))
                link(dve.tensor_tensor(dst_hot, iota[:, None, :].to_broadcast([P, T16, n]), bt(first, n), ALU.is_equal))

            dve.wait_ge(iota_ok, 6)
            link(dve.tensor_reduce(gm[:, :], LG, AX.X, ALU.max))
            dve.tensor_tensor(g3[:, :, :], LG, bt(gm, G), ALU.subtract).then_inc(split_ok, 1)
            dve.wait_ge(act_ok, 1)
            link(dve.tensor_reduce(pg[:, :], ge[:, :, :], AX.X, ALU.add))
            link(dve.reciprocal(pg[:, :], pg[:, :]))
            first_of(goh[:, :, :], LG, gm, big4, gi[:, :], g3[:, :, :], G)
            link(dve.tensor_tensor(mix[:, :, :, :], LE, goh[:, :, :, None].to_broadcast([P, T16, G, E]), ALU.mult))
            link(dve.tensor_reduce(sel[:, :, :], mix[:, :, :, :].rearrange("p t g e -> p t e g"), AX.X, ALU.add))
            for j in range(2):
                link(dve.tensor_reduce(v[j][:, :], sel[:, :, :], AX.X, ALU.max))
                first_of(hot[j][:, :, :], sel[:, :, :], v[j], big8, vi[:, :], s3[:, :, :], E)
                if j == 0:
                    link(dve.scalar_tensor_tensor(sel[:, :, :], hot[0][:, :, :], -BIG, sel[:, :, :], ALU.mult, ALU.add))
                link(dve.tensor_tensor(M[j][:, :, :, :], goh[:, :, :, None].to_broadcast([P, T16, G, E]),
                                       hot[j][:, :, None, :].to_broadcast([P, T16, G, E]), ALU.mult))
            dve.tensor_tensor(flat(M[2][:, :, :, :]), flat(M[0][:, :, :, :]), flat(M[1][:, :, :, :]), ALU.add).then_inc(masks_ok, 1)
            dve.tensor_tensor(dv[:, :], v[1][:, :], v[0][:, :], ALU.subtract).then_inc(split_ok, 1)
            dve.wait_ge(act_ok, 2)
            link(dve.tensor_scalar(dv[:, :], e1[:, :], 1.0, None, ALU.add))
            link(dve.reciprocal(dv[:, :], dv[:, :]))
            link(dve.tensor_tensor(keep.weights[:, 0, :], dv[:, :], pg[:, :], ALU.mult))
            link(dve.tensor_tensor(keep.weights[:, 1, :], keep.weights[:, 0, :], e1[:, :], ALU.mult))
            dve.wait_ge(hot_mm, 1)
            link(dve.tensor_copy(tot[:, :, :].rearrange("p t e -> p (t e)"), total[:, :]))
            link(dve.memset(base[:, 0, :], 0.0))
            for t in range(1, T16):
                link(dve.tensor_tensor(base[:, t, :], base[:, t - 1, :], tot[:, t - 1, :], ALU.add))
            link(dve.tensor_tensor(cnt[:, :], base[:, T16 - 1, :], tot[:, T16 - 1, :], ALU.add))
            link(dve.tensor_tensor(cmp1[:, :, :], cnt[:, :, None].to_broadcast([P, N, TILES]),
                                   iota16[:, None, :].to_broadcast([P, N, TILES]), ALU.is_gt))
            link(dve.tensor_reduce(nb[:, :], cmp1[:, :, :], AX.X, ALU.add))
            link(dve.tensor_tensor_scan(pend[:, :], keep.ones[:, 0:N], nb[:, :], 0.0, ALU.mult, ALU.add))
            link(dve.tensor_tensor(pst[:, :], pend[:, :], nb[:, :], ALU.subtract))
            link(dve.tensor_scalar(pst[:, :], pst[:, :], float(SLOTS_BLOCK), None, ALU.mult))
            link(dve.tensor_tensor(slot[:, :, :].rearrange("p t e -> p (t e)"), cum[:, :], base[:, :, :].rearrange("p t e -> p (t e)"), ALU.add))
            link(dve.tensor_tensor(slot[:, :, :], slot[:, :, :], pst[:, None, :].to_broadcast([P, T16, N]), ALU.add))
            for j in range(2):
                link(dve.tensor_tensor(pr[:, :, :], slot[:, :, :], by_exp(M[j][:, :, :, :]), ALU.mult))
                link(dve.tensor_reduce(dest[j][:, :], pr[:, :, :], AX.X, ALU.add))
                dve.tensor_copy(keep.dest[j][:, :], dest[j][:, :]).then_inc(dest_ok, 1)
            link(dve.tensor_tensor(cmp2[:, :, :], iota64[:, :, None].to_broadcast([P, N_BLOCKS, N]),
                                   pend[:, None, :].to_broadcast([P, N_BLOCKS, N]), ALU.is_ge))
            link(dve.tensor_reduce(be[:, :], cmp2[:, :, :], AX.X, ALU.add))
            link(dve.tensor_scalar(be[:, :], be[:, :], float(N_EXP - 1), None, ALU.min))
            link(dve.tensor_copy(keep.block_expert[:, :], be[:, :]))
            link(dve.tensor_scalar(keep.block_slot[:, :], keep.block_expert[:, :], 1, None, ALU.bitwise_and))
            link(dve.tensor_copy(keep.end_block[:, :], pend[:, :]))
            dve.wait_ge(turned, 1)
            link(dve.tensor_copy(keep.slot_token[:, :], turn[:, :]))


def experts(nc, a, keep, H2, YG):
    with ExitStack() as ctx:
        c = Core(nc, ctx, "experts")
        KE = D_EXP // P
        wg, wu, wd = c.sb("w_gate", [P, 2, KD, D_EXP]), c.sb("w_up", [P, 2, KD, D_EXP]), c.sb("w_down", [P, 2, KE, D])

        def two(name, shape, dt=F32):
            return [c.sb(f"{name}{b}", list(shape), dt) for b in range(2)]
        idx, xg, xT, sg, hh, hT, yo = (two("slot_token", (P, 1), I32), two("rows", (P, D)), two("rows_turned", (P, KD, P)), two("silu", (P, D_EXP)),
                                       two("hidden", (P, D_EXP)), two("hidden_turned", (P, KE, P)), two("y_rows", (P, D)))
        xp = [c.ps(f"row_turn{h}", [P, 512]) for h in range(2)]
        gp, up, hp = c.ps("gate", [P, D_EXP]), c.ps("up", [P, D_EXP]), c.ps("hidden_turn", [P, 512])
        yp = [c.ps(f"down{h}", [P, 512]) for h in range(2)]
        w_in_ = [c.sem(f"w_in{b}") for b in range(2)]
        x_in = [c.sem(f"x_in{b}") for b in range(2)]
        gather_go = c.sem("gather_go")
        y_out = [c.sem(f"y_out{b}") for b in range(2)]
        names = ("w_ready", "idx_ok", "x_used", "xturn_mm", "xturn_ok", "gate_mm", "up_mm", "silu_ok", "hid_ok", "hturn_mm", "hturn_ok",
                 "down_mm", "y_ok")
        (w_ready, idx_ok, x_used, xturn_mm, xturn_ok, gate_mm, up_mm, silu_ok, hid_ok, hturn_mm, hturn_ok, down_mm,
         y_ok) = (c.sem(n) for n in names)
        block = ctx.enter_context(nc.Block())

        @block.sync
        def _(sp):
            def load(e, s):
                for dst, src in ((wg, "moe_w_gate"), (wu, "moe_w_up"), (wd, "moe_w_down")):
                    sp.dma_start(dst[:, s, :, :], a[src][0, ds(e, 1), :, :].rearrange("e (k p) n -> p (e k) n", p=P)).then_inc(w_in_[s], 16)
            load(0, 0)
            load(1, 1)
            sp.wait_ge(w_in_[0], 48)
            sp.sem_inc(w_ready, 1)
            with sp.Fori(0, N_EXP // 2 - 1) as i:
                for s in range(2):
                    end = sp.value_load(keep.end_block[0:1, ds(i * 2 + s, 1)], min_val=0, max_val=N_BLOCKS)
                    sp.wait_ge(down_mm, end + 1)
                    load(i * 2 + (2 + s), s)
                    if s == 0:
                        sp.wait_ge(w_in_[1], i * 48 + 48)
                    else:
                        sp.wait_ge(w_in_[0], i * 48 + 96)
                    sp.sem_inc(w_ready, 1)
            sp.wait_ge(w_in_[1], 48 * (N_EXP // 2))
            sp.sem_inc(w_ready, 1)

        @block.gpsimd
        def _(pool):
            with pool.Fori(0, N_BLOCKS // 2) as i:
                for b in range(2):
                    pool.wait_ge(idx_ok, i * 2 + b + 1)
                    pool.wait_ge(xturn_mm, i * 2 + b + 1)
                    pool.sem_inc(gather_go, 1)
                    pool.indirect_dma_start(out=xg[b][:, :], out_offset=None, in_=H2,
                                            in_offset=bass.IndirectOffsetOnAxis(ap=idx[b][:, :], axis=0)).then_inc(x_in[b], 16)

        @block.tensor
        def _(pe):
            pe.sem_inc(xturn_mm, 2)
            pe.sem_inc(down_mm, 1)

            def turn(n, i, b):
                pe.wait_ge(x_in[b], i * 16 + 16)
                pe.wait_ge(xturn_ok, n * 2 + 2)
                for k in range(KD):
                    mm = pe.transpose(xp[k // 4][:, (k % 4) * P:(k % 4 + 1) * P], xg[b][:, k * P:(k + 1) * P], keep.ident[:, :])
                mm.then_inc(xturn_mm, 1)

            def hidden(n, b):
                e = pe.value_load(keep.block_expert[0:1, ds(n, 1)], min_val=0, max_val=N_EXP - 1)
                s = pe.value_load(keep.block_slot[0:1, ds(n, 1)], min_val=0, max_val=1)
                pe.wait_ge(w_ready, e + 1)
                pe.wait_ge(xturn_ok, n * 2 + 4)
                pe.wait_ge(silu_ok, n + 1)
                for k in range(KD):
                    mm = pe.matmul(gp[:, :], xT[b][:, k, :], wg[:, ds(s, 1), k, :].rearrange("p s n -> p (s n)"), start=k == 0, stop=k == KD - 1)
                mm.then_inc(gate_mm, 1)
                pe.wait_ge(hid_ok, n + 1)
                for k in range(KD):
                    mm = pe.matmul(up[:, :], xT[b][:, k, :], wu[:, ds(s, 1), k, :].rearrange("p s n -> p (s n)"), start=k == 0, stop=k == KD - 1)
                mm.then_inc(up_mm, 1)
                return s

            def down(n, b, s):
                pe.wait_ge(hid_ok, n + 2)
                for k in range(KE):
                    mm = pe.transpose(hp[:, k * P:(k + 1) * P], hh[b][:, k * P:(k + 1) * P], keep.ident[:, :])
                mm.then_inc(hturn_mm, 1)
                pe.wait_ge(hturn_ok, n + 1)
                pe.wait_ge(y_ok, n * 2 + 2)
                for h in range(2):
                    for k in range(KE):
                        mm = pe.matmul(yp[h][:, :], hT[b][:, k, :], wd[:, ds(s, 1), k, h * 512:(h + 1) * 512].rearrange("p s n -> p (s n)"),
                                       start=k == 0, stop=k == KE - 1)
                mm.then_inc(down_mm, 1)
            turn(0, 0, 0)
            with pe.Fori(0, N_BLOCKS // 2 - 1) as i:
                s = hidden(i * 2, 0)
                turn(i * 2 + 1, i, 1)
                down(i * 2, 0, s)
                s = hidden(i * 2 + 1, 1)
                turn(i * 2 + 2, i + 1, 0)
                down(i * 2 + 1, 1, s)
            s = hidden(N_BLOCKS - 2, 0)
            turn(N_BLOCKS - 1, N_BLOCKS // 2 - 1, 1)
            down(N_BLOCKS - 2, 0, s)
            s = hidden(N_BLOCKS - 1, 1)
            down(N_BLOCKS - 1, 1, s)

        @block.scalar
        def _(act):
            act.sem_inc(xturn_ok, 2)
            act.sem_inc(silu_ok, 1)
            for b in range(2):
                act.sem_inc(y_out[b], 16)

            def turned(n, b):
                act.wait_ge(xturn_mm, n + 3)
                for h in range(2):
                    act.activation(xT[b][:, 4 * h:4 * h + 4, :].rearrange("p k t -> p (k t)"), xp[h][:, :], ACT.Copy).then_inc(xturn_ok, 1)

            def rest(n, i, b, more):
                act.wait_ge(gate_mm, n + 1)
                act.activation(sg[b][:, :], gp[:, :], ACT.Silu).then_inc(silu_ok, 1)
                if more is not None:
                    turned(n + 1, 1 - b)
                act.wait_ge(hturn_mm, n + 1)
                act.activation(hT[b][:, :, :].rearrange("p k t -> p (k t)"), hp[:, :], ACT.Copy).then_inc(hturn_ok, 1)
                act.wait_ge(y_ok, n * 2 + 4)
                act.dma_start(YG[ds(n * P, P), :], yo[b][:, :]).then_inc(y_out[b], 16)
            turned(0, 0)
            with act.Fori(0, N_BLOCKS // 2 - 1) as i:
                rest(i * 2, i, 0, True)
                rest(i * 2 + 1, i, 1, True)
            rest(N_BLOCKS - 2, 0, 0, True)
            rest(N_BLOCKS - 1, 0, 1, None)
            for b in range(2):
                act.wait_ge(y_out[b], 16 + 16 * (N_BLOCKS // 2))

        @block.vector
        def _(dve):
            dve.sem_inc(hid_ok, 1)
            dve.sem_inc(y_ok, 2)

            def index(n, b):
                dve.tensor_scalar(idx[b][:, :], keep.slot_token[:, ds(n, 1)], 0.0, None, ALU.add).then_inc(idx_ok, 1)
            for b in range(2):
                index(b, b)

            def rest(n, i, b, more):
                dve.wait_ge(up_mm, n + 1)
                dve.wait_ge(silu_ok, n + 2)
                dve.tensor_tensor(hh[b][:, :], sg[b][:, :], up[:, :], ALU.mult).then_inc(hid_ok, 1)
                dve.wait_ge(down_mm, n + 2)
                dve.wait_ge(y_out[b], i * 16 + 16)
                for h in range(2):
                    dve.tensor_copy(yo[b][:, h * 512:(h + 1) * 512], yp[h][:, :]).then_inc(y_ok, 1)
                if more:
                    dve.wait_ge(xturn_mm, n + 3)
                    index(n + 2, b)
            with dve.Fori(0, N_BLOCKS // 2 - 1) as i:
                for b in range(2):
                    rest(i * 2 + b, i, b, True)
            for b in range(2):
                rest(N_BLOCKS - 2 + b, N_BLOCKS // 2 - 1, b, False)


def combine(nc, a, keep, X2, YG, out):
    with ExitStack() as ctx:
        c = Core(nc, ctx, "combine")

        def two(name, shape, dt=F32):
            return [c.sb(f"{name}{b}", list(shape), dt) for b in range(2)]
        gt, gf = c.sb("gt2_all", [P, D]), c.sb("final_g_all", [P, D])
        y0, y1, xt, ot, wt = two("y_first", (P, D)), two("y_second", (P, D)), two("x2", (P, D)), two("out", (P, D)), two("weights", (P, 2))
        idxs = [[c.sb(f"slot{j}{b}", [P, 1], I32) for j in range(2)] for b in range(2)]
        sq, ss, rt, rs, eps = c.sb("sq", [P, D]), c.sb("sum_sq", [P, 2]), c.sb("root", [P, 2]), c.sb("rstd", [P, 2]), c.sb("eps", [P, 1])
        acc = [c.ps(f"row{h}", [P, 512]) for h in range(2)]
        gather_go = c.sem("gather_go")
        y_in, x_in, o_out = ([c.sem(f"{x}{b}") for b in range(2)] for x in ("y_in", "x_in", "o_out"))
        names = ("const_in", "rows_mm", "rows_ok", "cols_ok", "first_ok", "both_ok", "gated", "x3_ok", "sq_ok", "root_ok", "rstd_ok", "out_ok",
                 "eps_ok")
        (const_in, rows_mm, rows_ok, cols_ok, first_ok, both_ok, gated, x3_ok, sq_ok, root_ok, rstd_ok, out_ok,
         eps_ok) = (c.sem(n) for n in names)
        block = ctx.enter_context(nc.Block())

        @block.sync
        def _(sp):
            sp.dma_start(gf[:, :], a["final_norm_g"].rearrange("(o n) -> o n", o=1).to_broadcast([P, D])).then_inc(const_in, 16)
            for b in range(2):
                sp.sem_inc(o_out[b], 16)
            for b in range(2):
                sp.dma_start(xt[b][:, :], X2[b * P:(b + 1) * P, :]).then_inc(x_in[b], 16)

            def store(n, b, row):
                sp.wait_ge(out_ok, n + 1)
                sp.dma_start(out[0][ds(row, P), :], ot[b][:, :]).then_inc(o_out[b], 16)
            with sp.Fori(0, TILES // 2 - 1) as i:
                for b in range(2):
                    store(i * 2 + b, b, i * (2 * P) + b * P)
                    sp.dma_start(xt[b][:, :], X2[ds(i * (2 * P) + (2 + b) * P, P), :]).then_inc(x_in[b], 16)
            for b in range(2):
                store(TILES - 2 + b, b, (TILES - 2 + b) * P)
            for b in range(2):
                sp.wait_ge(o_out[b], 16 + 16 * (TILES // 2))

        @block.gpsimd
        def _(pool):
            with pool.Fori(0, TILES // 2) as i:
                for b in range(2):
                    n = i * 2 + b
                    pool.wait_ge(cols_ok, n * 3 + 3)
                    pool.wait_ge(x3_ok, n + 1)
                    pool.sem_inc(gather_go, 1)
                    for j, y in enumerate((y0, y1)):
                        pool.indirect_dma_start(out=y[b][:, :], out_offset=None, in_=YG,
                                                in_offset=bass.IndirectOffsetOnAxis(ap=idxs[b][j][:, :], axis=0)).then_inc(y_in[b], 16)

        @block.tensor
        def _(pe):
            for h in range(2):
                mm = row_of(pe, acc[h][:, :], keep, 5, h * 512)
            mm.then_inc(rows_mm, 1)

        @block.scalar
        def _(act):
            act.wait_ge(eps_ok, 1)
            act.wait_ge(rows_ok, 2)
            with act.Fori(0, TILES // 2) as i:
                for b in range(2):
                    n = i * 2 + b
                    act.wait_ge(y_in[b], i * 32 + 32)
                    act.activation(y0[b][:, :], y0[b][:, :], ACT.Copy, scale=wt[b][:, 0:1]).then_inc(first_ok, 1)
                    act.wait_ge(x3_ok, n + 3)
                    act.activation(sq[:, :], xt[b][:, :], ACT.Square, accum_out=ss[:, b:b + 1]).then_inc(sq_ok, 1)
                    act.wait_ge(sq_ok, n + 1)
                    act.activation(rt[:, b:b + 1], ss[:, b:b + 1], ACT.Sqrt, bias=eps[:, :], scale=1.0 / D).then_inc(root_ok, 1)

        @block.vector
        def _(dve):
            dve.memset(eps[:, :], NORM_EPS).then_inc(eps_ok, 1)
            dve.sem_inc(both_ok, 2)
            dve.sem_inc(x3_ok, 2)
            dve.wait_ge(rows_mm, 1)
            for h in range(2):
                dve.tensor_copy(gt[:, h * 512:(h + 1) * 512], acc[h][:, :]).then_inc(rows_ok, 1)
            dve.wait_ge(rows_ok, 2)
            dve.wait_ge(const_in, 16)

            def columns(n, b):
                for j in range(2):
                    dve.tensor_scalar(idxs[b][j][:, :], keep.dest[j][:, ds(n, 1)], 0.0, None, ALU.add).then_inc(cols_ok, 1)
                w = keep.weights[:, :, ds(n, 1)].rearrange("p j n -> p (j n)")
                dve.tensor_scalar(wt[b][:, :], w, 1.0, None, ALU.mult).then_inc(cols_ok, 1)

            def tile(n, i, b, more):
                dve.wait_ge(first_ok, n + 1)
                dve.scalar_tensor_tensor(y0[b][:, :], y1[b][:, :], wt[b][:, 1:2], y0[b][:, :], ALU.mult, ALU.add).then_inc(both_ok, 1)
                dve.wait_ge(both_ok, n + 3)
                dve.tensor_tensor(y1[b][:, :], y0[b][:, :], gt[:, :], ALU.mult).then_inc(gated, 1)
                dve.wait_ge(gated, n + 1)
                dve.wait_ge(x_in[b], i * 16 + 16)
                dve.tensor_tensor(xt[b][:, :], xt[b][:, :], y1[b][:, :], ALU.add).then_inc(x3_ok, 1)
                dve.wait_ge(root_ok, n + 1)
                dve.reciprocal(rs[:, b:b + 1], rt[:, b:b + 1]).then_inc(rstd_ok, 1)
                dve.wait_ge(rstd_ok, n + 1)
                dve.wait_ge(o_out[b], i * 16 + 16)
                dve.scalar_tensor_tensor(ot[b][:, :], xt[b][:, :], rs[:, b:b + 1], gf[:, :], ALU.mult, ALU.mult).then_inc(out_ok, 1)
                if more:
                    columns(n + 2, b)
            for b in range(2):
                columns(b, b)
            with dve.Fori(0, TILES // 2 - 1) as i:
                for b in range(2):
                    tile(i * 2 + b, i, b, True)
            for b in range(2):
                tile(TILES - 2 + b, TILES // 2 - 1, b, False)


class Keep:

    def __init__(self, nc, ctx):
        c = Core(nc, ctx, "keep")
        self.ident = c.sb("ident", [P, P])
        self.ones = c.sb("ones", [P, 512])
        self.quarter = c.sb("quarter", [P, 4, 32])
        self.dirq = c.sb("dirq", [P, 4])
        self.mod = c.sb("mod_rows", [2, 6 * D])
        self.modc = c.sb("mod_cols", [P, 48, 2])
        self.par = c.sb("par_cols", [P, N_PC])
        self.scale1 = c.sb("scale1", [P, 2, KD])
        self.mu_rest = c.sb("mu_rest", [P, MA])
        self.mu_dir = c.sb("mu_dir", [P, 6, MA])
        self.ka_rest = c.sb("ka_rest", [P, PAIRS])
        self.heads = c.sb("head_blocks", [P, P])
        self.restart = c.sb("chunk_restart", [P, 512])
        self.head_of = c.sb("head_of", [P, 2])
        self.logits = c.sb("router_logits", [P, TILES, N_GRP + N_EXP])
        self.weights = c.sb("expert_weights", [P, 2, TILES])
        self.dest = [c.sb(f"slot_of_choice{j}", [P, TILES], I32) for j in range(2)]
        self.block_expert = c.sb("block_expert", [P, N_BLOCKS], I32)
        self.block_slot = c.sb("block_place", [P, N_BLOCKS], I32)
        self.end_block = c.sb("end_block", [P, N_EXP], I32)
        self.slot_token = c.sb("slot_token", [P, N_BLOCKS])


def build(nc, a, out):
    def scratch(name, shape):
        return nc.dram_tensor(name, shape, F32, kind="Internal").ap()
    ZA, UU, GT = scratch("z_shifted", (MA, P, ALL)), scratch("u_gelu", (GROUPS_SG, P, SEQ)), scratch("gates", (2 * KD, P, SEQ))
    YB, OPS, Y = scratch("y_b", (GROUPS_SG, P, SEQ)), scratch("scan_operands", (STEPS, UNITS, P, OPW)), scratch("y_scan", (2, PAIRS, P, ALL))
    YA, X2, H2 = scratch("y_a", (PAIRS, P, SEQ)), scratch("x2", (SEQ, D)), scratch("h2", (SEQ, D))
    ROWTOK, YG = scratch("slot_to_token", (N_BLOCKS * SLOTS_BLOCK, 1)), scratch("expert_rows", (N_BLOCKS * SLOTS_BLOCK, D))
    with ExitStack() as ctx:
        keep = Keep(nc, ctx)
        modulation(nc, a, keep)
        with nc.sbuf_tensor("h_turned", [P, KD, ALL], F32) as hT:
            normalise(nc, a, keep, hT)
            project(nc, a, keep, hT, ZA, UU, GT)
            spatial_gate(nc, a, keep, hT, UU, YB)
        prepare(nc, a, keep, ZA, OPS)
        scan(nc, a, keep, OPS, Y)
        mixer_out(nc, a, keep, ZA, Y, YA)
        with nc.sbuf_tensor("merged", [P, KD, SEQ], F32) as merged:
            merge(nc, a, keep, YA, YB, GT, merged)
            residual(nc, a, keep, merged, X2, H2)
        routing(nc, a, keep, ROWTOK)
        experts(nc, a, keep, H2, YG)
        combine(nc, a, keep, X2, YG, out)


_INS = ("x", "c", "ctx", "c_ctx", "ada_w", "ada_b", "norm1_g", "norm2_g", "w_in", "shift_mu", "rwkv_w0", "rwkv_w_up", "rwkv_a0",
        "rwkv_a_up", "rwkv_g_up", "rwkv_k_k", "rwkv_k_a", "rwkv_r_k", "rwkv_ln_w", "rwkv_ln_b", "w_branch_a", "sg_ln_w", "sg_ln_b",
        "sg_w", "sg_b", "w_branch_b", "w_out", "moe_grp_w", "moe_grp_b", "moe_exp_w", "moe_exp_b", "moe_w_gate", "moe_w_up",
        "moe_w_down", "final_norm_g")


def kernel(**inputs):
    import concourse.bacc as bacc
    from concourse.bass_utils import run_bass_kernel_spmd

    nc = bacc.Bacc("TRN2", target_bir_lowering=False, num_devices=1)
    arrays = {f"in_{n}": np.ascontiguousarray(inputs[n]) for n in _INS}
    arrays["in_scan_masks"] = scan_masks()
    a = {n[3:]: nc.dram_tensor(n, v.shape, mybir.dt.from_np(v.dtype), kind="ExternalInput").ap() for n, v in arrays.items()}
    out = nc.dram_tensor("out", (1, SEQ, D), F32, kind="ExternalOutput").ap()
    build(nc, a, out)
    return run_bass_kernel_spmd(nc, [arrays], core_ids=[0]).results[0]["out"]
```

```python
from contextlib import ExitStack

import numpy as np

import concourse.bass as bass
from concourse import mybir

F32 = mybir.dt.float32
I32 = mybir.dt.int32
U32 = mybir.dt.uint32
ALU = mybir.AluOpType
ACT = mybir.ActivationFunctionType
AX = mybir.AxisListType
ds = bass.ds

P = 128
D = 1024
KD = D // P
SEQ = 2048
CTX = 256
ALL = CTX + SEQ
GRID_W = 64
HEAD = 64
D_RWKV = 512
PAIRS = D_RWKV // P
CHUNK = 64
NCTX = CTX // CHUNK
NLAT = SEQ // CHUNK
STEPS = NCTX + NLAT
UNITS = 2 * PAIRS
OPW = 5 * CHUNK + 1
P_A = 1920
MA = P_A // P
D_SG = 512
GROUPS_SG = D_SG // P
Z_U = P_A
Z_V = P_A + D_SG
Z_G = P_A + 2 * D_SG
Z_COLS = Z_G + 2 * D
N_GRP = 4
PER_GRP = 8
N_EXP = N_GRP * PER_GRP
D_EXP = 512
SLOTS_BLOCK = 128
N_BLOCKS = 2 * SEQ // SLOTS_BLOCK + N_EXP
TILES = SEQ // P
NORM_EPS = 1e-6
GN_EPS = 64e-5
KAPPA = float(np.exp(-0.5))

PC = {}
_at = 0
for _name, _n in (("ada_b", 48), ("norm1_g", 8), ("shift_mu", MA), ("rwkv_w0", 8), ("rwkv_a0", 8), ("rwkv_k_k", 4),
                  ("rwkv_k_a", 4), ("rwkv_r_k", 4), ("rwkv_ln_w", 4), ("rwkv_ln_b", 4)):
    PC[_name] = _at
    _at += _n
N_PC = _at


class Core:

    def __init__(self, nc, ctx, stage):
        self.nc, self.ctx, self.stage, self.sems = nc, ctx, stage, []
        ctx.callback(self.clear)

    def sb(self, name, shape, dt=F32):
        return self.ctx.enter_context(self.nc.sbuf_tensor(f"{self.stage}_{name}", shape, dt))

    def ps(self, name, shape, dt=F32):
        return self.ctx.enter_context(self.nc.psum_tensor(f"{self.stage}_{name}", shape, dt))

    def sem(self, name):
        self.sems.append(self.nc.alloc_semaphore(f"{self.stage}_{name}"))
        return self.sems[-1]

    def clear(self):
        if self.sems:
            self.nc.clear_and_free_semaphores(self.sems)
            self.nc.all_engine_barrier()


def modulation(nc, a, keep, MOD):
    with ExitStack() as ctx:
        c = Core(nc, ctx, "modulation")
        NB = 512
        w = [c.sb(f"ada_tile{b}", [P, KD, NB]) for b in range(2)]
        cc = c.sb("cond", [P, 2, KD])
        cs = c.sb("cond_silu", [P, KD, 2])
        bias, mod = c.sb("ada_bias", [2, 6 * D]), c.sb("mod_rows", [2, 6 * D])
        rows = c.sb("par_rows", [N_PC, P])
        acc = [c.ps(f"ada_acc{b}", [P, NB]) for b in range(2)]
        turn = c.ps("par_turn", [P, NB])
        turn2 = c.ps("mod_turn", [P, NB])
        cond_in, rows_in, w_in_, mod_stored = c.sem("cond_in"), c.sem("rows_in"), [c.sem(f"ada_w_in{b}") for b in range(2)], c.sem("mod_stored")
        eye0, eye, silu_ok, acc_ok, mod_ok = c.sem("eye0"), c.sem("eye"), c.sem("silu_ok"), c.sem("acc_ok"), c.sem("mod_ok")
        turned, par_ok, cols_ok, z_ok = c.sem("turned"), c.sem("par_ok"), c.sem("cols_ok"), c.sem("zeroed")
        bias_in = c.sem("bias_in")
        block = ctx.enter_context(nc.Block())
        adaw = a["ada_w"][0].rearrange("(p k) n -> p k n", k=KD)

        @block.sync
        def _(sp):
            sp.dma_start(cc[:, 0, :], a["c"][0].rearrange("(p k) -> p k", k=KD)).then_inc(cond_in, 16)
            sp.dma_start(cc[:, 1, :], a["c_ctx"].rearrange("(p k) -> p k", k=KD)).then_inc(cond_in, 16)
            with sp.Fori(0, 6) as i:
                for b in range(2):
                    sp.wait_ge(mod_ok, i * 2 + b + 1)
                    sp.dma_start(w[b][:, :, :], adaw[:, :, ds(i * (2 * NB) + b * NB, NB)]).then_inc(w_in_[b], 16)
            sp.wait_ge(mod_ok, 14)
            sp.dma_start(MOD, mod[:, :]).then_inc(mod_stored, 16)
            sp.wait_ge(mod_stored, 16)

        @block.gpsimd
        def _(pool):
            for r in range(2):
                pool.dma_start(bias[r:r + 1, :], a["ada_b"]).then_inc(bias_in, 16)
            flat = {"ada_b": a["ada_b"][0], "norm1_g": a["norm1_g"][0], "shift_mu": a["shift_mu"][0],
                    "rwkv_w0": a["rwkv_w0"][0].rearrange("d c -> (d c)"), "rwkv_a0": a["rwkv_a0"][0].rearrange("d c -> (d c)"),
                    "rwkv_k_k": a["rwkv_k_k"][0], "rwkv_k_a": a["rwkv_k_a"][0],
                    "rwkv_r_k": a["rwkv_r_k"][0].rearrange("h k -> (h k)"),
                    "rwkv_ln_w": a["rwkv_ln_w"][0], "rwkv_ln_b": a["rwkv_ln_b"][0]}
            for name, at in PC.items():
                v = flat[name].rearrange("(r p) -> r p", p=P)
                pool.dma_start(rows[at:at + v.shape[0], :], v).then_inc(rows_in, 16)
            pool.memset(keep.ident[:, :], 0.0).then_inc(eye0, 1)
            pool.memset(keep.heads[:, :], 0.0).then_inc(eye0, 1)
            pool.memset(keep.head_of[:, :], 0.0).then_inc(eye0, 1)
            pool.memset(keep.restart[:, :], 1.0).then_inc(eye0, 1)
            pool.memset(keep.quarter[:, :, :], 0.0).then_inc(eye0, 1)
            pool.memset(keep.ones[:, :], 1.0).then_inc(eye, 1)
            pool.wait_ge(eye0, 5)
            pool.wait_ge(eye, 1)
            for h in range(2):
                pool.wait_ge(eye, h + 1)
                pool.memset(keep.heads[h * HEAD:(h + 1) * HEAD, h * HEAD:(h + 1) * HEAD], 1.0).then_inc(eye, 1)
            for h in range(2):
                pool.wait_ge(eye, h + 3)
                pool.memset(keep.head_of[h * HEAD:(h + 1) * HEAD, h:h + 1], 1.0).then_inc(eye, 1)
            pool.wait_ge(eye, 5)
            pool.memset(keep.restart[:, :].rearrange("p (c t) -> p c t", t=CHUNK)[:, :, 0:1], 0.0).then_inc(eye, 1)
            pool.affine_select(out=keep.ident[:, :], in_=keep.ident[:, :], compare_op=ALU.not_equal, fill=1.0, base=0,
                               pattern=[[-1, P]], channel_multiplier=1).then_inc(eye, 1)
            pool.affine_select(out=keep.quarter[:, :, :], in_=keep.quarter[:, :, :], compare_op=ALU.not_equal, fill=1.0,
                               base=0, pattern=[[-1, 4], [-4, 32]], channel_multiplier=1).then_inc(eye, 1)

        @block.scalar
        def _(act):
            act.wait_ge(cond_in, 32)
            for v in range(2):
                act.activation(cs[:, :, v], cc[:, v, :], ACT.Silu).then_inc(silu_ok, 1)

        @block.tensor
        def _(pe):
            pe.wait_ge(silu_ok, 2)
            with pe.Fori(0, 6) as i:
                for b in range(2):
                    pe.wait_ge(w_in_[b], i * 16 + 16)
                    pe.wait_ge(mod_ok, i * 2 + b + 1)
                    for k in range(KD):
                        mm = pe.matmul(acc[b][0:2, :], cs[:, k, :], w[b][:, k, :], start=k == 0, stop=k == KD - 1)
                    mm.then_inc(acc_ok, 1)
            pe.wait_ge(eye, 8)
            pe.wait_ge(rows_in, 16 * len(PC))
            pe.transpose(turn[:, 0:N_PC], rows[:, :], keep.ident[0:N_PC, 0:N_PC]).then_inc(turned, 1)
            pe.wait_ge(mod_ok, 14)
            for t in range(48):
                mm = pe.transpose(turn2[:, 2 * t:2 * t + 2], mod[:, t * P:(t + 1) * P], keep.ident[0:2, 0:2])
            mm.then_inc(turned, 1)

        @block.vector
        def _(dve):
            dve.sem_inc(mod_ok, 2)
            dve.wait_ge(bias_in, 32)
            with dve.Fori(0, 6) as i:
                for b in range(2):
                    dve.wait_ge(acc_ok, i * 2 + b + 1)
                    dve.tensor_tensor(mod[:, ds(i * (2 * NB) + b * NB, NB)], acc[b][0:2, :],
                                      bias[:, ds(i * (2 * NB) + b * NB, NB)], ALU.add).then_inc(mod_ok, 1)
            dve.wait_ge(eye, 8)
            dve.tensor_reduce(keep.dirq[:, :], keep.quarter[:, :, :], AX.X, ALU.add).then_inc(z_ok, 1)
            dve.wait_ge(turned, 1)
            dve.tensor_copy(keep.par[:, :], turn[:, 0:N_PC]).then_inc(par_ok, 1)
            dve.wait_ge(turned, 2)
            dve.tensor_copy(keep.modc[:, :, :], turn2[:, 0:96].rearrange("p (t v) -> p t v", v=2)).then_inc(par_ok, 1)
            dve.wait_ge(par_ok, 2)
            dve.wait_ge(z_ok, 1)
            for v in range(2):
                dve.scalar_tensor_tensor(keep.scale1[:, v, :], keep.modc[:, KD:2 * KD, v], 1.0,
                                         keep.par[:, PC["norm1_g"]:PC["norm1_g"] + KD], ALU.add, ALU.mult).then_inc(cols_ok, 1)
            mu = keep.par[:, PC["shift_mu"]:PC["shift_mu"] + MA]
            dve.tensor_scalar(keep.mu_rest[:, :], mu, -1.0, 1.0, ALU.mult, ALU.add).then_inc(cols_ok, 1)
            for q in range(4):
                dve.tensor_scalar(keep.mu_dir[:, q, :], mu, keep.dirq[:, q:q + 1], None, ALU.mult).then_inc(cols_ok, 1)
            dve.wait_ge(cols_ok, 7)
            for q in range(2):
                dve.tensor_tensor(keep.mu_dir[:, 4 + q, :], keep.mu_dir[:, q, :], keep.mu_dir[:, q + 2, :],
                                  ALU.add).then_inc(cols_ok, 1)
            ka = keep.par[:, PC["rwkv_k_a"]:PC["rwkv_k_a"] + PAIRS]
            dve.tensor_scalar(keep.ka_rest[:, :], ka, -1.0, 1.0, ALU.mult, ALU.add).then_inc(cols_ok, 1)


def normalise(nc, a, keep, hT):
    with ExitStack() as ctx:
        c = Core(nc, ctx, "normalise")
        xt = [c.sb(f"x_tile{b}", [P, D]) for b in range(2)]
        xn = [c.sb(f"x_normed{b}", [P, D]) for b in range(2)]
        sq = c.sb("x_squared", [P, D])
        ss = c.sb("sum_squares", [P, 2])
        rt = c.sb("root", [P, 2])
        rs = c.sb("rstd", [P, 2])
        eps = c.sb("eps", [P, 1])
        turn = [c.ps(f"x_turn{b}", [P, D]) for b in range(2)]
        x_in = [c.sem(f"x_in{b}") for b in range(2)]
        names = ("x_sq", "x_root", "x_rstd", "x_norm", "x_turned", "h_ok", "eps_ok")
        x_sq, x_root, x_rstd, x_norm, x_turned, h_ok, eps_ok = (c.sem(n) for n in names)
        block = ctx.enter_context(nc.Block())
        TC = CTX // P
        ctx_rows = a["ctx"][0]
        lat_rows = a["x"][0]

        @block.sync
        def _(sp):
            for b in range(TC):
                sp.dma_start(xt[b][:, :], ctx_rows[b * P:(b + 1) * P, :]).then_inc(x_in[b], 16)
            with sp.Fori(0, TILES // 2) as i:
                for b in range(2):
                    sp.wait_ge(x_norm, i * 2 + b + 1)
                    sp.dma_start(xt[b][:, :], lat_rows[ds(i * (2 * P) + b * P, P), :]).then_inc(x_in[b], 16)

        @block.scalar
        def _(act):
            def tile(n, b, loads):
                act.wait_ge(x_in[b], loads * 16)
                act.wait_ge(x_rstd, n + 1)
                act.activation(sq[:, :], xt[b][:, :], ACT.Square, accum_out=ss[:, b:b + 1]).then_inc(x_sq, 1)
                act.wait_ge(x_sq, n + 1)
                act.activation(rt[:, b:b + 1], ss[:, b:b + 1], ACT.Sqrt, bias=eps[:, :], scale=1.0 / D).then_inc(x_root, 1)
                act.wait_ge(x_rstd, n + 3)
                act.wait_ge(x_turned, n + 1)
                act.activation(xn[b][:, :], xt[b][:, :], ACT.Copy, scale=rs[:, b:b + 1]).then_inc(x_norm, 1)
            act.wait_ge(eps_ok, 1)
            for b in range(TC):
                tile(b, b, 1)
            with act.Fori(0, TILES // 2) as i:
                for b in range(2):
                    tile(i * 2 + b + TC, b, i + 2)

        @block.tensor
        def _(pe):
            pe.sem_inc(x_turned, 2)

            def tile(n, b):
                pe.wait_ge(x_norm, n + 1)
                pe.wait_ge(h_ok, n + 1)
                for k in range(KD):
                    mm = pe.transpose(turn[b][:, k * P:(k + 1) * P], xn[b][:, k * P:(k + 1) * P], keep.ident[:, :])
                mm.then_inc(x_turned, 1)
            for b in range(TC):
                tile(b, b)
            with pe.Fori(0, TILES // 2) as i:
                for b in range(2):
                    tile(i * 2 + b + TC, b)

        @block.vector
        def _(dve):
            dve.memset(eps[:, :], NORM_EPS).then_inc(eps_ok, 1)
            dve.sem_inc(x_rstd, 2)
            dve.sem_inc(h_ok, 2)

            def tile(n, b, v, col):
                dve.wait_ge(x_root, n + 1)
                dve.reciprocal(rs[:, b:b + 1], rt[:, b:b + 1]).then_inc(x_rstd, 1)
                dve.wait_ge(x_turned, n + 3)
                for k in range(KD):
                    ins = dve.tensor_scalar(hT[:, k, ds(col, P)], turn[b][:, k * P:(k + 1) * P], keep.scale1[:, v, k:k + 1],
                                            keep.modc[:, k, v:v + 1], ALU.mult, ALU.add)
                ins.then_inc(h_ok, 1)
            for b in range(TC):
                tile(b, b, 1, b * P)
            with dve.Fori(0, TILES // 2) as i:
                for b in range(2):
                    tile(i * 2 + b + TC, b, 0, i * (2 * P) + (b * P + CTX))


def project(nc, a, keep, hT, ZA, UU, GT):
    with ExitStack() as ctx:
        c = Core(nc, ctx, "project")
        NW = 3
        w = [c.sb(f"w_tile{b}", [P, KD, P]) for b in range(NW)]
        zr = [c.sb(f"z_raw{b}", [P, ALL]) for b in range(2)]
        zm = [c.sb(f"z_mixed{b}", [P, ALL]) for b in range(2)]
        NG = 5
        acc = [c.ps(f"z_acc{g}", [P, 512]) for g in range(NG)]
        w_ready = [c.sem(f"w_ready{b}") for b in range(NW)]
        names = ("z_done", "z_out", "mixed", "stored", "shift", "z_free")
        z_done, z_out, mixed, stored, shift, z_free = (c.sem(n) for n in names)
        block = ctx.enter_context(nc.Block())
        GC = [(0, CTX)] + [(CTX + 512 * g, 512) for g in range(4)]
        win = a["w_in"][0].rearrange("(k p) n -> p k n", p=P)
        REST = (D_SG + 2 * D) // P

        @block.sync
        def _(sp):
            def load(b, col):
                sp.dma_start(w[b][:, :, :], win[:, :, ds(col, P)]).then_inc(w_ready[b], 16)
            for b in range(NW):
                load(b, b * P)
            with sp.Fori(0, MA // NW - 1) as i:
                for b in range(NW):
                    sp.wait_ge(z_done, i * (NW * NG) + (b + 1) * NG)
                    load(b, i * (NW * P) + (NW + b) * P)
            tiles = 0
            for col, count in ((Z_U, D_SG // P), (Z_G, 2 * D // P)):
                with sp.Fori(0, count // 2) as i:
                    for b in range(2):
                        sp.wait_ge(z_done, i * 8 + (MA * NG + (tiles + b - 1) * 4))
                        load(b, i * (2 * P) + (col + b * P))
                tiles += count

        @block.tensor
        def _(pe):
            def tile(loads, b, g0, done):
                pe.wait_ge(w_ready[b], loads * 16)
                for g in range(g0, NG):
                    pe.wait_ge(z_out, done + (g - g0 + 1))
                    col, nt = GC[g]
                    for k in range(KD):
                        mm = pe.matmul(acc[g][:, 0:nt], w[b][:, k, :], hT[:, k, col:col + nt], start=k == 0, stop=k == KD - 1)
                    mm.then_inc(z_done, 1)
            with pe.Fori(0, MA // 3) as i:
                for b in range(3):
                    tile(i + 1, b, 0, i * 15 + b * 5)
            with pe.Fori(0, REST // 2) as i:
                for b in range(2):
                    tile(i + (MA // 3 + 1), b, 1, i * 8 + (MA * 5 + b * 4 + 1))

        @block.scalar
        def _(act):
            act.sem_inc(z_out, NG)

            def tile(n, b, g0, done, func):
                if g0 == 0:
                    act.wait_ge(mixed, n + 1)
                else:
                    act.wait_ge(z_free, n + 1)
                for g in range(g0, NG):
                    act.wait_ge(z_done, done + (g - g0 + 1))
                    col, nt = GC[g]
                    act.activation(zr[b][:, col:col + nt], acc[g][:, 0:nt], func).then_inc(z_out, 1)
            with act.Fori(0, (MA - 1) // 2) as i:
                for b in range(2):
                    tile(i * 2 + b, b, 0, i * 10 + b * 5, ACT.Copy)
            tile(MA - 1, 0, 0, (MA - 1) * 5, ACT.Copy)
            act.wait_ge(mixed, MA + 2)
            base = MA * 5
            with act.Fori(0, D_SG // P // 2) as i:
                for b in range(2):
                    tile(i * 2 + (MA + b), b, 1, i * 8 + (base + b * 4), ACT.Gelu_apprx_tanh)
            base += 4 * 4
            with act.Fori(0, 2 * D // P // 2) as i:
                for b in range(2):
                    tile(i * 2 + (MA + 4 + b), b, 1, i * 8 + (base + b * 4), ACT.Sigmoid)

        @block.vector
        def _(dve):
            dve.sem_inc(mixed, 2)

            def tile(n, b):
                z, m = zr[b], zm[b]
                mu = lambda q: keep.mu_dir[:, q, ds(n, 1)]
                dve.wait_ge(z_out, n * 5 + (NG + 5))
                dve.wait_ge(z_free, n + 1)
                dve.tensor_scalar(m[:, :], z[:, :], keep.mu_rest[:, ds(n, 1)], None, ALU.mult).then_inc(shift, 1)
                steps = []
                for q, (to, frm) in enumerate(((slice(1, GRID_W), slice(0, GRID_W - 1)), (slice(0, GRID_W - 1), slice(1, GRID_W)))):
                    mg = m[:, CTX:ALL].rearrange("p (r w) -> p r w", w=GRID_W)
                    zg = z[:, CTX:ALL].rearrange("p (r w) -> p r w", w=GRID_W)
                    steps.append((mg[:, :, to], zg[:, :, frm], q))
                steps.append((m[:, CTX + GRID_W:ALL], z[:, CTX:ALL - GRID_W], 2))
                steps.append((m[:, CTX:ALL - GRID_W], z[:, CTX + GRID_W:ALL], 3))
                steps.append((m[:, 1:CTX], z[:, 0:CTX - 1], 4))
                steps.append((m[:, 0:CTX - 1], z[:, 1:CTX], 5))
                for j, (to, frm, q) in enumerate(steps):
                    dve.wait_ge(shift, n * 6 + (j + 1))
                    ins = dve.scalar_tensor_tensor(to, frm, mu(q), to, ALU.mult, ALU.add)
                    ins.then_inc(mixed if j == 5 else shift, 1)
            with dve.Fori(0, (MA - 1) // 2) as i:
                for b in range(2):
                    tile(i * 2 + b, b)
            tile(MA - 1, 0)

        @block.gpsimd
        def _(pool):
            pool.sem_inc(z_free, 2)

            def store(n, dst, src):
                pool.dma_start(dst, src).then_inc(stored, 16)
                pool.wait_ge(stored, n * 16 + 16)
                pool.sem_inc(z_free, 1)
            with pool.Fori(0, (MA - 1) // 2) as i:
                for b in range(2):
                    pool.wait_ge(mixed, i * 2 + (b + 3))
                    store(i * 2 + b, ZA[ds(i * 2 + b, 1), :, :].rearrange("m p t -> (m p) t"), zm[b][:, :])
            pool.wait_ge(mixed, MA + 2)
            store(MA - 1, ZA[MA - 1], zm[0][:, :])
            base, tiles = NG + MA * 5, MA
            for dst, count in ((UU, D_SG // P), (GT, 2 * D // P)):
                with pool.Fori(0, count // 2) as i:
                    for b in range(2):
                        pool.wait_ge(z_out, i * 8 + (base + b * 4 + 4))
                        store(i * 2 + (tiles + b), dst[ds(i * 2 + b, 1), :, :].rearrange("m p t -> (m p) t"), zr[b][:, CTX:ALL])
                base, tiles = base + 4 * count, tiles + count


def spatial_gate(nc, a, keep, hT, UU, YB):
    with ExitStack() as ctx:
        c = Core(nc, ctx, "spatial_gate")
        wv = c.sb("w_v", [P, KD, D_SG])
        hs = [c.sb(f"h_tile{b}", [P, KD, P]) for b in range(2)]
        v = [c.sb(f"v_gelu{b}", [P, D_SG]) for b in range(2)]
        vn = [c.sb(f"v_normed{b}", [P, D_SG]) for b in range(2)]
        ut = [c.sb(f"u_tile{b}", [P, GROUPS_SG, P]) for b in range(2)]
        yb = [c.sb(f"yb_tile{b}", [P, GROUPS_SG, P]) for b in range(2)]
        lnw, lnb = c.sb("sg_ln_w_all", [P, D_SG]), c.sb("sg_ln_b_all", [P, D_SG])
        sgb = c.sb("sg_b_all", [P, GROUPS_SG * P])
        sgw, sgwT = c.sb("sg_w_rows", [P, GROUPS_SG, P]), c.sb("sg_w_turned", [P, GROUPS_SG, P])
        st, mv, rt, rs = c.sb("v_stats", [P, 2, 6]), c.sb("v_meanvar", [P, 2, 2]), c.sb("v_root", [P, 2]), c.sb("v_rstd", [P, 2])
        eps = c.sb("ln_eps", [P, 1])
        acc = [c.ps(f"v_acc{b}", [P, D_SG]) for b in range(2)]
        mix = [c.ps(f"mix_acc{b}", [P, GROUPS_SG * P]) for b in range(2)]
        turn = c.ps("sg_turn", [P, GROUPS_SG * P])
        u_in = [c.sem(f"u_in{b}") for b in range(2)]
        aggr_go = c.sem("aggr_go")
        yb_stored = [c.sem(f"yb_stored{b}") for b in range(2)]
        names = ("const_in", "h_copied", "v_acc_ok", "v_ok", "stats_ok", "mv_ok", "root_ok", "rstd_ok", "centred", "scaled", "vn_ok",
                 "mix_ok", "biased", "yb_ok", "sg_turned", "sg_ready", "eps_ok")
        (const_in, h_copied, v_acc_ok, v_ok, stats_ok, mv_ok, root_ok, rstd_ok, centred, scaled, vn_ok, mix_ok, biased, yb_ok,
         sg_turned, sg_ready, eps_ok) = (c.sem(n) for n in names)
        block = ctx.enter_context(nc.Block())
        win = a["w_in"][0].rearrange("(k p) n -> p k n", p=P)

        @block.sync
        def _(sp):
            sp.dma_start(wv[:, :, :], win[:, :, Z_V:Z_V + D_SG]).then_inc(const_in, 16)
            sp.dma_start(lnw[:, :], a["sg_ln_w"].to_broadcast([P, D_SG])).then_inc(const_in, 16)
            sp.dma_start(lnb[:, :], a["sg_ln_b"].to_broadcast([P, D_SG])).then_inc(const_in, 16)
            sp.dma_start(sgb[:, :], a["sg_b"].rearrange("o g p -> o (g p)").to_broadcast([P, GROUPS_SG * P])).then_inc(const_in, 16)
            sp.dma_start(sgw[:, :, :], a["sg_w"][0].rearrange("g p q -> p g q")).then_inc(const_in, 16)
            for b in range(2):
                sp.sem_inc(yb_stored[b], 16)
                sp.dma_start(ut[b][:, :, :], UU[:, :, b * P:(b + 1) * P].rearrange("m p t -> p m t")).then_inc(u_in[b], 16)
            def store(n, b, col):
                sp.wait_ge(yb_ok, n + 1)
                sp.dma_start(YB[:, :, ds(col, P)].rearrange("m p t -> p m t"), yb[b][:, :, :]).then_inc(yb_stored[b], 16)
            with sp.Fori(0, TILES // 2 - 1) as i:
                for b in range(2):
                    store(i * 2 + b, b, i * (2 * P) + b * P)
                    sp.dma_start(ut[b][:, :, :],
                                 UU[:, :, ds(i * (2 * P) + (2 + b) * P, P)].rearrange("m p t -> p m t")).then_inc(u_in[b], 16)
            for b in range(2):
                store(TILES - 2 + b, b, (TILES - 2 + b) * P)
            for b in range(2):
                sp.wait_ge(yb_stored[b], 16 * (TILES // 2 + 1))

        @block.gpsimd
        def _(pool):
            with pool.Fori(0, TILES // 2) as i:
                for b in range(2):
                    pool.wait_ge(v_acc_ok, i * 2 + b + 1)
                    pool.tensor_copy(hs[b][:, :, :], hT[:, :, ds(i * (2 * P) + (CTX + b * P), P)]).then_inc(h_copied, 1)

        @block.tensor
        def _(pe):
            pe.sem_inc(v_acc_ok, 2)
            pe.wait_ge(const_in, 80)
            for g in range(GROUPS_SG):
                mm = pe.transpose(turn[:, g * P:(g + 1) * P], sgw[:, g, :], keep.ident[:, :])
            mm.then_inc(sg_turned, 1)

            def values(n, b):
                pe.wait_ge(h_copied, n + 1)
                pe.wait_ge(v_ok, n + 1)
                for k in range(KD):
                    mm = pe.matmul(acc[b][:, :], hs[b][:, k, :], wv[:, k, :], start=k == 0, stop=k == KD - 1)
                mm.then_inc(v_acc_ok, 1)

            def mixing(n, b):
                pe.wait_ge(vn_ok, n + 1)
                pe.wait_ge(biased, n + 1)
                for g in range(GROUPS_SG):
                    mm = pe.matmul(mix[b][:, g * P:(g + 1) * P], vn[b][:, g * P:(g + 1) * P], sgwT[:, g, :], start=True, stop=True)
                mm.then_inc(mix_ok, 1)
            pe.wait_ge(sg_ready, 1)
            values(0, 0)
            with pe.Fori(0, TILES // 2 - 1) as i:
                values(i * 2 + 1, 1)
                mixing(i * 2, 0)
                values(i * 2 + 2, 0)
                mixing(i * 2 + 1, 1)
            values(TILES - 1, 1)
            mixing(TILES - 2, 0)
            mixing(TILES - 1, 1)

        @block.scalar
        def _(act):
            act.sem_inc(v_ok, 2)
            act.wait_ge(eps_ok, 1)
            with act.Fori(0, TILES // 2) as i:
                for b in range(2):
                    n = i * 2 + b
                    act.wait_ge(v_acc_ok, n + 3)
                    act.wait_ge(centred, n + 1)
                    act.activation(v[b][:, :], acc[b][:, :], ACT.Gelu_apprx_tanh).then_inc(v_ok, 1)
                    act.wait_ge(mv_ok, n + 1)
                    act.activation(rt[:, b:b + 1], mv[:, b, 1:2], ACT.Sqrt, bias=eps[:, :]).then_inc(root_ok, 1)

        @block.vector
        def _(dve):
            dve.memset(eps[:, :], 1e-5).then_inc(eps_ok, 1)
            dve.sem_inc(centred, 2)
            dve.sem_inc(biased, 2)
            dve.wait_ge(sg_turned, 1)
            dve.tensor_copy(sgwT[:, :, :].rearrange("p g q -> p (g q)"), turn[:, :]).then_inc(sg_ready, 1)
            dve.wait_ge(const_in, 80)
            with dve.Fori(0, TILES // 2) as i:
                for b in range(2):
                    n = i * 2 + b
                    dve.wait_ge(v_ok, n + 3)
                    dve.bn_stats(st[:, b, :], v[b][:, :]).then_inc(stats_ok, 1)
                    dve.wait_ge(stats_ok, n + 1)
                    dve.sem_inc(aggr_go, 1)
                    dve.bn_aggr(mv[:, b, :], st[:, b, :]).then_inc(mv_ok, 1)
                    dve.wait_ge(root_ok, n + 1)
                    dve.reciprocal(rs[:, b:b + 1], rt[:, b:b + 1]).then_inc(rstd_ok, 1)
                    dve.wait_ge(rstd_ok, n + 1)
                    dve.tensor_scalar(vn[b][:, :], v[b][:, :], mv[:, b, 0:1], rs[:, b:b + 1], ALU.subtract, ALU.mult).then_inc(centred, 1)
                    dve.wait_ge(centred, n + 3)
                    dve.tensor_tensor(vn[b][:, :], vn[b][:, :], lnw[:, :], ALU.mult).then_inc(scaled, 1)
                    dve.wait_ge(scaled, n + 1)
                    dve.tensor_tensor(vn[b][:, :], vn[b][:, :], lnb[:, :], ALU.add).then_inc(vn_ok, 1)
                    dve.wait_ge(mix_ok, n + 1)
                    dve.wait_ge(yb_stored[b], i * 16 + 16)
                    yf = yb[b][:, :, :].rearrange("p g t -> p (g t)")
                    dve.tensor_tensor(yf, mix[b][:, :], sgb[:, :], ALU.add).then_inc(biased, 1)
                    dve.wait_ge(biased, n + 3)
                    dve.wait_ge(u_in[b], i * 16 + 16)
                    dve.tensor_tensor(yf, yf, ut[b][:, :, :].rearrange("p g t -> p (g t)"), ALU.mult).then_inc(yb_ok, 1)


def prepare(nc, a, keep, ZA, OPS):
    with ExitStack() as ctx:
        c = Core(nc, ctx, "prepare")
        NT = 512

        def two(name, shape=(P, NT)):
            return [c.sb(f"{name}{b}", list(shape)) for b in range(2)]
        r, k, v, wd, ad, wu, au = two("r"), two("k"), two("v"), two("wd"), two("ad"), two("w_up", (P, P)), two("a_up", (P, P))
        th, kk, sq, nrm = two("wd_tanh"), two("kk"), two("kk_sq"), two("kk_norm")
        four = (P, 2, NT)
        sg, av, lc, y, q = two("decay_sig", four), two("a_gate", four), two("log_sum", four), two("log_mid", four), two("log_prev", four)
        pp = two("pair_par", (P, 8))
        half = two("half", (P, 2, NT // CHUNK))
        ea, er, eb, kd, kka = two("exp_a", four), two("exp_r", four), two("exp_b", four), two("k_dir", four), two("kk_a", four)
        ops = [[c.sb(f"ops{b}{d}", [P, NT // CHUNK, OPW]) for d in range(2)] for b in range(2)]
        argw = [c.ps(f"arg_w{d}", [P, NT]) for d in range(2)]
        arga = [c.ps(f"arg_a{d}", [P, NT]) for d in range(2)]
        ssum = c.ps("kk_sum", [P, NT])
        z_in = [c.sem(f"z_in{b}") for b in range(2)]
        stored = [c.sem(f"ops_stored{b}") for b in range(2)]
        names = ("tanh_ok", "args_ok", "sig_ok", "sums_ok", "kk1_ok", "sq_ok", "norm_ok", "root_ok", "scan_ok", "half_ok", "mid_ok",
                 "prev_ok", "exp_ok", "act_end", "floor_ok", "inv_ok", "kk_ok", "kdir1_ok", "kdir2_ok", "pool_end", "slot_ok", "dve_end",
                 "pe_end", "ops_free", "par_pair_ok")
        (tanh_ok, args_ok, sig_ok, sums_ok, kk1_ok, sq_ok, norm_ok, root_ok, scan_ok, half_ok, mid_ok, prev_ok, exp_ok, act_end,
         floor_ok, inv_ok, kk_ok, kdir1_ok, kdir2_ok, pool_end, slot_ok, dve_end, pe_end,
         ops_free, par_pair_ok) = (c.sem(n) for n in names)
        block = ctx.enter_context(nc.Block())

        def instances(eng, body):
            with eng.Fori(0, PAIRS // 2) as i:
                for b in range(2):
                    p = i * 2 + b
                    body(p, i, b, p, 0, CTX, 0)
            with eng.Fori(0, PAIRS) as p:
                with eng.Fori(0, 2) as s:
                    for b in range(2):
                        seg = s * 2 + b
                        body(p * 4 + seg + 4, p * 2 + s + 2, b, p, seg * NT + CTX, NT, seg * (NT // CHUNK) + NCTX)

        @block.sync
        def _(sp):
            def body(n, m, b, p, col, nt, chunk):
                for e in (dve_end, act_end, pool_end, pe_end):
                    sp.wait_ge(e, n + 1)
                for dst, tile in ((r, p), (k, p + PAIRS), (v, p + 2 * PAIRS), (wd, 3 * PAIRS), (ad, 3 * PAIRS + 1)):
                    sp.dma_start(dst[b][:, 0:nt], ZA[ds(tile, 1), :, ds(col, nt)].rearrange("m p t -> (m p) t")).then_inc(z_in[b], 16)
                sp.dma_start(wu[b][:, :], a["rwkv_w_up"][0].rearrange("d r c -> (d r) c")[:, ds(p * P, P)]).then_inc(z_in[b], 16)
                sp.dma_start(au[b][:, :], a["rwkv_a_up"][0].rearrange("d r c -> (d r) c")[:, ds(p * P, P)]).then_inc(z_in[b], 16)
            instances(sp, body)

        @block.tensor
        def _(pe):
            pe.sem_inc(pe_end, 2)

            def body(n, m, b, p, col, nt, chunk):
                pe.wait_ge(tanh_ok, n + 1)
                pe.wait_ge(sig_ok, n * 4 + 4)
                for d in range(2):
                    h = slice(HEAD * d, HEAD * d + HEAD)
                    pe.matmul(argw[d][:, 0:nt], wu[b][h, :], th[b][h, 0:nt], start=True, stop=True)
                    mm = pe.matmul(arga[d][:, 0:nt], au[b][h, :], ad[b][h, 0:nt], start=True, stop=True)
                mm.then_inc(args_ok, 1)
                pe.wait_ge(sq_ok, n + 1)
                pe.wait_ge(root_ok, n + 1)
                pe.matmul(ssum[:, 0:nt], keep.heads[:, :], sq[b][:, 0:nt], start=True, stop=True).then_inc(pe_end, 1)
            instances(pe, body)

        @block.scalar
        def _(act):
            act.sem_inc(sig_ok, 4)
            act.sem_inc(root_ok, 1)
            act.sem_inc(act_end, 2)

            def body(n, m, b, p, col, nt, chunk):
                act.wait_ge(z_in[b], m * 112 + 112)
                act.wait_ge(pe_end, n + 1)
                act.activation(th[b][:, 0:nt], wd[b][:, 0:nt], ACT.Tanh).then_inc(tanh_ok, 1)
                act.wait_ge(args_ok, n + 1)
                act.wait_ge(par_pair_ok, n * 2 + 2)
                act.wait_ge(dve_end, n + 1)
                act.wait_ge(pool_end, n + 1)
                for d in range(2):
                    act.activation(sg[b][:, d, 0:nt], argw[d][:, 0:nt], ACT.Sigmoid,
                                   bias=pp[b][:, d:d + 1]).then_inc(sig_ok, 1)
                    act.activation(av[b][:, d, 0:nt], arga[d][:, 0:nt], ACT.Sigmoid,
                                   bias=pp[b][:, 2 + d:3 + d]).then_inc(sig_ok, 1)
                act.wait_ge(sig_ok, n * 4 + 8)
                for d in range(2):
                    act.activation(kd[b][:, d, 0:nt], av[b][:, d, 0:nt], ACT.Identity, scale=pp[b][:, 5:6],
                                   bias=pp[b][:, 6:7]).then_inc(kdir1_ok, 1)
                act.wait_ge(kk1_ok, n + 1)
                act.activation(sq[b][:, 0:nt], kk[b][:, 0:nt], ACT.Square).then_inc(sq_ok, 1)
                act.wait_ge(pe_end, n + 3)
                act.activation(nrm[b][:, 0:nt], ssum[:, 0:nt], ACT.Sqrt).then_inc(root_ok, 1)
                act.wait_ge(ops_free, n + 1)
                for d in range(2):
                    act.wait_ge(prev_ok, n * 2 + (d + 1))
                    y_, q_ = y[b][:, d, 0:nt], q[b][:, d, 0:nt]
                    table = ((er, y_, -1), (ea, q_, -1), (eb, y_, 1)) if d == 0 else ((ea, y_, 1), (er, q_, 1), (eb, q_, -1))
                    for dst, src, sign in table:
                        act.activation(dst[b][:, d, 0:nt], src, ACT.Exp, scale=sign * KAPPA).then_inc(exp_ok, 1)
                    nch = nt // CHUNK
                    act.activation(ops[b][d][:, 0:nch, 5 * CHUNK], half[b][:, d, 0:nch], ACT.Exp, scale=-KAPPA).then_inc(exp_ok, 1)
                for d in range(2):
                    act.activation(ops[b][d][:, 0:nt // CHUNK, 4 * CHUNK:5 * CHUNK],
                                   v[b][:, 0:nt].rearrange("p (c t) -> p c t", t=CHUNK), ACT.Copy).then_inc(act_end if d else exp_ok, 1)
            instances(act, body)

        @block.gpsimd
        def _(pool):
            pool.sem_inc(pool_end, 2)
            pool.sem_inc(ops_free, 2)

            def body(n, m, b, p, col, nt, chunk):
                pool.wait_ge(sig_ok, n * 4 + 8)
                pool.wait_ge(z_in[b], m * 112 + 112)
                pool.wait_ge(dve_end, n + 1)
                for d in range(2):
                    pool.wait_ge(kdir1_ok, n * 2 + (d + 1))
                    pool.tensor_tensor(kd[b][:, d, 0:nt], kd[b][:, d, 0:nt], k[b][:, 0:nt], ALU.mult).then_inc(kdir2_ok, 1)
                pool.wait_ge(kk_ok, n + 1)
                for d in range(2):
                    pool.tensor_tensor(kka[b][:, d, 0:nt], kk[b][:, 0:nt], av[b][:, d, 0:nt],
                                       ALU.mult).then_inc(pool_end if d else kdir2_ok, 1)
                nch = nt // CHUNK
                pool.wait_ge(dve_end, n + 3)
                pool.wait_ge(act_end, n + 3)
                for d in range(2):
                    pool.dma_start(OPS[ds(chunk, nch), ds(p + PAIRS * d, 1), :, :].rearrange("s u p w -> p (s u) w"),
                                   ops[b][d][:, 0:nch, :]).then_inc(stored[b], 16)
                pool.wait_ge(stored[b], m * 32 + 32)
                pool.sem_inc(ops_free, 1)
            instances(pool, body)

        @block.vector
        def _(dve):
            dve.sem_inc(dve_end, 2)

            def body(n, m, b, p, col, nt, chunk):
                nch = nt // CHUNK
                by_chunk = lambda x: x.rearrange("p (c t) -> p c t", t=CHUNK)
                dve.wait_ge(z_in[b], m * 112 + 112)
                dve.wait_ge(pool_end, n + 1)
                dve.wait_ge(act_end, n + 1)
                dve.tensor_scalar(pp[b][:, 0:6], keep.par[:, PC["rwkv_w0"]:PC["rwkv_w0"] + 6 * PAIRS].rearrange(
                    "p (v q) -> p v q", q=PAIRS)[:, :, ds(p, 1)].rearrange("p v q -> p (v q)"), 1.0, None, ALU.mult).then_inc(par_pair_ok, 1)
                dve.tensor_scalar(pp[b][:, 6:7], keep.ka_rest[:, ds(p, 1)], 1.0, None, ALU.mult).then_inc(par_pair_ok, 1)
                dve.wait_ge(par_pair_ok, n * 2 + 2)
                dve.tensor_scalar(kk[b][:, 0:nt], k[b][:, 0:nt], pp[b][:, 4:5], None,
                                  ALU.mult).then_inc(kk1_ok, 1)
                dve.wait_ge(sig_ok, n * 4 + 8)
                for d in range(2):
                    dve.tensor_tensor_scan(lc[b][:, d, 0:nt], keep.restart[:, 0:nt], sg[b][:, d, 0:nt], 0.0, ALU.mult,
                                           ALU.add).then_inc(scan_ok, 1)
                for d in range(2):
                    dve.wait_ge(scan_ok, n * 2 + (d + 1))
                    dve.tensor_scalar(half[b][:, d, 0:nch], by_chunk(lc[b][:, d, 0:nt])[:, :, CHUNK - 1], 0.5, None,
                                      ALU.mult).then_inc(half_ok, 1)
                for d in range(2):
                    dve.wait_ge(half_ok, n * 2 + (d + 1))
                    dve.tensor_tensor(by_chunk(y[b][:, d, 0:nt]), by_chunk(lc[b][:, d, 0:nt]),
                                      half[b][:, d, 0:nch, None].to_broadcast([P, nch, CHUNK]), ALU.subtract).then_inc(mid_ok, 1)
                for d in range(2):
                    dve.wait_ge(mid_ok, n * 2 + (d + 1))
                    dve.tensor_tensor(q[b][:, d, 0:nt], y[b][:, d, 0:nt], sg[b][:, d, 0:nt], ALU.subtract).then_inc(prev_ok, 1)
                dve.wait_ge(root_ok, n + 2)
                dve.tensor_scalar(nrm[b][:, 0:nt], nrm[b][:, 0:nt], 1e-12, None, ALU.max).then_inc(floor_ok, 1)
                dve.wait_ge(floor_ok, n + 1)
                dve.reciprocal(nrm[b][:, 0:nt], nrm[b][:, 0:nt]).then_inc(inv_ok, 1)
                dve.wait_ge(inv_ok, n + 1)
                dve.tensor_tensor(kk[b][:, 0:nt], kk[b][:, 0:nt], nrm[b][:, 0:nt], ALU.mult).then_inc(kk_ok, 1)
                dve.wait_ge(kk_ok, n + 1)
                dve.wait_ge(ops_free, n + 1)
                for d in range(2):
                    dve.wait_ge(exp_ok, n * 9 + 4 * (d + 1))
                    if d == 0:
                        dve.wait_ge(pool_end, n + 3)
                    for s, (x, e) in enumerate(((kk[b][:, 0:nt], ea), (r[b][:, 0:nt], er), (kka[b][:, d, 0:nt], eb),
                                                (kd[b][:, d, 0:nt], eb))):
                        dve.tensor_tensor(ops[b][d][:, 0:nch, s * CHUNK:(s + 1) * CHUNK], by_chunk(x),
                                          by_chunk(e[b][:, d, 0:nt]), ALU.mult).then_inc(dve_end if (d, s) == (1, 3) else slot_ok, 1)
            instances(dve, body)


LEVELS = 5
N_MASKS = 4 + 1 + LEVELS


def scan_masks():
    s, t = np.arange(P)[:, None], np.arange(P)[None, :]
    same = s // CHUNK == t // CHUNK
    out = np.zeros((P, 2, N_MASKS, P), np.float32)
    for d in range(2):
        a, b = (s, t) if d == 0 else (t, s)
        for j in range(4):
            out[:, d, j] = same & ((a < b) if j % 2 == 0 else (a <= b))
        for lv in range(LEVELS + 1):
            w = 1 << lv
            out[:, d, 4 + lv] = (a // (2 * w) == b // (2 * w)) & (a // w < b // w)
        out[:, d, 4] *= -1
    return out


def scan(nc, a, keep, OPS, Y):
    with ExitStack() as ctx:
        c = Core(nc, ctx, "scan")
        U4 = PAIRS
        BD = U4 + 1
        masks = c.sb("masks", [P, 2, N_MASKS, P])

        def g2(name, shape):
            return [c.sb(f"{name}{g}", shape) for g in range(2)]

        def g2b(name, shape):
            return [[c.sb(f"{name}{g}{b}", shape) for b in range(2)] for g in range(2)]
        st, bd, yo, dh = g2b("staged", [P, U4, OPW]), g2b("diag", [P, U4, 5, P]), g2b("y_out", [P, U4, CHUNK]), g2b("decay", [P, U4])
        gm, tm, lv = g2("products", [P, U4, 4, P]), g2("by_token", [P, U4, 3, P]), g2("level_parts", [P, U4, LEVELS, P])
        T, TT, Z = g2("inv", [P, U4, P]), g2("inv_turned", [P, U4, P]), g2("level_prod", [P, U4, P])
        ru, uu, sp_, sn = g2("u_rhs", [P, U4, P]), g2("u", [P, U4, P]), g2b("state_mid", [P, U4, P]), g2("state", [P, U4, P])
        d2 = g2("decay_two", [P, U4])
        bank = [[c.ps(f"bank{g}{j}", [P, 512]) for j in range(4)] for g in range(2)]

        def s2(name):
            return [c.sem(f"{name}{g}") for g in range(2)]
        ops_in = [[c.sem(f"ops_in{g}{b}") for b in range(2)] for g in range(2)]
        y_stored = [[c.sem(f"y_stored{g}{b}") for b in range(2)] for g in range(2)]
        masks_in, zeroed = c.sem("masks_in"), c.sem("diag_zeroed")
        bd_ok, decay_ok, mid_ok, lv_ok = s2("diag_ok"), s2("decay_ok"), s2("state_mid_ok"), s2("levels_ok")
        tr_mm, g_mm, ru_mm, t0_mm, z_mm, p_mm = s2("turned"), s2("products_mm"), s2("u_rhs_mm"), s2("inv0_mm"), s2("z_mm"), s2("p_mm")
        u_mm, s_mm, y_mm = s2("u_mm"), s2("state_mm"), s2("y_mm")
        tm_ok, ru_ok, z_ok, u_ok, y_ok = s2("by_token_ok"), s2("u_rhs_ok"), s2("z_ok"), s2("u_ok"), s2("y_ok")
        gm_ok, pair_ok, tt0_ok, t0_ok, t_ok, tt_ok, sn_ok = (s2("products_ok"), s2("pairs_ok"), s2("inv0_turned_ok"), s2("inv0_ok"),
                                                             s2("inv_ok"), s2("inv_turned_ok"), s2("state_ok"))
        block = ctx.enter_context(nc.Block())

        def steps(eng, body):
            with eng.Fori(0, NCTX // 2) as i:
                for b in range(2):
                    body(i * 2 + b, i, b, (i * 2 + b, i * (-2) + (NCTX - 1 - b)))
            with eng.Fori(0, NLAT // 2) as i:
                for b in range(2):
                    body(i * 2 + (NCTX + b), i + NCTX // 2, b, (i * 2 + (NCTX + b), i * (-2) + (STEPS - 1 - b)))

        @block.sync
        def _(sp):
            sp.dma_start(masks[:, :, :, :], a["scan_masks"]).then_inc(masks_in, 16)

            def body(n, m, b, chunk):
                for g in range(2):
                    sp.wait_ge(bd_ok[g], n * BD + BD)
                    sp.dma_start(st[g][b][:, :, :],
                                 OPS[ds(chunk[g], 1), U4 * g:U4 * g + U4, :, :].rearrange("c u p w -> p (c u) w")).then_inc(ops_in[g][b], 16)
            steps(sp, body)

        @block.gpsimd
        def _(pool):
            for g in range(2):
                pool.sem_inc(bd_ok[g], 2 * BD)
                pool.memset(sn[g][:, :, :], 0.0).then_inc(zeroed, 1)
                pool.memset(dh[g][1][:, :], 1.0).then_inc(zeroed, 1)
            pool.wait_ge(zeroed, 4)
            pool.wait_ge(masks_in, 16)

            def body(n, m, b, chunk):
                for g in range(2):
                    pool.wait_ge(ops_in[g][b], m * 16 + 16)
                    pool.wait_ge(y_mm[g], n + 1)
                    for u in range(U4):
                        pool.tensor_tensor(bd[g][b][:, u, :, :].rearrange("p o (h t) -> p o h t", h=2),
                                           st[g][b][:, u, 0:5 * CHUNK].rearrange("p (o x t) -> p o x t", o=5, x=1).to_broadcast([P, 5, 2, CHUNK]),
                                           keep.head_of[:, None, :, None].to_broadcast([P, 5, 2, CHUNK]), ALU.mult).then_inc(bd_ok[g], 1)
                    pool.tensor_tensor(dh[g][b][:, :], st[g][b][:, :, 5 * CHUNK], keep.ones[:, 0:U4], ALU.mult).then_inc(bd_ok[g], 1)
                for g in range(2):
                    pool.wait_ge(bd_ok[g], n * BD + 3 * BD)
                    pool.tensor_tensor(d2[g][:, :], dh[g][b][:, :], dh[g][1 - b][:, :], ALU.mult).then_inc(decay_ok[g], 1)
                    pool.wait_ge(decay_ok[g], n + 1)
                    pool.wait_ge(sn_ok[g], n + 1)
                    pool.tensor_tensor(sp_[g][b][:, :, :], sn[g][:, :, :], d2[g][:, :, None].to_broadcast([P, U4, P]),
                                       ALU.mult).then_inc(mid_ok[g], 1)
                for g in range(2):
                    pool.wait_ge(gm_ok[g], n * 4 + 4)
                    pool.tensor_tensor(lv[g][:, :, :, :], gm[g][:, :, 0:1, :].to_broadcast([P, U4, LEVELS, P]),
                                       masks[:, g:g + 1, 5:5 + LEVELS, :].to_broadcast([P, U4, LEVELS, P]), ALU.mult).then_inc(lv_ok[g], 1)
            steps(pool, body)

        @block.tensor
        def _(pe):
            for g in range(2):
                pe.sem_inc(y_mm[g], 2)

            def body(n, m, b, chunk):
                def mm(g, j, u, lhsT, rhs, start=True, stop=True, w=P):
                    return pe.matmul(bank[g][j][:, u * w:(u + 1) * w], lhsT, rhs, start=start, stop=stop)
                for g in range(2):
                    pe.wait_ge(bd_ok[g], n * BD + 3 * BD)
                    for e in (u_ok, sn_ok, ru_ok):
                        pe.wait_ge(e[g], n + 1)
                    pe.wait_ge(y_ok[g], n * 2 + 2)
                    for u in range(U4):
                        for j in range(3):
                            x = pe.transpose(bank[g][u][:, j * P:(j + 1) * P], bd[g][b][:, u, 2 + j, :], keep.ident[:, :])
                        x.then_inc(tr_mm[g], 1)
                for g in range(2):
                    for u in range(U4):
                        pe.wait_ge(tm_ok[g], n * 4 + (u + 1))
                        ar = bd[g][b][:, u, 0:2, :]
                        for j in range(2):
                            x = pe.matmul(bank[g][u][:, j * 256:(j + 1) * 256], bd[g][b][:, u, 2 + j, :], ar, start=True, stop=True)
                        x.then_inc(g_mm[g], 1)
                for g in range(2):
                    pe.wait_ge(mid_ok[g], n + 1)
                    pe.wait_ge(gm_ok[g], n * 4 + 4)
                    for u in range(U4):
                        mm(g, 3, u, bd[g][b][:, u, 0, :], sp_[g][b][:, u, :], stop=False)
                        x = mm(g, 3, u, gm[g][:, u, 2, :], tm[g][:, u, 2, :], start=False)
                    x.then_inc(ru_mm[g], 1)
                for g in range(2):
                    pe.wait_ge(tt0_ok[g], n + 1)
                    for u in range(U4):
                        x = pe.transpose(bank[g][0][:, u * P:(u + 1) * P], TT[g][:, u, :], keep.ident[:, :])
                    x.then_inc(t0_mm[g], 1)
                for l in range(1, LEVELS + 1):
                    for g in range(2):
                        if l == 1:
                            pe.wait_ge(lv_ok[g], n + 1)
                            pe.wait_ge(t0_ok[g], n + 1)
                        else:
                            pe.wait_ge(t_ok[g], n * (LEVELS - 1) + (l - 1))
                        for u in range(U4):
                            x = mm(g, 0, u, lv[g][:, u, l - 1, :], T[g][:, u, :])
                        x.then_inc(z_mm[g], 1)
                    for g in range(2):
                        pe.wait_ge(z_ok[g], n * LEVELS + l)
                        if l > 1:
                            pe.wait_ge(tt_ok[g], n * LEVELS + (l - 1))
                        if l < LEVELS:
                            for u in range(U4):
                                mm(g, 1, u, TT[g][:, u, :], Z[g][:, u, :])
                        for u in range(U4):
                            x = mm(g, 2, u, Z[g][:, u, :], TT[g][:, u, :])
                        x.then_inc(p_mm[g], 1)
                for g in range(2):
                    pe.wait_ge(tt_ok[g], n * LEVELS + LEVELS)
                    pe.wait_ge(ru_ok[g], n + 2)
                    for u in range(U4):
                        x = mm(g, 0, u, TT[g][:, u, :], ru[g][:, u, :])
                    x.then_inc(u_mm[g], 1)
                for g in range(2):
                    pe.wait_ge(u_ok[g], n + 2)
                    for u in range(U4):
                        mm(g, 1, u, tm[g][:, u, 0, :], uu[g][:, u, :], stop=False)
                        x = mm(g, 1, u, tm[g][:, u, 1, :], tm[g][:, u, 2, :], start=False)
                    x.then_inc(s_mm[g], 1)
                for g in range(2):
                    for u in range(U4):
                        mm(g, 2, u, sp_[g][b][:, u, :], bd[g][b][:, u, 1, :], stop=False)
                        mm(g, 2, u, uu[g][:, u, :], gm[g][:, u, 1, :], start=False, stop=False)
                        x = mm(g, 2, u, tm[g][:, u, 2, :], gm[g][:, u, 3, :], start=False)
                    x.then_inc(y_mm[g], 1)
            steps(pe, body)

        @block.scalar
        def _(act):
            for g in range(2):
                act.sem_inc(u_ok[g], 1)
                act.sem_inc(ru_ok[g], 1)
                act.sem_inc(y_ok[g], 2)
                for b in range(2):
                    act.sem_inc(y_stored[g][b], 16)
            flat = lambda x: x.rearrange("p u t -> p (u t)")

            def body(n, m, b, chunk):
                for g in range(2):
                    for u in range(U4):
                        act.wait_ge(tr_mm[g], n * 4 + (u + 1))
                        act.activation(tm[g][:, u, :, :].rearrange("p o t -> p (o t)"), bank[g][u][:, 0:3 * P],
                                       ACT.Copy).then_inc(tm_ok[g], 1)
                for g in range(2):
                    act.wait_ge(ru_mm[g], n + 1)
                    act.activation(flat(ru[g][:, :, :]), bank[g][3][:, :], ACT.Copy).then_inc(ru_ok[g], 1)
                for l in range(1, LEVELS + 1):
                    for g in range(2):
                        act.wait_ge(z_mm[g], n * LEVELS + l)
                        act.activation(flat(Z[g][:, :, :]), bank[g][0][:, :], ACT.Copy).then_inc(z_ok[g], 1)
                for g in range(2):
                    act.wait_ge(u_mm[g], n + 1)
                    act.activation(flat(uu[g][:, :, :]), bank[g][0][:, :], ACT.Copy, scale=-1.0).then_inc(u_ok[g], 1)
                for g in range(2):
                    act.wait_ge(y_mm[g], n + 3)
                    act.wait_ge(y_stored[g][b], m * 16 + 16)
                    for h in range(2):
                        hp = slice(HEAD * h, HEAD * h + HEAD)
                        act.activation(yo[g][b][hp, :, :], bank[g][2][hp, :].rearrange("p (u t) -> p u t", t=P)[:, :, hp],
                                       ACT.Copy).then_inc(y_ok[g], 1)
                    act.wait_ge(y_ok[g], n * 2 + 4)
                    act.dma_start(Y[g, :, :, ds(chunk[g] * CHUNK, CHUNK)].rearrange("u p t -> p u t"),
                                  yo[g][b][:, :, :]).then_inc(y_stored[g][b], 16)
            steps(act, body)
            for g in range(2):
                for b in range(2):
                    act.wait_ge(y_stored[g][b], 16 + 16 * (STEPS // 2))

        @block.vector
        def _(dve):
            for g in range(2):
                dve.sem_inc(sn_ok[g], 1)
            dve.wait_ge(masks_in, 16)
            flat = lambda x: x.rearrange("p u t -> p (u t)")

            def body(n, m, b, chunk):
                for g in range(2):
                    for u in range(U4):
                        dve.wait_ge(g_mm[g], n * 4 + (u + 1))
                        dve.tensor_tensor(gm[g][:, u, :, :].rearrange("p o t -> p (o t)"), bank[g][u][:, :],
                                          masks[:, g, 0:4, :].rearrange("p o t -> p (o t)"), ALU.mult).then_inc(gm_ok[g], 1)
                    dve.wait_ge(gm_ok[g], n * 4 + 4)
                    dve.tensor_tensor(TT[g][:, :, :], gm[g][:, :, 0, :], masks[:, g, 4:5, :].to_broadcast([P, U4, P]),
                                      ALU.mult).then_inc(pair_ok[g], 1)
                    dve.wait_ge(pair_ok[g], n + 1)
                    dve.tensor_tensor(TT[g][:, :, :], TT[g][:, :, :], keep.ident[:, None, :].to_broadcast([P, U4, P]),
                                      ALU.add).then_inc(tt0_ok[g], 1)
                for g in range(2):
                    dve.wait_ge(t0_mm[g], n + 1)
                    dve.tensor_copy(flat(T[g][:, :, :]), bank[g][0][:, :]).then_inc(t0_ok[g], 1)
                for l in range(1, LEVELS + 1):
                    for g in range(2):
                        dve.wait_ge(p_mm[g], n * LEVELS + l)
                        if l < LEVELS:
                            dve.tensor_tensor(flat(T[g][:, :, :]), flat(T[g][:, :, :]), bank[g][1][:, :], ALU.subtract).then_inc(t_ok[g], 1)
                        dve.tensor_tensor(flat(TT[g][:, :, :]), flat(TT[g][:, :, :]), bank[g][2][:, :], ALU.subtract).then_inc(tt_ok[g], 1)
                for g in range(2):
                    dve.wait_ge(s_mm[g], n + 1)
                    dve.tensor_tensor(flat(sn[g][:, :, :]), flat(sp_[g][b][:, :, :]), bank[g][1][:, :], ALU.add).then_inc(sn_ok[g], 1)
            steps(dve, body)


def branches(nc, a, keep, ZA, Y, YB, GT, merged):
    with ExitStack() as ctx:
        c = Core(nc, ctx, "branches")
        NT, K4, QP = 512, D_RWKV // P, KD // PAIRS
        SEGS = SEQ // NT
        N = SEGS * PAIRS

        def two(name, shape=(P, NT)):
            return [c.sb(f"{name}{b}", list(shape)) for b in range(2)]
        yf, yr, r, k, v, gd, gu, yc = two("y_fwd"), two("y_rev"), two("r"), two("k"), two("v"), two("gd"), two("g_up", (P, P)), two("y_mid")
        sq, rt, eps = c.sb("y_sq", [P, NT]), c.sb("y_root", [P, NT]), c.sb("gn_eps", [P, 1])
        wa, wb = c.sb("w_branch_a", [P, K4, D]), c.sb("w_branch_b", [P, K4, D])
        ya, yb, gates, t = two("ya", (P, K4, NT)), two("yb", (P, K4, NT)), two("gates", (P, 2, NT)), c.sb("gated", [P, 2, NT])
        mean, bonus, gate, var = c.ps("mean", [P, NT]), c.ps("bonus", [P, NT]), c.ps("gate", [P, NT]), c.ps("var", [P, NT])
        acc = [[c.ps(f"branch{j}{x}", [P, NT]) for x in range(2)] for j in range(2)]
        y_in, yb_in, g_in = ([c.sem(f"{x}{b}") for b in range(2)] for x in ("y_in", "yb_in", "gates_in"))
        names = ("w_branch_in", "y_sum", "rk_ok", "g_sig_ok", "sums_mm", "mid_ok", "sq_ok", "var_mm", "root_ok", "inv_ok", "norm_ok",
                 "affine_ok", "bonus_ok", "ya_ok", "eps_ok", "branch_mm", "gated_ok", "summed")
        (w_in_, y_sum, rk_ok, g_sig_ok, sums_mm, mid_ok, sq_ok, var_mm, root_ok, inv_ok, norm_ok, affine_ok, bonus_ok, ya_ok, eps_ok,
         branch_mm, gated, summed) = (c.sem(n) for n in names)
        block = ctx.enter_context(nc.Block())

        def tiles_at(n):
            return [q for q in range((n - PAIRS) * QP, (n - PAIRS + 1) * QP) if 0 <= q < SEGS * KD]

        @block.sync
        def _(sp):
            def load_instance(n):
                seg, p, b = n // PAIRS, n % PAIRS, n % 2
                if n >= 2:
                    sp.wait_ge(ya_ok, n - 1)
                cols = slice(CTX + seg * NT, CTX + (seg + 1) * NT)
                for d, dst in enumerate((yf, yr)):
                    sp.dma_start(dst[b][:, :], Y[d, p, :, cols]).then_inc(y_in[b], 16)
                for dst, tile in ((r, p), (k, p + PAIRS), (v, p + 2 * PAIRS), (gd, MA - 1)):
                    sp.dma_start(dst[b][:, :], ZA[tile, :, cols]).then_inc(y_in[b], 16)
                sp.dma_start(gu[b][:, :], a["rwkv_g_up"][0][:, p * P:(p + 1) * P]).then_inc(y_in[b], 16)

            def load_yb(seg):
                if seg >= 2:
                    sp.wait_ge(branch_mm, (seg - 1) * KD)
                sp.dma_start(yb[seg % 2][:, :, :], YB[:, :, seg * NT:(seg + 1) * NT].rearrange("m p t -> p m t")).then_inc(yb_in[seg % 2], 16)

            def load_gates(q):
                seg, m, j = q // KD, q % KD, q % 2
                if q >= 2:
                    sp.wait_ge(gated, 2 * q - 2)
                sp.dma_start(gates[j][:, :, :], GT.rearrange("(x m) p t -> m p x t", x=2)[m][:, :, seg * NT:(seg + 1) * NT]).then_inc(g_in[j], 16)
            load_instance(0)
            load_instance(1)
            sp.dma_start(wa[:, :, :], a["w_branch_a"][0].rearrange("(k p) n -> p k n", p=P)).then_inc(w_in_, 16)
            sp.dma_start(wb[:, :, :], a["w_branch_b"][0].rearrange("(k p) n -> p k n", p=P)).then_inc(w_in_, 16)
            for n in range(2, N + PAIRS + 1):
                if n < N:
                    load_instance(n)
                if n % PAIRS == 2 and n < N:
                    load_yb(n // PAIRS)
                for q in tiles_at(n - 1):
                    load_gates(q)

        @block.tensor
        def _(pe):
            def sums(n):
                b = n % 2
                pe.wait_ge(y_sum, n + 1)
                if n:
                    pe.wait_ge(ya_ok, n)
                pe.matmul(mean[:, :], keep.heads[:, :], yf[b][:, :], start=True, stop=True)
                pe.wait_ge(rk_ok, n + 1)
                pe.matmul(bonus[:, :], keep.heads[:, :], r[b][:, :], start=True, stop=True)
                pe.wait_ge(g_sig_ok, n + 1)
                pe.matmul(gate[:, :], gu[b][:, :], gd[b][:, :], start=True, stop=True).then_inc(sums_mm, 1)

            def variance(n):
                pe.wait_ge(sq_ok, n + 1)
                if n:
                    pe.wait_ge(root_ok, n)
                pe.matmul(var[:, :], keep.heads[:, :], sq[:, :], start=True, stop=True).then_inc(var_mm, 1)

            def product(q):
                seg, m, j = q // KD, q % KD, q % 2
                if q == 0:
                    pe.wait_ge(w_in_, 32)
                if m == 0:
                    pe.wait_ge(ya_ok, (seg + 1) * PAIRS)
                    pe.wait_ge(yb_in[seg % 2], 16 * (seg // 2 + 1))
                if q >= 2:
                    pe.wait_ge(gated, 2 * q - 2)
                for x, (w, y) in enumerate(((wa, ya), (wb, yb))):
                    for kk in range(K4):
                        mm = pe.matmul(acc[j][x][:, :], w[:, kk, m * P:(m + 1) * P], y[seg % 2][:, kk, :], start=kk == 0, stop=kk == K4 - 1)
                mm.then_inc(branch_mm, 1)
            for n in range(N + PAIRS):
                if n < N:
                    sums(n)
                for q in tiles_at(n)[:QP // 2]:
                    product(q)
                if n < N:
                    variance(n)
                for q in tiles_at(n)[QP // 2:]:
                    product(q)

        @block.scalar
        def _(act):
            act.wait_ge(eps_ok, 1)

            def gate_sigmoid(n):
                b = n % 2
                act.wait_ge(y_in[b], 112 * (n // 2 + 1))
                act.activation(gd[b][:, :], gd[b][:, :], ACT.Sigmoid).then_inc(g_sig_ok, 1)
            gate_sigmoid(0)
            for n in range(N):
                act.wait_ge(mid_ok, n + 1)
                if n:
                    act.wait_ge(var_mm, n)
                act.activation(sq[:, :], yc[n % 2][:, :], ACT.Square).then_inc(sq_ok, 1)
                if n + 1 < N:
                    gate_sigmoid(n + 1)
                act.wait_ge(var_mm, n + 1)
                if n:
                    act.wait_ge(norm_ok, n)
                act.activation(rt[:, :], var[:, :], ACT.Sqrt, bias=eps[:, :], scale=1.0 / HEAD).then_inc(root_ok, 1)

        @block.vector
        def _(dve):
            dve.memset(eps[:, :], GN_EPS).then_inc(eps_ok, 1)

            def par(name, p):
                return keep.par[:, PC[name] + p:PC[name] + p + 1]

            def inputs(n):
                p, b = n % PAIRS, n % 2
                dve.wait_ge(y_in[b], 112 * (n // 2 + 1))
                dve.tensor_tensor(yf[b][:, :], yf[b][:, :], yr[b][:, :], ALU.add).then_inc(y_sum, 1)
                dve.scalar_tensor_tensor(r[b][:, :], r[b][:, :], par("rwkv_r_k", p), k[b][:, :], ALU.mult, ALU.mult).then_inc(rk_ok, 1)

            def centre(n):
                b = n % 2
                dve.wait_ge(sums_mm, n + 1)
                dve.scalar_tensor_tensor(yc[b][:, :], mean[:, :], -1.0 / HEAD, yf[b][:, :], ALU.mult, ALU.add).then_inc(mid_ok, 1)
                dve.tensor_tensor(v[b][:, :], v[b][:, :], bonus[:, :], ALU.mult).then_inc(bonus_ok, 1)

            def normed(n):
                seg, p, b = n // PAIRS, n % PAIRS, n % 2
                dve.wait_ge(root_ok, n + 1)
                dve.reciprocal(rt[:, :], rt[:, :]).then_inc(inv_ok, 1)
                dve.wait_ge(inv_ok, n + 1)
                dve.tensor_tensor(yc[b][:, :], yc[b][:, :], rt[:, :], ALU.mult).then_inc(norm_ok, 1)
                dve.wait_ge(norm_ok, n + 1)
                dve.wait_ge(bonus_ok, n + 1)
                dve.scalar_tensor_tensor(yc[b][:, :], yc[b][:, :], par("rwkv_ln_w", p), v[b][:, :], ALU.mult, ALU.add).then_inc(affine_ok, 1)
                dve.wait_ge(affine_ok, n + 1)
                if seg >= 2:
                    dve.wait_ge(branch_mm, (seg - 1) * KD)
                dve.scalar_tensor_tensor(ya[seg % 2][:, p, :], yc[b][:, :], par("rwkv_ln_b", p), gate[:, :], ALU.add, ALU.mult).then_inc(ya_ok, 1)

            def gated_sum(q):
                seg, m, j = q // KD, q % KD, q % 2
                dve.wait_ge(branch_mm, q + 1)
                dve.wait_ge(g_in[j], 16 * (q // 2 + 1))
                if q:
                    dve.wait_ge(summed, q)
                for x in range(2):
                    dve.tensor_tensor(t[:, x, :], gates[j][:, x, :], acc[j][x][:, :], ALU.mult).then_inc(gated, 1)
                dve.wait_ge(gated, 2 * q + 2)
                dve.tensor_tensor(merged[:, m, seg * NT:(seg + 1) * NT], t[:, 0, :], t[:, 1, :], ALU.add).then_inc(summed, 1)
            inputs(0)
            for n in range(N + PAIRS):
                if n < N:
                    centre(n)
                for q in tiles_at(n - 1)[QP // 2:]:
                    gated_sum(q)
                if n + 1 < N:
                    inputs(n + 1)
                for q in tiles_at(n)[:QP // 2]:
                    gated_sum(q)
                if n < N:
                    normed(n)
            for q in tiles_at(N + PAIRS - 1)[QP // 2:]:
                gated_sum(q)


def row_of(MOD, row):
    return MOD[0:1, row * D:(row + 1) * D].to_broadcast([P, D])


def residual(nc, a, keep, MOD, merged, X2, H2):
    with ExitStack() as ctx:
        c = Core(nc, ctx, "residual")
        NR = N_GRP + N_EXP

        def two(name, shape):
            return [c.sb(f"{name}{b}", list(shape)) for b in range(2)]
        wo, wr = c.sb("w_out", [P, KD, D]), c.sb("w_router", [P, KD, NR])
        br, gt, sc, sh = c.sb("b_router", [P, NR]), c.sb("gt1_all", [P, D]), c.sb("scale2_all", [P, D]), c.sb("shift2_all", [P, D])
        ms, xt, x2, h2, hT = two("merged_tile", (P, KD, P)), two("x_tile", (P, D)), two("x2", (P, D)), two("h2", (P, D)), two("h2_turned", (P, KD, P))
        sq = c.sb("x2_sq", [P, D])
        ss, rt, rs, eps = c.sb("sum_sq", [P, 2]), c.sb("root", [P, 2]), c.sb("rstd", [P, 2]), c.sb("eps", [P, 1])
        acc = [[c.ps(f"out{b}{h}", [P, 512]) for h in range(2)] for b in range(2)]
        turn = [c.ps(f"h2_turn{h}", [P, 512]) for h in range(2)]
        lg = c.ps("logits", [P, NR])
        const_in, x_in = c.sem("const_in"), [c.sem(f"x_in{b}") for b in range(2)]
        r_in = c.sem("router_in")
        st = [c.sem(f"rows_stored{b}") for b in range(2)]
        names = ("scale_ok", "copied", "out_mm", "gated", "x2_ok", "sq_ok", "root_ok", "rstd_ok", "normed", "scaled", "h2_ok",
                 "turn_mm", "turn_ok", "lg_mm", "lg_ok", "eps_ok")
        (scale_ok, copied, out_mm, gated, x2_ok, sq_ok, root_ok, rstd_ok, normed, scaled, h2_ok, turn_mm, turn_ok, lg_mm, lg_ok,
         eps_ok) = (c.sem(n) for n in names)
        block = ctx.enter_context(nc.Block())

        @block.sync
        def _(sp):
            sp.dma_start(wo[:, :, :], a["w_out"][0].rearrange("(k p) n -> p k n", p=P)).then_inc(const_in, 16)
            for row, dst in ((2, gt), (4, sc), (3, sh)):
                sp.dma_start(dst[:, :], row_of(MOD, row)).then_inc(const_in, 16)
            sp.dma_start(wr[:, :, 0:N_GRP], a["moe_grp_w"][0].rearrange("(k p) n -> p k n", p=P)).then_inc(const_in, 16)
            sp.dma_start(wr[:, :, N_GRP:NR], a["moe_exp_w"][0].rearrange("(k p) n -> p k n", p=P)).then_inc(const_in, 16)
            sp.dma_start(br[:, 0:N_GRP], a["moe_grp_b"].to_broadcast([P, N_GRP])).then_inc(const_in, 16)
            sp.dma_start(br[:, N_GRP:NR], a["moe_exp_b"].to_broadcast([P, N_EXP])).then_inc(const_in, 16)
            sp.dma_start(sq[:, :], a["norm2_g"].to_broadcast([P, D])).then_inc(const_in, 16)
            for b in range(2):
                sp.sem_inc(st[b], 32)
            with sp.Fori(0, TILES // 2) as i:
                for b in range(2):
                    rows = ds(i * (2 * P) + b * P, P)
                    n = i * 2 + b
                    sp.wait_ge(x2_ok, n * 2 + 2)
                    sp.dma_start(xt[b][:, :], a["x"][0][rows, :]).then_inc(x_in[b], 16)
                    sp.wait_ge(x2_ok, n * 2 + 6)
                    sp.dma_start(X2[rows, :], x2[b][:, :]).then_inc(st[b], 16)
                    sp.wait_ge(h2_ok, n + 1)
                    sp.dma_start(H2[rows, :], h2[b][:, :]).then_inc(st[b], 16)
            for b in range(2):
                sp.wait_ge(st[b], 32 + 32 * (TILES // 2))

        @block.gpsimd
        def _(pool):
            with pool.Fori(0, TILES // 2) as i:
                for b in range(2):
                    pool.wait_ge(out_mm, i * 2 + b + 1)
                    pool.tensor_copy(ms[b][:, :, :], merged[:, :, ds(i * (2 * P) + b * P, P)]).then_inc(copied, 1)

        @block.tensor
        def _(pe):
            pe.sem_inc(out_mm, 2)
            pe.wait_ge(const_in, 144)

            def out(n, b):
                pe.wait_ge(copied, n + 1)
                pe.wait_ge(gated, n * 2 + 2)
                for h in range(2):
                    for k in range(KD):
                        mm = pe.matmul(acc[b][h][:, :], ms[b][:, k, :], wo[:, k, h * 512:(h + 1) * 512], start=k == 0, stop=k == KD - 1)
                mm.then_inc(out_mm, 1)

            def router(n, b):
                pe.wait_ge(h2_ok, n + 1)
                pe.wait_ge(turn_ok, n * 2 + 2)
                for k in range(KD):
                    mm = pe.transpose(turn[k // 4][:, (k % 4) * P:(k % 4 + 1) * P], h2[b][:, k * P:(k + 1) * P], keep.ident[:, :])
                mm.then_inc(turn_mm, 1)
                pe.wait_ge(turn_ok, n * 2 + 4)
                pe.wait_ge(lg_ok, n + 1)
                for k in range(KD):
                    mm = pe.matmul(lg[:, :], hT[b][:, k, :], wr[:, k, :], start=k == 0, stop=k == KD - 1)
                mm.then_inc(lg_mm, 1)
            out(0, 0)
            with pe.Fori(0, TILES // 2 - 1) as i:
                out(i * 2 + 1, 1)
                router(i * 2, 0)
                out(i * 2 + 2, 0)
                router(i * 2 + 1, 1)
            out(TILES - 1, 1)
            router(TILES - 2, 0)
            router(TILES - 1, 1)

        @block.scalar
        def _(act):
            act.sem_inc(turn_ok, 2)
            act.wait_ge(eps_ok, 1)
            act.wait_ge(scale_ok, 1)
            with act.Fori(0, TILES // 2) as i:
                for b in range(2):
                    n = i * 2 + b
                    act.wait_ge(x2_ok, n * 2 + 6)
                    act.activation(sq[:, :], x2[b][:, :], ACT.Square, accum_out=ss[:, b:b + 1]).then_inc(sq_ok, 1)
                    act.wait_ge(sq_ok, n + 1)
                    act.activation(rt[:, b:b + 1], ss[:, b:b + 1], ACT.Sqrt, bias=eps[:, :], scale=1.0 / D).then_inc(root_ok, 1)
                    act.wait_ge(rstd_ok, n + 1)
                    act.wait_ge(st[b], i * 32 + 32)
                    act.wait_ge(turn_mm, n + 1)
                    act.activation(h2[b][:, :], x2[b][:, :], ACT.Copy, scale=rs[:, b:b + 1]).then_inc(normed, 1)
                    act.wait_ge(turn_mm, n + 3)
                    for h in range(2):
                        act.activation(hT[b][:, 4 * h:4 * h + 4, :].rearrange("p k t -> p (k t)"), turn[h][:, :], ACT.Copy).then_inc(turn_ok, 1)

        @block.vector
        def _(dve):
            dve.memset(eps[:, :], NORM_EPS).then_inc(eps_ok, 1)
            dve.sem_inc(gated, 4)
            dve.sem_inc(x2_ok, 4)
            dve.sem_inc(lg_ok, 1)
            dve.sem_inc(turn_mm, 2)
            dve.wait_ge(const_in, 144)
            dve.scalar_tensor_tensor(sc[:, :], sc[:, :], 1.0, sq[:, :], ALU.add, ALU.mult).then_inc(scale_ok, 1)
            dve.wait_ge(scale_ok, 1)

            def first(n, i, b):
                dve.wait_ge(out_mm, n + 3)
                dve.wait_ge(x_in[b], i * 16 + 16)
                dve.wait_ge(st[b], i * 32 + 32)
                for h in range(2):
                    cols = slice(h * 512, (h + 1) * 512)
                    dve.tensor_tensor(x2[b][:, cols], acc[b][h][:, :], gt[:, cols], ALU.mult).then_inc(gated, 1)
                for h in range(2):
                    cols = slice(h * 512, (h + 1) * 512)
                    dve.wait_ge(gated, n * 2 + (5 + h))
                    dve.tensor_tensor(x2[b][:, cols], x2[b][:, cols], xt[b][:, cols], ALU.add).then_inc(x2_ok, 1)
                dve.wait_ge(root_ok, n + 1)
                dve.reciprocal(rs[:, b:b + 1], rt[:, b:b + 1]).then_inc(rstd_ok, 1)
                dve.wait_ge(normed, n + 1)
                dve.tensor_tensor(h2[b][:, :], h2[b][:, :], sc[:, :], ALU.mult).then_inc(scaled, 1)
                dve.wait_ge(scaled, n + 1)
                dve.tensor_tensor(h2[b][:, :], h2[b][:, :], sh[:, :], ALU.add).then_inc(h2_ok, 1)

            def second(n):
                dve.wait_ge(lg_mm, n + 1)
                dve.tensor_tensor(keep.logits[:, ds(n, 1), :].rearrange("p n e -> p (n e)"), lg[:, :], br[:, :], ALU.add).then_inc(lg_ok, 1)
            first(0, 0, 0)
            with dve.Fori(0, TILES // 2 - 1) as i:
                second(i * 2)
                first(i * 2 + 1, i, 1)
                second(i * 2 + 1)
                first(i * 2 + 2, i + 1, 0)
            second(TILES - 2)
            first(TILES - 1, TILES // 2 - 1, 1)
            second(TILES - 1)


def routing(nc, a, keep, ROWTOK):
    with ExitStack() as ctx:
        c = Core(nc, ctx, "routing")
        G, E, N, T16 = N_GRP, PER_GRP, N_EXP, TILES
        BIG = 1e30

        g3, gm, gi, goh = c.sb("grp_tmp", [P, T16, G]), c.sb("grp_max", [P, T16]), c.sb("grp_first", [P, T16]), c.sb("grp_hot", [P, T16, G])
        ge, pg = c.sb("grp_exp", [P, T16, G]), c.sb("p_grp", [P, T16])
        mix, sel, s3 = c.sb("grp_logits", [P, T16, G, E]), c.sb("selected", [P, T16, E]), c.sb("sel_tmp", [P, T16, E])
        v = [c.sb(f"top{j}", [P, T16]) for j in range(2)]
        vi = c.sb("top_first", [P, T16])
        hot = [c.sb(f"hot{j}", [P, T16, E]) for j in range(2)]
        M = [c.sb(f"mask{j}", [P, T16, G, E]) for j in range(3)]
        big4, big8 = c.sb("iota_grp", [P, G]), c.sb("iota_exp", [P, E])
        iota16, iota64, tok = c.sb("iota_blocks", [P, TILES]), c.sb("iota_all_blocks", [P, N_BLOCKS]), c.sb("token", [P, T16])
        tri = c.sb("before", [P, P])
        dv, e1 = c.sb("v_diff", [P, T16]), c.sb("v_exp", [P, T16])
        base, tot, slot = c.sb("tile_base", [P, T16, N]), c.sb("tile_total", [P, T16, N]), c.sb("slot_of", [P, T16, N])
        cnt, cmp1, nb, pend, pst = (c.sb("count", [P, N]), c.sb("count_cmp", [P, N, TILES]), c.sb("n_blocks", [P, N]), c.sb("end_block", [P, N]),
                                    c.sb("first_slot", [P, N]))
        used, rank, eo, endq = (c.sb(x, [P, N]) for x in ("used", "rank", "rank_tmp", "rank_end"))
        cmp2, be, pr = c.sb("block_cmp", [P, N_BLOCKS, N]), c.sb("block_exp", [P, N_BLOCKS]), c.sb("prod", [P, T16, N])
        dest = [c.sb(f"dest{j}", [P, T16]) for j in range(2)]
        zero, rows = c.sb("zero_rows", [N_BLOCKS, P]), c.sb("slot_rows", [N_BLOCKS, P])
        cum, total, turn = c.ps("cum", [P, T16 * N]), c.ps("total", [P, T16 * N]), c.ps("slot_turn", [P, N_BLOCKS])
        iota_ok, chain, act_ok, hot_mm, dest_ok = c.sem("iota_ok"), c.sem("chain"), c.sem("act_ok"), c.sem("hot_mm"), c.sem("dest_ok")
        tri0, zero_out, scattered, rows_in, turned, split_ok = (c.sem("tri0"), c.sem("zero_out"), c.sem("scattered"), c.sem("rows_in"),
                                                               c.sem("turned"), c.sem("hot_ok"))
        masks_ok = c.sem("masks_ok")
        block = ctx.enter_context(nc.Block())
        LG, LE = keep.logits[:, :, 0:G], keep.logits[:, :, G:G + N].rearrange("p t (g e) -> p t g e", g=G)
        flat = lambda x: x.rearrange("p t g e -> p (t g e)")
        by_exp = lambda x: x.rearrange("p t g e -> p t (g e)")

        @block.gpsimd
        def _(pool):
            pool.memset(tri[:, :], 1.0).then_inc(tri0, 1)
            pool.memset(zero[:, :], 0.0).then_inc(tri0, 1)
            pool.iota(big4[:, :], pattern=[[1, G]], base=0, channel_multiplier=0, allow_small_or_imprecise_dtypes=True).then_inc(iota_ok, 1)
            pool.iota(big8[:, :], pattern=[[1, E]], base=0, channel_multiplier=0, allow_small_or_imprecise_dtypes=True).then_inc(iota_ok, 1)
            pool.iota(iota16[:, :], pattern=[[SLOTS_BLOCK, TILES]], base=0, channel_multiplier=0,
                      allow_small_or_imprecise_dtypes=True).then_inc(iota_ok, 1)
            pool.iota(iota64[:, :], pattern=[[1, N_BLOCKS]], base=0, channel_multiplier=0,
                      allow_small_or_imprecise_dtypes=True).then_inc(iota_ok, 1)
            pool.iota(tok[:, :], pattern=[[P, T16]], base=0, channel_multiplier=1, allow_small_or_imprecise_dtypes=True).then_inc(iota_ok, 1)
            pool.wait_ge(tri0, 2)
            pool.affine_select(out=tri[:, :], in_=tri[:, :], compare_op=ALU.is_gt, fill=0.0, base=0, pattern=[[1, P]],
                               channel_multiplier=-1).then_inc(iota_ok, 1)
            pool.dma_start(ROWTOK.rearrange("(b p) o -> b (p o)", p=P), zero[:, :]).then_inc(zero_out, 16)
            pool.wait_ge(zero_out, 16)
            pool.wait_ge(dest_ok, 2)
            for j in range(2):
                for t in range(T16):
                    pool.indirect_dma_start(out=ROWTOK, out_offset=bass.IndirectOffsetOnAxis(ap=keep.dest[j][:, t:t + 1], axis=0),
                                            in_=tok[:, t:t + 1], in_offset=None).then_inc(scattered, 16)
            pool.wait_ge(scattered, 16 * 2 * T16)
            pool.dma_start(rows[:, :], ROWTOK.rearrange("(b p) o -> b (p o)", p=P)).then_inc(rows_in, 16)

        @block.scalar
        def _(act):
            act.wait_ge(split_ok, 1)
            act.activation(ge[:, :, :], g3[:, :, :], ACT.Exp).then_inc(act_ok, 1)
            act.wait_ge(split_ok, 2)
            act.activation(e1[:, :], dv[:, :], ACT.Exp).then_inc(act_ok, 1)

        @block.tensor
        def _(pe):
            pe.wait_ge(iota_ok, 6)
            pe.wait_ge(masks_ok, 1)
            pe.matmul(cum[:, :], tri[:, :], flat(M[2][:, :, :, :]), start=True, stop=True)
            pe.matmul(total[:, :], keep.ones[:, 0:P], flat(M[2][:, :, :, :]), start=True, stop=True).then_inc(hot_mm, 1)
            pe.wait_ge(rows_in, 16)
            pe.transpose(turn[:, :], rows[:, :], keep.ident[0:N_BLOCKS, 0:N_BLOCKS]).then_inc(turned, 1)

        @block.vector
        def _(dve):
            done = [0]

            def link(ins):
                done[0] += 1
                ins.then_inc(chain, 1)
                dve.wait_ge(chain, done[0])

            bt = lambda x, n: x[:, :, None].to_broadcast([P, T16, n])

            def first_of(dst_hot, vals, top, iota, first, tmp, n):
                link(dve.tensor_tensor(tmp, vals, bt(top, n), ALU.is_lt))
                link(dve.scalar_tensor_tensor(tmp, tmp, BIG, iota[:, None, :].to_broadcast([P, T16, n]), ALU.mult, ALU.add))
                link(dve.tensor_reduce(first, tmp, AX.X, ALU.min))
                link(dve.tensor_tensor(dst_hot, iota[:, None, :].to_broadcast([P, T16, n]), bt(first, n), ALU.is_equal))

            dve.wait_ge(iota_ok, 6)
            link(dve.tensor_reduce(gm[:, :], LG, AX.X, ALU.max))
            dve.tensor_tensor(g3[:, :, :], LG, bt(gm, G), ALU.subtract).then_inc(split_ok, 1)
            dve.wait_ge(act_ok, 1)
            link(dve.tensor_reduce(pg[:, :], ge[:, :, :], AX.X, ALU.add))
            link(dve.reciprocal(pg[:, :], pg[:, :]))
            first_of(goh[:, :, :], LG, gm, big4, gi[:, :], g3[:, :, :], G)
            link(dve.tensor_tensor(mix[:, :, :, :], LE, goh[:, :, :, None].to_broadcast([P, T16, G, E]), ALU.mult))
            link(dve.tensor_reduce(sel[:, :, :], mix[:, :, :, :].rearrange("p t g e -> p t e g"), AX.X, ALU.add))
            for j in range(2):
                link(dve.tensor_reduce(v[j][:, :], sel[:, :, :], AX.X, ALU.max))
                first_of(hot[j][:, :, :], sel[:, :, :], v[j], big8, vi[:, :], s3[:, :, :], E)
                if j == 0:
                    link(dve.scalar_tensor_tensor(sel[:, :, :], hot[0][:, :, :], -BIG, sel[:, :, :], ALU.mult, ALU.add))
                link(dve.tensor_tensor(M[j][:, :, :, :], goh[:, :, :, None].to_broadcast([P, T16, G, E]),
                                       hot[j][:, :, None, :].to_broadcast([P, T16, G, E]), ALU.mult))
            dve.tensor_tensor(flat(M[2][:, :, :, :]), flat(M[0][:, :, :, :]), flat(M[1][:, :, :, :]), ALU.add).then_inc(masks_ok, 1)
            dve.tensor_tensor(dv[:, :], v[1][:, :], v[0][:, :], ALU.subtract).then_inc(split_ok, 1)
            dve.wait_ge(act_ok, 2)
            link(dve.tensor_scalar(dv[:, :], e1[:, :], 1.0, None, ALU.add))
            link(dve.reciprocal(dv[:, :], dv[:, :]))
            link(dve.tensor_tensor(keep.weights[:, 0, :], dv[:, :], pg[:, :], ALU.mult))
            link(dve.tensor_tensor(keep.weights[:, 1, :], keep.weights[:, 0, :], e1[:, :], ALU.mult))
            dve.wait_ge(hot_mm, 1)
            link(dve.tensor_copy(tot[:, :, :].rearrange("p t e -> p (t e)"), total[:, :]))
            link(dve.memset(base[:, 0, :], 0.0))
            for t in range(1, T16):
                link(dve.tensor_tensor(base[:, t, :], base[:, t - 1, :], tot[:, t - 1, :], ALU.add))
            link(dve.tensor_tensor(cnt[:, :], base[:, T16 - 1, :], tot[:, T16 - 1, :], ALU.add))
            link(dve.tensor_tensor(cmp1[:, :, :], cnt[:, :, None].to_broadcast([P, N, TILES]),
                                   iota16[:, None, :].to_broadcast([P, N, TILES]), ALU.is_gt))
            link(dve.tensor_reduce(nb[:, :], cmp1[:, :, :], AX.X, ALU.add))
            link(dve.tensor_tensor_scan(pend[:, :], keep.ones[:, 0:N], nb[:, :], 0.0, ALU.mult, ALU.add))
            link(dve.tensor_tensor(pst[:, :], pend[:, :], nb[:, :], ALU.subtract))
            link(dve.tensor_scalar(pst[:, :], pst[:, :], float(SLOTS_BLOCK), None, ALU.mult))
            link(dve.tensor_tensor(slot[:, :, :].rearrange("p t e -> p (t e)"), cum[:, :], base[:, :, :].rearrange("p t e -> p (t e)"), ALU.add))
            link(dve.tensor_tensor(slot[:, :, :], slot[:, :, :], pst[:, None, :].to_broadcast([P, T16, N]), ALU.add))
            for j in range(2):
                link(dve.tensor_tensor(pr[:, :, :], slot[:, :, :], by_exp(M[j][:, :, :, :]), ALU.mult))
                link(dve.tensor_reduce(dest[j][:, :], pr[:, :, :], AX.X, ALU.add))
                dve.tensor_copy(keep.dest[j][:, :], dest[j][:, :]).then_inc(dest_ok, 1)
            allq = iota64[:, 0:N]
            link(dve.tensor_scalar(used[:, :], nb[:, :], 0.0, None, ALU.is_gt))
            link(dve.tensor_tensor_scan(rank[:, :], keep.ones[:, 0:N], used[:, :], 0.0, ALU.mult, ALU.add))
            link(dve.tensor_tensor(cmp2[:, 0:N, :], allq[:, :, None].to_broadcast([P, N, N]), rank[:, None, :].to_broadcast([P, N, N]), ALU.is_ge))
            link(dve.tensor_reduce(eo[:, :], cmp2[:, 0:N, :], AX.X, ALU.add))
            link(dve.tensor_scalar(eo[:, :], eo[:, :], float(N_EXP - 1), None, ALU.min))
            link(dve.tensor_copy(keep.rank_expert[:, :], eo[:, :]))
            link(dve.tensor_scalar(eo[:, :], rank[:, :], -1.0, None, ALU.add))
            link(dve.tensor_tensor(cmp2[:, 0:N, :], allq[:, :, None].to_broadcast([P, N, N]), eo[:, None, :].to_broadcast([P, N, N]), ALU.is_ge))
            link(dve.tensor_tensor(cmp2[:, 0:N, :], cmp2[:, 0:N, :], nb[:, None, :].to_broadcast([P, N, N]), ALU.mult))
            link(dve.tensor_reduce(endq[:, :], cmp2[:, 0:N, :], AX.X, ALU.add))
            link(dve.tensor_copy(keep.end_block[:, :], endq[:, :]))
            link(dve.tensor_tensor(cmp2[:, :, :], iota64[:, :, None].to_broadcast([P, N_BLOCKS, N]),
                                   endq[:, None, :].to_broadcast([P, N_BLOCKS, N]), ALU.is_ge))
            link(dve.tensor_reduce(be[:, :], cmp2[:, :, :], AX.X, ALU.add))
            link(dve.tensor_scalar(eo[:, 0:1], rank[:, N - 1:N], -1.0, None, ALU.add))
            link(dve.tensor_scalar(be[:, :], be[:, :], eo[:, 0:1], None, ALU.min))
            link(dve.tensor_copy(keep.block_rank[:, :], be[:, :]))
            link(dve.tensor_scalar(keep.block_place[:, :], keep.block_rank[:, :], 1, None, ALU.bitwise_and))
            link(dve.tensor_scalar(keep.block_even[:, :], keep.block_rank[:, :], N_EXP - 2, None, ALU.bitwise_and))
            link(dve.tensor_scalar(eo[:, 0:1], pend[:, N - 1:N], 0.5, None, ALU.mult))
            link(dve.tensor_scalar(be[:, 0:N_BLOCKS // 2 - 1], iota64[:, 1:N_BLOCKS // 2], eo[:, 0:1], None, ALU.is_lt))
            link(dve.tensor_reduce(eo[:, 1:2], be[:, 0:N_BLOCKS // 2 - 1], AX.X, ALU.add))
            link(dve.tensor_copy(keep.pairs_less_one[:, :], eo[:, 1:2]))
            dve.wait_ge(turned, 1)
            link(dve.tensor_copy(keep.slot_token[:, :], turn[:, :]))


def experts(nc, a, keep, H2, YG):
    with ExitStack() as ctx:
        c = Core(nc, ctx, "experts")
        KE = D_EXP // P
        wg, wu, wd = c.sb("w_gate", [P, 2, KD, D_EXP]), c.sb("w_up", [P, 2, KD, D_EXP]), c.sb("w_down", [P, 2, KE, D])

        def two(name, shape, dt=F32):
            return [c.sb(f"{name}{b}", list(shape), dt) for b in range(2)]
        idx, xg, xT, sg, hh, hT, yo = (two("slot_token", (P, 1), I32), two("rows", (P, D)), two("rows_turned", (P, KD, P)), two("silu", (P, D_EXP)),
                                       two("hidden", (P, D_EXP)), two("hidden_turned", (P, KE, P)), two("y_rows", (P, D)))
        xp = [c.ps(f"row_turn{h}", [P, 512]) for h in range(2)]
        gp, up, hp = c.ps("gate", [P, D_EXP]), c.ps("up", [P, D_EXP]), c.ps("hidden_turn", [P, 512])
        yp = [c.ps(f"down{h}", [P, 512]) for h in range(2)]
        gu_in, d_in = [c.sem(f"gate_up_in{b}") for b in range(2)], [c.sem(f"down_in{b}") for b in range(2)]
        x_in = [c.sem(f"x_in{b}") for b in range(2)]
        gather_go = c.sem("gather_go")
        all_stored, zero_ok, zero_out = c.sem("all_stored"), c.sem("zero_ok"), c.sem("zero_out")
        zero_rows = c.sb("zero_rows", [P, D])
        y_out = [c.sem(f"y_out{b}") for b in range(2)]
        names = ("idx_ok", "x_used", "xturn_mm", "xturn_ok", "gate_mm", "up_mm", "silu_ok", "hid_ok", "hturn_mm", "hturn_ok",
                 "down_mm", "y_ok")
        (idx_ok, x_used, xturn_mm, xturn_ok, gate_mm, up_mm, silu_ok, hid_ok, hturn_mm, hturn_ok, down_mm,
         y_ok) = (c.sem(n) for n in names)
        block = ctx.enter_context(nc.Block())
        PAIRS_MAX = N_BLOCKS // 2

        def all_pairs(eng, body, last):
            less_one = eng.value_load(keep.pairs_less_one[0:1, 0:1], min_val=0, max_val=PAIRS_MAX - 1)
            with eng.Fori(0, PAIRS_MAX - 1) as i:
                with eng.If(i < less_one):
                    body(i)
            last(less_one)

        @block.sync
        def _(sp):
            sp.sem_inc(gu_in[1], 32)
            sp.sem_inc(d_in[1], 16)

            def expert(q):
                return sp.value_load(keep.rank_expert[0:1, ds(q, 1)], min_val=0, max_val=N_EXP - 1)

            def gate_up(e, s):
                for dst, src in ((wg, "moe_w_gate"), (wu, "moe_w_up")):
                    sp.dma_start(dst[:, s, :, :], a[src][0, ds(e, 1), :, :].rearrange("e (k p) n -> p (e k) n", p=P)).then_inc(gu_in[s], 16)

            def down(e, s):
                sp.dma_start(wd[:, s, :, :], a["moe_w_down"][0, ds(e, 1), :, :].rearrange("e (k p) n -> p (e k) n", p=P)).then_inc(d_in[s], 16)
            for s in range(2):
                e = expert(s)
                gate_up(e, s)
                down(e, s)
            with sp.Fori(0, N_EXP // 2 - 1) as i:
                for s in range(2):
                    e = expert(i * 2 + (2 + s))
                    end = sp.value_load(keep.end_block[0:1, ds(i * 2 + s, 1)], min_val=1, max_val=N_BLOCKS)
                    sp.wait_ge(up_mm, end)
                    gate_up(e, s)
                    sp.wait_ge(down_mm, end + 1)
                    down(e, s)
            for s in range(2):
                sp.wait_ge(gu_in[s], 32 * (N_EXP // 2 + s))
                sp.wait_ge(d_in[s], 16 * (N_EXP // 2 + s))
            less_one = sp.value_load(keep.pairs_less_one[0:1, 0:1], min_val=0, max_val=PAIRS_MAX - 1)
            sp.wait_ge(zero_ok, 1)
            with sp.Fori(0, PAIRS_MAX) as i:
                with sp.If(i > less_one):
                    for b in range(2):
                        sp.dma_start(YG[ds(i * 2 * P + b * P, P), :], zero_rows[:, :]).then_inc(zero_out, 16)
                with sp.If(i <= less_one):
                    sp.sem_inc(zero_out, 32)
            sp.wait_ge(zero_out, PAIRS_MAX * 32)

        @block.gpsimd
        def _(pool):
            pool.memset(zero_rows[:, :], 0.0).then_inc(zero_ok, 1)

            def gathers(i):
                for b in range(2):
                    pool.wait_ge(idx_ok, i * 2 + b + 1)
                    pool.wait_ge(xturn_mm, i * 2 + b + 1)
                    pool.sem_inc(gather_go, 1)
                    pool.indirect_dma_start(out=xg[b][:, :], out_offset=None, in_=H2,
                                            in_offset=bass.IndirectOffsetOnAxis(ap=idx[b][:, :], axis=0)).then_inc(x_in[b], 16)
            all_pairs(pool, gathers, gathers)

        @block.tensor
        def _(pe):
            pe.sem_inc(xturn_mm, 2)
            pe.sem_inc(down_mm, 1)

            def turn(n, i, b):
                pe.wait_ge(x_in[b], i * 16 + 16)
                pe.wait_ge(xturn_ok, n * 2 + 2)
                for k in range(KD):
                    mm = pe.transpose(xp[k // 4][:, (k % 4) * P:(k % 4 + 1) * P], xg[b][:, k * P:(k + 1) * P], keep.ident[:, :])
                mm.then_inc(xturn_mm, 1)

            def even_place(n):
                return (pe.value_load(keep.block_even[0:1, ds(n, 1)], min_val=0, max_val=N_EXP - 2),
                        pe.value_load(keep.block_place[0:1, ds(n, 1)], min_val=0, max_val=1))

            def hidden(n, b):
                even, s = even_place(n)
                pe.wait_ge(gu_in[0], even * 16 + 32)
                pe.wait_ge(gu_in[1], (even + s * 2) * 16 + 32)
                pe.wait_ge(xturn_ok, n * 2 + 4)
                pe.wait_ge(silu_ok, n + 1)
                for k in range(KD):
                    mm = pe.matmul(gp[:, :], xT[b][:, k, :], wg[:, ds(s, 1), k, :].rearrange("p s n -> p (s n)"), start=k == 0, stop=k == KD - 1)
                mm.then_inc(gate_mm, 1)
                pe.wait_ge(hid_ok, n + 1)
                for k in range(KD):
                    mm = pe.matmul(up[:, :], xT[b][:, k, :], wu[:, ds(s, 1), k, :].rearrange("p s n -> p (s n)"), start=k == 0, stop=k == KD - 1)
                mm.then_inc(up_mm, 1)

            def turn_hidden(n, b):
                pe.wait_ge(hid_ok, n + 2)
                pe.wait_ge(hturn_ok, n + 1)
                for k in range(KE):
                    mm = pe.transpose(hp[:, k * P:(k + 1) * P], hh[b][:, k * P:(k + 1) * P], keep.ident[:, :])
                mm.then_inc(hturn_mm, 1)

            def down(n, b):
                even, s = even_place(n)
                pe.wait_ge(d_in[0], even * 8 + 16)
                pe.wait_ge(d_in[1], (even + s * 2) * 8 + 16)
                pe.wait_ge(hturn_ok, n + 2)
                pe.wait_ge(y_ok, n * 2 + 2)
                for h in range(2):
                    for k in range(KE):
                        mm = pe.matmul(yp[h][:, :], hT[b][:, k, :], wd[:, ds(s, 1), k, h * 512:(h + 1) * 512].rearrange("p s n -> p (s n)"),
                                       start=k == 0, stop=k == KE - 1)
                mm.then_inc(down_mm, 1)

            def pair(i):
                hidden(i * 2 + 1, 1)
                turn_hidden(i * 2, 0)
                turn(i * 2 + 2, i + 1, 0)
                down(i * 2, 0)
                hidden(i * 2 + 2, 0)
                turn_hidden(i * 2 + 1, 1)
                turn(i * 2 + 3, i + 1, 1)
                down(i * 2 + 1, 1)

            def last_pair(i):
                hidden(i * 2 + 1, 1)
                turn_hidden(i * 2, 0)
                down(i * 2, 0)
                turn_hidden(i * 2 + 1, 1)
                down(i * 2 + 1, 1)
            turn(0, 0, 0)
            hidden(0, 0)
            turn(1, 0, 1)
            all_pairs(pe, pair, last_pair)

        @block.scalar
        def _(act):
            act.sem_inc(xturn_ok, 2)
            act.sem_inc(silu_ok, 1)
            act.sem_inc(hturn_ok, 1)
            for b in range(2):
                act.sem_inc(y_out[b], 16)

            def turned(n, b):
                act.wait_ge(xturn_mm, n + 3)
                for h in range(2):
                    act.activation(xT[b][:, 4 * h:4 * h + 4, :].rearrange("p k t -> p (k t)"), xp[h][:, :], ACT.Copy).then_inc(xturn_ok, 1)

            def silu(n, b):
                act.wait_ge(gate_mm, n + 1)
                act.activation(sg[b][:, :], gp[:, :], ACT.Silu).then_inc(silu_ok, 1)

            def hidden_turned(n, b):
                act.wait_ge(hturn_mm, n + 1)
                act.activation(hT[b][:, :, :].rearrange("p k t -> p (k t)"), hp[:, :], ACT.Copy).then_inc(hturn_ok, 1)

            def store(n, b):
                act.wait_ge(y_ok, n * 2 + 4)
                act.dma_start(YG[ds(n * P, P), :], yo[b][:, :]).then_inc(y_out[b], 16)

            def pair(i):
                silu(i * 2 + 1, 1)
                hidden_turned(i * 2, 0)
                turned(i * 2 + 2, 0)
                silu(i * 2 + 2, 0)
                store(i * 2, 0)
                hidden_turned(i * 2 + 1, 1)
                turned(i * 2 + 3, 1)
                store(i * 2 + 1, 1)

            def last_pair(i):
                silu(i * 2 + 1, 1)
                hidden_turned(i * 2, 0)
                store(i * 2, 0)
                hidden_turned(i * 2 + 1, 1)
                store(i * 2 + 1, 1)
                for b in range(2):
                    act.wait_ge(y_out[b], i * 16 + 32)
                act.sem_inc(all_stored, 1)
            turned(0, 0)
            silu(0, 0)
            turned(1, 1)
            all_pairs(act, pair, last_pair)

        @block.vector
        def _(dve):
            dve.sem_inc(hid_ok, 1)
            dve.sem_inc(y_ok, 2)

            def index(n, b):
                dve.tensor_scalar(idx[b][:, :], keep.slot_token[:, ds(n, 1)], 0.0, None, ALU.add).then_inc(idx_ok, 1)
            for b in range(2):
                index(b, b)

            def product(n, b):
                dve.wait_ge(up_mm, n + 1)
                dve.wait_ge(silu_ok, n + 2)
                dve.tensor_tensor(hh[b][:, :], sg[b][:, :], up[:, :], ALU.mult).then_inc(hid_ok, 1)

            def rows(n, i, b):
                dve.wait_ge(down_mm, n + 2)
                dve.wait_ge(y_out[b], i * 16 + 16)
                for h in range(2):
                    dve.tensor_copy(yo[b][:, h * 512:(h + 1) * 512], yp[h][:, :]).then_inc(y_ok, 1)

            def pair(i):
                for b in range(2):
                    index(i * 2 + (b + 2), b)
                    product(i * 2 + b + 1, 1 - b)
                    rows(i * 2 + b, i, b)

            def last_pair(i):
                product(i * 2 + 1, 1)
                for b in range(2):
                    rows(i * 2 + b, i, b)
            product(0, 0)
            all_pairs(dve, pair, last_pair)


def combine(nc, a, keep, MOD, X2, YG, out):
    with ExitStack() as ctx:
        c = Core(nc, ctx, "combine")

        def two(name, shape, dt=F32):
            return [c.sb(f"{name}{b}", list(shape), dt) for b in range(2)]
        gt, gf = c.sb("gt2_all", [P, D]), c.sb("final_g_all", [P, D])
        y0, y1, xt, ot, wt = two("y_first", (P, D)), two("y_second", (P, D)), two("x2", (P, D)), two("out", (P, D)), two("weights", (P, 2))
        idxs = [[c.sb(f"slot{j}{b}", [P, 1], I32) for j in range(2)] for b in range(2)]
        sq, ss, rt, rs, eps = c.sb("sq", [P, D]), c.sb("sum_sq", [P, 2]), c.sb("root", [P, 2]), c.sb("rstd", [P, 2]), c.sb("eps", [P, 1])
        gather_go = c.sem("gather_go")
        y_in, x_in, o_out = ([c.sem(f"{x}{b}") for b in range(2)] for x in ("y_in", "x_in", "o_out"))
        names = ("const_in", "cols_ok", "first_ok", "both_ok", "gated", "x3_ok", "sq_ok", "root_ok", "rstd_ok", "out_ok",
                 "eps_ok")
        (const_in, cols_ok, first_ok, both_ok, gated, x3_ok, sq_ok, root_ok, rstd_ok, out_ok,
         eps_ok) = (c.sem(n) for n in names)
        block = ctx.enter_context(nc.Block())

        @block.sync
        def _(sp):
            sp.dma_start(gf[:, :], a["final_norm_g"].rearrange("(o n) -> o n", o=1).to_broadcast([P, D])).then_inc(const_in, 16)
            sp.dma_start(gt[:, :], row_of(MOD, 5)).then_inc(const_in, 16)
            for b in range(2):
                sp.sem_inc(o_out[b], 16)
            for b in range(2):
                sp.dma_start(xt[b][:, :], X2[b * P:(b + 1) * P, :]).then_inc(x_in[b], 16)

            def store(n, b, row):
                sp.wait_ge(out_ok, n + 1)
                sp.dma_start(out[0][ds(row, P), :], ot[b][:, :]).then_inc(o_out[b], 16)
            with sp.Fori(0, TILES // 2 - 1) as i:
                for b in range(2):
                    store(i * 2 + b, b, i * (2 * P) + b * P)
                    sp.dma_start(xt[b][:, :], X2[ds(i * (2 * P) + (2 + b) * P, P), :]).then_inc(x_in[b], 16)
            for b in range(2):
                store(TILES - 2 + b, b, (TILES - 2 + b) * P)
            for b in range(2):
                sp.wait_ge(o_out[b], 16 + 16 * (TILES // 2))

        @block.gpsimd
        def _(pool):
            with pool.Fori(0, TILES // 2) as i:
                for b in range(2):
                    n = i * 2 + b
                    pool.wait_ge(cols_ok, n * 3 + 3)
                    pool.wait_ge(x3_ok, n + 1)
                    pool.sem_inc(gather_go, 1)
                    for j, y in enumerate((y0, y1)):
                        pool.indirect_dma_start(out=y[b][:, :], out_offset=None, in_=YG,
                                                in_offset=bass.IndirectOffsetOnAxis(ap=idxs[b][j][:, :], axis=0)).then_inc(y_in[b], 16)

        @block.scalar
        def _(act):
            act.wait_ge(eps_ok, 1)
            with act.Fori(0, TILES // 2) as i:
                for b in range(2):
                    n = i * 2 + b
                    act.wait_ge(y_in[b], i * 32 + 32)
                    act.activation(y0[b][:, :], y0[b][:, :], ACT.Copy, scale=wt[b][:, 0:1]).then_inc(first_ok, 1)
                    act.wait_ge(x3_ok, n + 3)
                    act.activation(sq[:, :], xt[b][:, :], ACT.Square, accum_out=ss[:, b:b + 1]).then_inc(sq_ok, 1)
                    act.wait_ge(sq_ok, n + 1)
                    act.activation(rt[:, b:b + 1], ss[:, b:b + 1], ACT.Sqrt, bias=eps[:, :], scale=1.0 / D).then_inc(root_ok, 1)

        @block.vector
        def _(dve):
            dve.memset(eps[:, :], NORM_EPS).then_inc(eps_ok, 1)
            dve.sem_inc(both_ok, 2)
            dve.sem_inc(x3_ok, 2)
            dve.wait_ge(const_in, 32)

            def columns(n, b):
                for j in range(2):
                    dve.tensor_scalar(idxs[b][j][:, :], keep.dest[j][:, ds(n, 1)], 0.0, None, ALU.add).then_inc(cols_ok, 1)
                w = keep.weights[:, :, ds(n, 1)].rearrange("p j n -> p (j n)")
                dve.tensor_scalar(wt[b][:, :], w, 1.0, None, ALU.mult).then_inc(cols_ok, 1)

            def tile(n, i, b, more):
                dve.wait_ge(first_ok, n + 1)
                dve.scalar_tensor_tensor(y0[b][:, :], y1[b][:, :], wt[b][:, 1:2], y0[b][:, :], ALU.mult, ALU.add).then_inc(both_ok, 1)
                dve.wait_ge(both_ok, n + 3)
                dve.tensor_tensor(y1[b][:, :], y0[b][:, :], gt[:, :], ALU.mult).then_inc(gated, 1)
                dve.wait_ge(gated, n + 1)
                dve.wait_ge(x_in[b], i * 16 + 16)
                dve.tensor_tensor(xt[b][:, :], xt[b][:, :], y1[b][:, :], ALU.add).then_inc(x3_ok, 1)
                dve.wait_ge(root_ok, n + 1)
                dve.reciprocal(rs[:, b:b + 1], rt[:, b:b + 1]).then_inc(rstd_ok, 1)
                dve.wait_ge(rstd_ok, n + 1)
                dve.wait_ge(o_out[b], i * 16 + 16)
                dve.scalar_tensor_tensor(ot[b][:, :], xt[b][:, :], rs[:, b:b + 1], gf[:, :], ALU.mult, ALU.mult).then_inc(out_ok, 1)
                if more:
                    columns(n + 2, b)
            for b in range(2):
                columns(b, b)
            with dve.Fori(0, TILES // 2 - 1) as i:
                for b in range(2):
                    tile(i * 2 + b, i, b, True)
            for b in range(2):
                tile(TILES - 2 + b, TILES // 2 - 1, b, False)


class Keep:

    def __init__(self, nc, ctx):
        c = Core(nc, ctx, "keep")
        self.ident = c.sb("ident", [P, P])
        self.ones = c.sb("ones", [P, 512])
        self.quarter = c.sb("quarter", [P, 4, 32])
        self.dirq = c.sb("dirq", [P, 4])
        self.modc = c.sb("mod_cols", [P, 48, 2])
        self.par = c.sb("par_cols", [P, N_PC])
        self.scale1 = c.sb("scale1", [P, 2, KD])
        self.mu_rest = c.sb("mu_rest", [P, MA])
        self.mu_dir = c.sb("mu_dir", [P, 6, MA])
        self.ka_rest = c.sb("ka_rest", [P, PAIRS])
        self.heads = c.sb("head_blocks", [P, P])
        self.restart = c.sb("chunk_restart", [P, 512])
        self.head_of = c.sb("head_of", [P, 2])
        self.logits = c.sb("router_logits", [P, TILES, N_GRP + N_EXP])
        self.weights = c.sb("expert_weights", [P, 2, TILES])
        self.dest = [c.sb(f"slot_of_choice{j}", [P, TILES], I32) for j in range(2)]
        self.rank_expert = c.sb("rank_expert", [P, N_EXP], I32)
        self.block_rank = c.sb("block_rank", [P, N_BLOCKS], I32)
        self.block_even = c.sb("block_even", [P, N_BLOCKS], I32)
        self.block_place = c.sb("block_place", [P, N_BLOCKS], I32)
        self.pairs_less_one = c.sb("pairs_less_one", [P, 1], I32)
        self.end_block = c.sb("end_block", [P, N_EXP], I32)
        self.slot_token = c.sb("slot_token", [P, N_BLOCKS])


def build(nc, a, out):
    def scratch(name, shape):
        return nc.dram_tensor(name, shape, F32, kind="Internal").ap()
    ZA, UU, GT = scratch("z_shifted", (MA, P, ALL)), scratch("u_gelu", (GROUPS_SG, P, SEQ)), scratch("gates", (2 * KD, P, SEQ))
    YB, OPS, Y = scratch("y_b", (GROUPS_SG, P, SEQ)), scratch("scan_operands", (STEPS, UNITS, P, OPW)), scratch("y_scan", (2, PAIRS, P, ALL))
    X2, H2 = scratch("x2", (SEQ, D)), scratch("h2", (SEQ, D))
    ROWTOK, YG = scratch("slot_to_token", (N_BLOCKS * SLOTS_BLOCK, 1)), scratch("expert_rows", (N_BLOCKS * SLOTS_BLOCK, D))
    MOD = scratch("modulation_rows", (2, 6 * D))
    with ExitStack() as ctx:
        keep = Keep(nc, ctx)
        modulation(nc, a, keep, MOD)
        with nc.sbuf_tensor("h_turned", [P, KD, ALL], F32) as hT:
            normalise(nc, a, keep, hT)
            project(nc, a, keep, hT, ZA, UU, GT)
            spatial_gate(nc, a, keep, hT, UU, YB)
        prepare(nc, a, keep, ZA, OPS)
        scan(nc, a, keep, OPS, Y)
        with nc.sbuf_tensor("merged", [P, KD, SEQ], F32) as merged:
            branches(nc, a, keep, ZA, Y, YB, GT, merged)
            residual(nc, a, keep, MOD, merged, X2, H2)
        routing(nc, a, keep, ROWTOK)
        experts(nc, a, keep, H2, YG)
        combine(nc, a, keep, MOD, X2, YG, out)


_INS = ("x", "c", "ctx", "c_ctx", "ada_w", "ada_b", "norm1_g", "norm2_g", "w_in", "shift_mu", "rwkv_w0", "rwkv_w_up", "rwkv_a0",
        "rwkv_a_up", "rwkv_g_up", "rwkv_k_k", "rwkv_k_a", "rwkv_r_k", "rwkv_ln_w", "rwkv_ln_b", "w_branch_a", "sg_ln_w", "sg_ln_b",
        "sg_w", "sg_b", "w_branch_b", "w_out", "moe_grp_w", "moe_grp_b", "moe_exp_w", "moe_exp_b", "moe_w_gate", "moe_w_up",
        "moe_w_down", "final_norm_g")


def kernel(**inputs):
    import concourse.bacc as bacc
    from concourse.bass_utils import run_bass_kernel_spmd

    nc = bacc.Bacc("TRN2", target_bir_lowering=False, num_devices=1)
    arrays = {f"in_{n}": np.ascontiguousarray(inputs[n]) for n in _INS}
    arrays["in_scan_masks"] = scan_masks()
    a = {n[3:]: nc.dram_tensor(n, v.shape, mybir.dt.from_np(v.dtype), kind="ExternalInput").ap() for n, v in arrays.items()}
    out = nc.dram_tensor("out", (1, SEQ, D), F32, kind="ExternalOutput").ap()
    build(nc, a, out)
    return run_bass_kernel_spmd(nc, [arrays], core_ids=[0]).results[0]["out"]
```

```python
from contextlib import ExitStack

import numpy as np

import concourse.bass as bass
from concourse import mybir

F32 = mybir.dt.float32
F32R = mybir.dt.float32r
I32 = mybir.dt.int32
U32 = mybir.dt.uint32
ALU = mybir.AluOpType
ACT = mybir.ActivationFunctionType
AX = mybir.AxisListType
ds = bass.ds

P = 128
D = 1024
KD = D // P
SEQ = 2048
CTX = 256
ALL = CTX + SEQ
GRID_W = 64
HEAD = 64
D_RWKV = 512
PAIRS = D_RWKV // P
CHUNK = 64
NCTX = CTX // CHUNK
NLAT = SEQ // CHUNK
STEPS = NCTX + NLAT
UNITS = 2 * PAIRS
OPW = 4 * CHUNK + 1
P_A = 1920
MA = P_A // P
D_SG = 512
GROUPS_SG = D_SG // P
Z_U = P_A
Z_V = P_A + D_SG
Z_G = P_A + 2 * D_SG
Z_COLS = Z_G + 2 * D
N_GRP = 4
PER_GRP = 8
N_EXP = N_GRP * PER_GRP
D_EXP = 512
SLOTS_BLOCK = 128
N_BLOCKS = 2 * SEQ // SLOTS_BLOCK + N_EXP
TILES = SEQ // P
NORM_EPS = 1e-6
GN_EPS = 64e-5
KAPPA = float(np.exp(-0.5))

PC = {}
_at = 0
for _name, _n in (("ada_b", 48), ("norm1_g", 8), ("shift_mu", MA), ("rwkv_w0", 8), ("rwkv_a0", 8), ("rwkv_k_k", 4),
                  ("rwkv_k_a", 4), ("rwkv_r_k", 4), ("rwkv_ln_w", 4), ("rwkv_ln_b", 4)):
    PC[_name] = _at
    _at += _n
N_PC = _at


class Core:

    def __init__(self, nc, ctx, stage):
        self.nc, self.ctx, self.stage, self.sems = nc, ctx, stage, []
        ctx.callback(self.clear)

    def sb(self, name, shape, dt=F32):
        return self.ctx.enter_context(self.nc.sbuf_tensor(f"{self.stage}_{name}", shape, dt))

    def ps(self, name, shape, dt=F32):
        return self.ctx.enter_context(self.nc.psum_tensor(f"{self.stage}_{name}", shape, dt))

    def sem(self, name):
        self.sems.append(self.nc.alloc_semaphore(f"{self.stage}_{name}"))
        return self.sems[-1]

    def clear(self):
        if self.sems:
            self.nc.clear_and_free_semaphores(self.sems)
            self.nc.all_engine_barrier()


def modulation(nc, a, keep, MOD):
    with ExitStack() as ctx:
        c = Core(nc, ctx, "modulation")
        NB = 512
        w = [c.sb(f"ada_tile{b}", [P, KD, NB]) for b in range(2)]
        cc = c.sb("cond", [P, 2, KD])
        cs = c.sb("cond_silu", [P, KD, 2])
        bias, mod = c.sb("ada_bias", [2, 6 * D]), c.sb("mod_rows", [2, 6 * D])
        rows = c.sb("par_rows", [N_PC, P])
        acc = [c.ps(f"ada_acc{b}", [P, NB]) for b in range(2)]
        turn = c.ps("par_turn", [P, NB])
        turn2 = c.ps("mod_turn", [P, NB])
        cond_in, rows_in, w_in_, mod_stored = c.sem("cond_in"), c.sem("rows_in"), [c.sem(f"ada_w_in{b}") for b in range(2)], c.sem("mod_stored")
        eye0, eye, silu_ok, acc_ok, mod_ok = c.sem("eye0"), c.sem("eye"), c.sem("silu_ok"), c.sem("acc_ok"), c.sem("mod_ok")
        turned, par_ok, cols_ok, z_ok = c.sem("turned"), c.sem("par_ok"), c.sem("cols_ok"), c.sem("zeroed")
        bias_in = c.sem("bias_in")
        block = ctx.enter_context(nc.Block())
        adaw = a["ada_w"][0].rearrange("(p k) n -> p k n", k=KD)

        @block.sync
        def _(sp):
            sp.dma_start(cc[:, 0, :], a["c"][0].rearrange("(p k) -> p k", k=KD)).then_inc(cond_in, 16)
            sp.dma_start(cc[:, 1, :], a["c_ctx"].rearrange("(p k) -> p k", k=KD)).then_inc(cond_in, 16)
            with sp.Fori(0, 6) as i:
                for b in range(2):
                    sp.wait_ge(mod_ok, i * 2 + b + 1)
                    sp.dma_start(w[b][:, :, :], adaw[:, :, ds(i * (2 * NB) + b * NB, NB)]).then_inc(w_in_[b], 16)
            sp.wait_ge(mod_ok, 14)
            sp.dma_start(MOD, mod[:, :]).then_inc(mod_stored, 16)
            sp.wait_ge(mod_stored, 16)

        @block.gpsimd
        def _(pool):
            for r in range(2):
                pool.dma_start(bias[r:r + 1, :], a["ada_b"]).then_inc(bias_in, 16)
            flat = {"ada_b": a["ada_b"][0], "norm1_g": a["norm1_g"][0], "shift_mu": a["shift_mu"][0],
                    "rwkv_w0": a["rwkv_w0"][0].rearrange("d c -> (d c)"), "rwkv_a0": a["rwkv_a0"][0].rearrange("d c -> (d c)"),
                    "rwkv_k_k": a["rwkv_k_k"][0], "rwkv_k_a": a["rwkv_k_a"][0],
                    "rwkv_r_k": a["rwkv_r_k"][0].rearrange("h k -> (h k)"),
                    "rwkv_ln_w": a["rwkv_ln_w"][0], "rwkv_ln_b": a["rwkv_ln_b"][0]}
            for name, at in PC.items():
                v = flat[name].rearrange("(r p) -> r p", p=P)
                pool.dma_start(rows[at:at + v.shape[0], :], v).then_inc(rows_in, 16)
            pool.memset(keep.ident[:, :], 0.0).then_inc(eye0, 1)
            pool.memset(keep.heads[:, :], 0.0).then_inc(eye0, 1)
            pool.memset(keep.head_of[:, :], 0.0).then_inc(eye0, 1)
            pool.memset(keep.restart[:, :], 1.0).then_inc(eye0, 1)
            pool.memset(keep.quarter[:, :, :], 0.0).then_inc(eye0, 1)
            pool.memset(keep.ones[:, :], 1.0).then_inc(eye, 1)
            pool.wait_ge(eye0, 5)
            pool.wait_ge(eye, 1)
            for h in range(2):
                pool.wait_ge(eye, h + 1)
                pool.memset(keep.heads[h * HEAD:(h + 1) * HEAD, h * HEAD:(h + 1) * HEAD], 1.0).then_inc(eye, 1)
            for h in range(2):
                pool.wait_ge(eye, h + 3)
                pool.memset(keep.head_of[h * HEAD:(h + 1) * HEAD, h:h + 1], 1.0).then_inc(eye, 1)
            pool.wait_ge(eye, 5)
            pool.memset(keep.restart[:, :].rearrange("p (c t) -> p c t", t=CHUNK)[:, :, 0:1], 0.0).then_inc(eye, 1)
            pool.affine_select(out=keep.ident[:, :], in_=keep.ident[:, :], compare_op=ALU.not_equal, fill=1.0, base=0,
                               pattern=[[-1, P]], channel_multiplier=1).then_inc(eye, 1)
            pool.affine_select(out=keep.quarter[:, :, :], in_=keep.quarter[:, :, :], compare_op=ALU.not_equal, fill=1.0,
                               base=0, pattern=[[-1, 4], [-4, 32]], channel_multiplier=1).then_inc(eye, 1)

        @block.scalar
        def _(act):
            act.wait_ge(cond_in, 32)
            for v in range(2):
                act.activation(cs[:, :, v], cc[:, v, :], ACT.Silu).then_inc(silu_ok, 1)

        @block.tensor
        def _(pe):
            pe.wait_ge(silu_ok, 2)
            with pe.Fori(0, 6) as i:
                for b in range(2):
                    pe.wait_ge(w_in_[b], i * 16 + 16)
                    pe.wait_ge(mod_ok, i * 2 + b + 1)
                    for k in range(KD):
                        mm = pe.matmul(acc[b][0:2, :], cs[:, k, :], w[b][:, k, :], start=k == 0, stop=k == KD - 1)
                    mm.then_inc(acc_ok, 1)
            pe.wait_ge(eye, 8)
            pe.wait_ge(rows_in, 16 * len(PC))
            pe.transpose(turn[:, 0:N_PC], rows[:, :], keep.ident[0:N_PC, 0:N_PC]).then_inc(turned, 1)
            pe.wait_ge(mod_ok, 14)
            for t in range(48):
                mm = pe.transpose(turn2[:, 2 * t:2 * t + 2], mod[:, t * P:(t + 1) * P], keep.ident[0:2, 0:2])
            mm.then_inc(turned, 1)

        @block.vector
        def _(dve):
            dve.sem_inc(mod_ok, 2)
            dve.wait_ge(bias_in, 32)
            with dve.Fori(0, 6) as i:
                for b in range(2):
                    dve.wait_ge(acc_ok, i * 2 + b + 1)
                    dve.tensor_tensor(mod[:, ds(i * (2 * NB) + b * NB, NB)], acc[b][0:2, :],
                                      bias[:, ds(i * (2 * NB) + b * NB, NB)], ALU.add).then_inc(mod_ok, 1)
            dve.wait_ge(eye, 8)
            dve.tensor_reduce(keep.dirq[:, :], keep.quarter[:, :, :], AX.X, ALU.add).then_inc(z_ok, 1)
            dve.wait_ge(turned, 1)
            dve.tensor_copy(keep.par[:, :], turn[:, 0:N_PC]).then_inc(par_ok, 1)
            dve.wait_ge(turned, 2)
            dve.tensor_copy(keep.modc[:, :, :], turn2[:, 0:96].rearrange("p (t v) -> p t v", v=2)).then_inc(par_ok, 1)
            dve.wait_ge(par_ok, 2)
            dve.wait_ge(z_ok, 1)
            for v in range(2):
                dve.scalar_tensor_tensor(keep.scale1[:, v, :], keep.modc[:, KD:2 * KD, v], 1.0,
                                         keep.par[:, PC["norm1_g"]:PC["norm1_g"] + KD], ALU.add, ALU.mult).then_inc(cols_ok, 1)
            mu = keep.par[:, PC["shift_mu"]:PC["shift_mu"] + MA]
            dve.tensor_scalar(keep.mu_rest[:, :], mu, -1.0, 1.0, ALU.mult, ALU.add).then_inc(cols_ok, 1)
            for q in range(4):
                dve.tensor_scalar(keep.mu_dir[:, q, :], mu, keep.dirq[:, q:q + 1], None, ALU.mult).then_inc(cols_ok, 1)
            dve.wait_ge(cols_ok, 7)
            for q in range(2):
                dve.tensor_tensor(keep.mu_dir[:, 4 + q, :], keep.mu_dir[:, q, :], keep.mu_dir[:, q + 2, :],
                                  ALU.add).then_inc(cols_ok, 1)
            ka = keep.par[:, PC["rwkv_k_a"]:PC["rwkv_k_a"] + PAIRS]
            dve.tensor_scalar(keep.ka_rest[:, :], ka, -1.0, 1.0, ALU.mult, ALU.add).then_inc(cols_ok, 1)


HIGH_BITS = -4096


def mask_high(dve, high, x):
    return dve.tensor_scalar(high.bitcast(I32), x.bitcast(I32), HIGH_BITS, None, ALU.bitwise_and)


def normalise(nc, a, keep, lat, con):
    with ExitStack() as ctx:
        c = Core(nc, ctx, "normalise")
        xt = [c.sb(f"x_tile{b}", [P, D]) for b in range(2)]
        xn = [c.sb(f"x_normed{b}", [P, D]) for b in range(2)]
        sq = c.sb("x_squared", [P, D])
        ss = c.sb("sum_squares", [P, 2])
        rt = c.sb("root", [P, 2])
        rs = c.sb("rstd", [P, 2])
        eps = c.sb("eps", [P, 1])
        ht = [c.sb(f"h_tile{b}", [P, KD, P]) for b in range(2)]
        hm = [c.sb(f"h_masked{b}", [P, KD, P]) for b in range(2)]
        turn = [c.ps(f"x_turn{b}", [P, D]) for b in range(2)]
        x_in = [c.sem(f"x_in{b}") for b in range(2)]
        names = ("x_sq", "x_root", "x_rstd", "x_norm", "x_turned", "h_ok", "eps_ok", "masked", "high_ok", "low_ok")
        x_sq, x_root, x_rstd, x_norm, x_turned, h_ok, eps_ok, masked, high_ok, low_ok = (c.sem(n) for n in names)
        block = ctx.enter_context(nc.Block())
        TC = CTX // P
        ctx_rows = a["ctx"][0]
        lat_rows = a["x"][0]

        @block.sync
        def _(sp):
            for b in range(TC):
                sp.dma_start(xt[b][:, :], ctx_rows[b * P:(b + 1) * P, :]).then_inc(x_in[b], 16)
            with sp.Fori(0, TILES // 2) as i:
                for b in range(2):
                    sp.wait_ge(x_norm, i * 2 + b + 1)
                    sp.dma_start(xt[b][:, :], lat_rows[ds(i * (2 * P) + b * P, P), :]).then_inc(x_in[b], 16)

        @block.scalar
        def _(act):
            def tile(n, b, loads):
                act.wait_ge(x_in[b], loads * 16)
                act.wait_ge(x_rstd, n + 1)
                act.activation(sq[:, :], xt[b][:, :], ACT.Square, accum_out=ss[:, b:b + 1]).then_inc(x_sq, 1)
                act.wait_ge(x_sq, n + 1)
                act.activation(rt[:, b:b + 1], ss[:, b:b + 1], ACT.Sqrt, bias=eps[:, :], scale=1.0 / D).then_inc(x_root, 1)
                act.wait_ge(x_rstd, n + 3)
                act.wait_ge(x_turned, n + 1)
                act.activation(xn[b][:, :], xt[b][:, :], ACT.Copy, scale=rs[:, b:b + 1]).then_inc(x_norm, 1)
            act.wait_ge(eps_ok, 1)
            for b in range(TC):
                tile(b, b, 1)
            with act.Fori(0, TILES // 2) as i:
                for b in range(2):
                    tile(i * 2 + b + TC, b, i + 2)

        @block.tensor
        def _(pe):
            pe.sem_inc(x_turned, 2)

            def tile(n, b):
                pe.wait_ge(x_norm, n + 1)
                pe.wait_ge(h_ok, n + 1)
                for k in range(KD):
                    mm = pe.transpose(turn[b][:, k * P:(k + 1) * P], xn[b][:, k * P:(k + 1) * P], keep.ident[:, :])
                mm.then_inc(x_turned, 1)
            for b in range(TC):
                tile(b, b)
            with pe.Fori(0, TILES // 2) as i:
                for b in range(2):
                    tile(i * 2 + b + TC, b)

        @block.vector
        def _(dve):
            dve.memset(eps[:, :], NORM_EPS).then_inc(eps_ok, 1)
            dve.sem_inc(x_rstd, 2)
            dve.sem_inc(h_ok, 2)
            dve.sem_inc(high_ok, 2)

            def rstd(n, b):
                dve.wait_ge(x_root, n + 1)
                dve.reciprocal(rs[:, b:b + 1], rt[:, b:b + 1]).then_inc(x_rstd, 1)

            def tile(n, b, v, parts, col):
                dve.wait_ge(x_turned, n + 3)
                dve.wait_ge(low_ok, n + 1)
                for k in range(KD):
                    ins = dve.tensor_scalar(ht[b][:, k, :], turn[b][:, k * P:(k + 1) * P], keep.scale1[:, v, k:k + 1],
                                            keep.modc[:, k, v:v + 1], ALU.mult, ALU.add)
                ins.then_inc(h_ok, 1)
                dve.wait_ge(h_ok, n + 3)
                dve.wait_ge(high_ok, n + 1)
                mask_high(dve, hm[b][:, :, :], ht[b][:, :, :]).then_inc(masked, 1)
                dve.wait_ge(masked, n + 1)
                dve.tensor_scalar(parts[0][:, :, ds(col, P)].bitcast(F32R), hm[b][:, :, :], 1.0, None, ALU.mult).then_inc(high_ok, 1)
            rstd(0, 0)
            for b in range(TC):
                rstd(b + 1, 1 - b)
                tile(b, b, 1, con, b * P)
            with dve.Fori(0, TILES // 2 - 1) as i:
                for b in range(2):
                    rstd(i * 2 + (b + TC + 1), 1 - b)
                    tile(i * 2 + (b + TC), b, 0, lat, i * (2 * P) + b * P)
            rstd(TC + TILES - 1, 1)
            for b in range(2):
                tile(TC + TILES - 2 + b, b, 0, lat, (TILES - 2 + b) * P)

        @block.gpsimd
        def _(pool):
            pool.sem_inc(low_ok, 2)

            def tile(n, b, parts, col):
                pool.wait_ge(masked, n + 1)
                pool.tensor_tensor(parts[1][:, :, ds(col, P)].bitcast(F32R), ht[b][:, :, :], hm[b][:, :, :], ALU.subtract).then_inc(low_ok, 1)
            for b in range(TC):
                tile(b, b, con, b * P)
            with pool.Fori(0, TILES // 2) as i:
                for b in range(2):
                    tile(i * 2 + b + TC, b, lat, i * (2 * P) + b * P)


def project(nc, a, keep, lat, con, ZA, UU, GT):
    with ExitStack() as ctx:
        c = Core(nc, ctx, "project")
        raw, wm = c.sb("w_tile", [P, KD, P]), c.sb("w_masked", [P, KD, P])
        wh, wl = ([c.sb(f"w_{x}{b}", [P, KD, P]) for b in range(2)] for x in ("high", "low"))
        z = [c.sb("z_raw", [P, ALL]), c.sb("z_mixed", [P, ALL])]
        NG = 5
        acc = [c.ps(f"z_acc{g}", [P, 512]) for g in range(NG)]
        names = ("w_in", "w_masked", "w_copied", "w_split", "z_done", "z_out", "mixed", "stored", "shift", "z_free")
        w_in_, w_masked, w_copied, w_split, z_done, z_out, mixed, stored, shift, z_free = (c.sem(n) for n in names)
        block = ctx.enter_context(nc.Block())
        GC = [(0, CTX)] + [(CTX + 512 * g, 512) for g in range(4)]
        win = a["w_in"][0].rearrange("(k p) n -> p k n", p=P)
        REST, SHIFTED = (D_SG + 2 * D) // P, MA * NG

        @block.sync
        def _(sp):
            def load(col):
                sp.dma_start(raw[:, :, :], win[:, :, ds(col, P)]).then_inc(w_in_, 16)
            load(0)
            with sp.Fori(0, (MA - 1) // 2) as i:
                for b in range(2):
                    sp.wait_ge(w_split, i * 2 + (b + 1))
                    load(i * (2 * P) + (b + 1) * P)
            tiles = MA
            for col, count in ((Z_U, D_SG // P), (Z_G, 2 * D // P)):
                with sp.Fori(0, count // 2) as i:
                    for b in range(2):
                        sp.wait_ge(w_split, i * 2 + (tiles + b))
                        load(i * (2 * P) + (col + b * P))
                tiles += count

        @block.tensor
        def _(pe):
            def tile(n, b, g0, done):
                pe.wait_ge(w_split, n + 1)
                for g in range(g0, NG):
                    pe.wait_ge(z_out, done + (g - g0 + 1))
                    col, nt = GC[g]
                    high, low = lat if g else con
                    at = col - CTX if g else 0
                    for k in range(KD):
                        for j, (w, h) in enumerate(((wh, high), (wh, low), (wl, high))):
                            mm = pe.matmul(acc[g][:, 0:nt], w[b][:, k, :].bitcast(F32R), h[:, k, at:at + nt].bitcast(F32R),
                                           start=(k, j) == (0, 0), stop=(k, j) == (KD - 1, 2))
                    mm.then_inc(z_done, 1)
            with pe.Fori(0, (MA - 1) // 2) as i:
                for b in range(2):
                    tile(i * 2 + b, b, 0, i * (2 * NG) + b * NG)
            tile(MA - 1, 0, 0, (MA - 1) * NG)
            with pe.Fori(0, REST // 2) as i:
                for b in range(2):
                    tile(i * 2 + (MA + b), 1 - b, 1, i * 8 + (SHIFTED + b * 4 + 1))

        @block.scalar
        def _(act):
            act.sem_inc(z_out, NG)

            def tile(b, g0, done, func):
                for g in range(g0, NG):
                    act.wait_ge(z_done, done + (g - g0 + 1))
                    col, nt = GC[g]
                    act.activation(z[b][:, col:col + nt], acc[g][:, 0:nt], func).then_inc(z_out, 1)
            with act.Fori(0, (MA - 1) // 2) as i:
                for b in range(2):
                    act.wait_ge(mixed, i * 2 + (b + 1))
                    tile(0, 0, i * (2 * NG) + b * NG, ACT.Copy)
            act.wait_ge(mixed, MA)
            tile(0, 0, (MA - 1) * NG, ACT.Copy)
            act.wait_ge(mixed, MA + 1)
            done, tiles = SHIFTED, MA
            for count, func in ((D_SG // P, ACT.Gelu_apprx_tanh), (2 * D // P, ACT.Sigmoid)):
                with act.Fori(0, count // 2) as i:
                    for b in range(2):
                        act.wait_ge(z_free, i * 2 + (tiles + b))
                        tile(b, 1, i * 8 + (done + b * 4), func)
                done, tiles = done + 4 * count, tiles + count

        @block.vector
        def _(dve):
            dve.sem_inc(mixed, 1)

            def split(n, b):
                dve.wait_ge(w_in_, n * 16 + 16)
                flat = lambda x: x[:, :, :].rearrange("p k n -> p (k n)")
                mask_high(dve, flat(wm), flat(raw)).then_inc(w_masked, 1)
                dve.wait_ge(w_masked, n + 1)
                dve.tensor_copy(flat(wh[b]).bitcast(F32R), flat(wm)).then_inc(w_copied, 1)
                dve.wait_ge(w_copied, n + 1)
                dve.tensor_tensor(flat(wl[b]).bitcast(F32R), flat(raw), flat(wm), ALU.subtract).then_inc(w_split, 1)

            def mix(n):
                zr, m = z
                mu = lambda q: keep.mu_dir[:, q, ds(n, 1)]
                dve.wait_ge(z_out, n * 5 + (NG + 5))
                dve.wait_ge(z_free, n + 1)
                dve.tensor_scalar(m[:, :], zr[:, :], keep.mu_rest[:, ds(n, 1)], None, ALU.mult).then_inc(shift, 1)
                steps = []
                for q, (to, frm) in enumerate(((slice(1, GRID_W), slice(0, GRID_W - 1)), (slice(0, GRID_W - 1), slice(1, GRID_W)))):
                    mg = m[:, CTX:ALL].rearrange("p (r w) -> p r w", w=GRID_W)
                    zg = zr[:, CTX:ALL].rearrange("p (r w) -> p r w", w=GRID_W)
                    steps.append((mg[:, :, to], zg[:, :, frm], q))
                steps.append((m[:, CTX + GRID_W:ALL], zr[:, CTX:ALL - GRID_W], 2))
                steps.append((m[:, CTX:ALL - GRID_W], zr[:, CTX + GRID_W:ALL], 3))
                steps.append((m[:, 1:CTX], zr[:, 0:CTX - 1], 4))
                steps.append((m[:, 0:CTX - 1], zr[:, 1:CTX], 5))
                for j, (to, frm, q) in enumerate(steps):
                    dve.wait_ge(shift, n * 6 + (j + 1))
                    ins = dve.scalar_tensor_tensor(to, frm, mu(q), to, ALU.mult, ALU.add)
                    ins.then_inc(mixed if j == 5 else shift, 1)
            split(0, 0)
            split(1, 1)
            with dve.Fori(0, (MA - 1) // 2) as i:
                for b in range(2):
                    dve.wait_ge(z_done, i * (2 * NG) + (b + 1) * NG)
                    split(i * 2 + (b + 2), b)
                    mix(i * 2 + b)
            dve.wait_ge(z_done, SHIFTED)
            split(MA + 1, 0)
            mix(MA - 1)
            with dve.Fori(0, REST // 2 - 1) as i:
                for b in range(2):
                    dve.wait_ge(z_done, i * 8 + (SHIFTED + b * 4 + 4))
                    split(i * 2 + (MA + 2 + b), 1 - b)

        @block.gpsimd
        def _(pool):
            pool.sem_inc(z_free, 1)

            def store(n, dst, src):
                pool.dma_start(dst, src).then_inc(stored, 16)
                pool.wait_ge(stored, n * 16 + 16)
                pool.sem_inc(z_free, 1)
            with pool.Fori(0, (MA - 1) // 2) as i:
                for b in range(2):
                    pool.wait_ge(mixed, i * 2 + (b + 2))
                    store(i * 2 + b, ZA[ds(i * 2 + b, 1), :, :].rearrange("m p t -> (m p) t"), z[1][:, :])
            pool.wait_ge(mixed, MA + 1)
            store(MA - 1, ZA[MA - 1], z[1][:, :])
            base, tiles = NG + SHIFTED, MA
            for dst, count in ((UU, D_SG // P), (GT, 2 * D // P)):
                with pool.Fori(0, count // 2) as i:
                    for b in range(2):
                        pool.wait_ge(z_out, i * 8 + (base + b * 4 + 4))
                        store(i * 2 + (tiles + b), dst[ds(i * 2 + b, 1), :, :].rearrange("m p t -> (m p) t"), z[b][:, CTX:ALL])
                base, tiles = base + 4 * count, tiles + count


def spatial_gate(nc, a, keep, lat, UU, YB):
    with ExitStack() as ctx:
        c = Core(nc, ctx, "spatial_gate")
        wv = c.sb("w_v", [P, KD, D_SG])
        hs = [c.sb(f"h_tile{b}", [P, KD, P]) for b in range(2)]
        v = [c.sb(f"v_gelu{b}", [P, D_SG]) for b in range(2)]
        vn = [c.sb(f"v_normed{b}", [P, D_SG]) for b in range(2)]
        ut = [c.sb(f"u_tile{b}", [P, GROUPS_SG, P]) for b in range(2)]
        yb = [c.sb(f"yb_tile{b}", [P, GROUPS_SG, P]) for b in range(2)]
        lnw, lnb = c.sb("sg_ln_w_all", [P, D_SG]), c.sb("sg_ln_b_all", [P, D_SG])
        sgb = c.sb("sg_b_all", [P, GROUPS_SG * P])
        sgw, sgwT = c.sb("sg_w_rows", [P, GROUPS_SG, P]), c.sb("sg_w_turned", [P, GROUPS_SG, P])
        st, mv, rt, rs = c.sb("v_stats", [P, 2, 6]), c.sb("v_meanvar", [P, 2, 2]), c.sb("v_root", [P, 2]), c.sb("v_rstd", [P, 2])
        eps = c.sb("ln_eps", [P, 1])
        acc = [c.ps(f"v_acc{b}", [P, D_SG]) for b in range(2)]
        mix = [c.ps(f"mix_acc{b}", [P, GROUPS_SG * P]) for b in range(2)]
        turn = c.ps("sg_turn", [P, GROUPS_SG * P])
        u_in = [c.sem(f"u_in{b}") for b in range(2)]
        aggr_go = c.sem("aggr_go")
        yb_stored = [c.sem(f"yb_stored{b}") for b in range(2)]
        names = ("const_in", "h_copied", "v_acc_ok", "v_ok", "stats_ok", "mv_ok", "root_ok", "rstd_ok", "centred", "scaled", "vn_ok",
                 "mix_ok", "biased", "yb_ok", "sg_turned", "sg_ready", "eps_ok")
        (const_in, h_copied, v_acc_ok, v_ok, stats_ok, mv_ok, root_ok, rstd_ok, centred, scaled, vn_ok, mix_ok, biased, yb_ok,
         sg_turned, sg_ready, eps_ok) = (c.sem(n) for n in names)
        block = ctx.enter_context(nc.Block())
        win = a["w_in"][0].rearrange("(k p) n -> p k n", p=P)

        @block.sync
        def _(sp):
            sp.dma_start(wv[:, :, :], win[:, :, Z_V:Z_V + D_SG]).then_inc(const_in, 16)
            sp.dma_start(lnw[:, :], a["sg_ln_w"].to_broadcast([P, D_SG])).then_inc(const_in, 16)
            sp.dma_start(lnb[:, :], a["sg_ln_b"].to_broadcast([P, D_SG])).then_inc(const_in, 16)
            sp.dma_start(sgb[:, :], a["sg_b"].rearrange("o g p -> o (g p)").to_broadcast([P, GROUPS_SG * P])).then_inc(const_in, 16)
            sp.dma_start(sgw[:, :, :], a["sg_w"][0].rearrange("g p q -> p g q")).then_inc(const_in, 16)
            for b in range(2):
                sp.sem_inc(yb_stored[b], 16)
                sp.dma_start(ut[b][:, :, :], UU[:, :, b * P:(b + 1) * P].rearrange("m p t -> p m t")).then_inc(u_in[b], 16)
            def store(n, b, col):
                sp.wait_ge(yb_ok, n + 1)
                sp.dma_start(YB[:, :, ds(col, P)].rearrange("m p t -> p m t"), yb[b][:, :, :]).then_inc(yb_stored[b], 16)
            with sp.Fori(0, TILES // 2 - 1) as i:
                for b in range(2):
                    store(i * 2 + b, b, i * (2 * P) + b * P)
                    sp.dma_start(ut[b][:, :, :],
                                 UU[:, :, ds(i * (2 * P) + (2 + b) * P, P)].rearrange("m p t -> p m t")).then_inc(u_in[b], 16)
            for b in range(2):
                store(TILES - 2 + b, b, (TILES - 2 + b) * P)
            for b in range(2):
                sp.wait_ge(yb_stored[b], 16 * (TILES // 2 + 1))

        @block.gpsimd
        def _(pool):
            with pool.Fori(0, TILES // 2) as i:
                for b in range(2):
                    pool.wait_ge(v_acc_ok, i * 2 + b + 1)
                    high, low = (h[:, :, ds(i * (2 * P) + b * P, P)] for h in lat)
                    pool.tensor_tensor(hs[b][:, :, :], high, low, ALU.add).then_inc(h_copied, 1)

        @block.tensor
        def _(pe):
            pe.sem_inc(v_acc_ok, 2)
            pe.wait_ge(const_in, 80)
            for g in range(GROUPS_SG):
                mm = pe.transpose(turn[:, g * P:(g + 1) * P], sgw[:, g, :], keep.ident[:, :])
            mm.then_inc(sg_turned, 1)

            def values(n, b):
                pe.wait_ge(h_copied, n + 1)
                pe.wait_ge(v_ok, n + 1)
                for k in range(KD):
                    mm = pe.matmul(acc[b][:, :], hs[b][:, k, :], wv[:, k, :], start=k == 0, stop=k == KD - 1)
                mm.then_inc(v_acc_ok, 1)

            def mixing(n, b):
                pe.wait_ge(vn_ok, n + 1)
                pe.wait_ge(biased, n + 1)
                for g in range(GROUPS_SG):
                    mm = pe.matmul(mix[b][:, g * P:(g + 1) * P], vn[b][:, g * P:(g + 1) * P], sgwT[:, g, :], start=True, stop=True)
                mm.then_inc(mix_ok, 1)
            pe.wait_ge(sg_ready, 1)
            values(0, 0)
            with pe.Fori(0, TILES // 2 - 1) as i:
                values(i * 2 + 1, 1)
                mixing(i * 2, 0)
                values(i * 2 + 2, 0)
                mixing(i * 2 + 1, 1)
            values(TILES - 1, 1)
            mixing(TILES - 2, 0)
            mixing(TILES - 1, 1)

        @block.scalar
        def _(act):
            act.sem_inc(v_ok, 2)
            act.wait_ge(eps_ok, 1)
            with act.Fori(0, TILES // 2) as i:
                for b in range(2):
                    n = i * 2 + b
                    act.wait_ge(v_acc_ok, n + 3)
                    act.wait_ge(centred, n + 1)
                    act.activation(v[b][:, :], acc[b][:, :], ACT.Gelu_apprx_tanh).then_inc(v_ok, 1)
                    act.wait_ge(mv_ok, n + 1)
                    act.activation(rt[:, b:b + 1], mv[:, b, 1:2], ACT.Sqrt, bias=eps[:, :]).then_inc(root_ok, 1)

        @block.vector
        def _(dve):
            dve.memset(eps[:, :], 1e-5).then_inc(eps_ok, 1)
            dve.sem_inc(centred, 2)
            dve.sem_inc(biased, 2)
            dve.wait_ge(sg_turned, 1)
            dve.tensor_copy(sgwT[:, :, :].rearrange("p g q -> p (g q)"), turn[:, :]).then_inc(sg_ready, 1)
            dve.wait_ge(const_in, 80)
            with dve.Fori(0, TILES // 2) as i:
                for b in range(2):
                    n = i * 2 + b
                    dve.wait_ge(v_ok, n + 3)
                    dve.bn_stats(st[:, b, :], v[b][:, :]).then_inc(stats_ok, 1)
                    dve.wait_ge(stats_ok, n + 1)
                    dve.sem_inc(aggr_go, 1)
                    dve.bn_aggr(mv[:, b, :], st[:, b, :]).then_inc(mv_ok, 1)
                    dve.wait_ge(root_ok, n + 1)
                    dve.reciprocal(rs[:, b:b + 1], rt[:, b:b + 1]).then_inc(rstd_ok, 1)
                    dve.wait_ge(rstd_ok, n + 1)
                    dve.tensor_scalar(vn[b][:, :], v[b][:, :], mv[:, b, 0:1], rs[:, b:b + 1], ALU.subtract, ALU.mult).then_inc(centred, 1)
                    dve.wait_ge(centred, n + 3)
                    dve.tensor_tensor(vn[b][:, :], vn[b][:, :], lnw[:, :], ALU.mult).then_inc(scaled, 1)
                    dve.wait_ge(scaled, n + 1)
                    dve.tensor_tensor(vn[b][:, :], vn[b][:, :], lnb[:, :], ALU.add).then_inc(vn_ok, 1)
                    dve.wait_ge(mix_ok, n + 1)
                    dve.wait_ge(yb_stored[b], i * 16 + 16)
                    yf = yb[b][:, :, :].rearrange("p g t -> p (g t)")
                    dve.tensor_tensor(yf, mix[b][:, :], sgb[:, :], ALU.add).then_inc(biased, 1)
                    dve.wait_ge(biased, n + 3)
                    dve.wait_ge(u_in[b], i * 16 + 16)
                    dve.tensor_tensor(yf, yf, ut[b][:, :, :].rearrange("p g t -> p (g t)"), ALU.mult).then_inc(yb_ok, 1)


def prepare(nc, a, keep, ZA, OPS):
    with ExitStack() as ctx:
        c = Core(nc, ctx, "prepare")
        NT = 512
        SEGS = SEQ // NT
        N = (1 + SEGS) * PAIRS

        def two(name, shape=(P, NT)):
            return [c.sb(f"{name}{b}", list(shape)) for b in range(2)]
        r, k = two("r"), two("k")
        th, ad, wu, au = c.sb("wd_tanh", [P, ALL]), c.sb("ad", [P, ALL]), c.sb("w_up", [P, 2, D_RWKV]), c.sb("a_up", [P, 2, D_RWKV])
        ks, kk, nrm, sq = two("kk_scaled"), two("kk"), two("kk_norm"), c.sb("kk_sq", [P, NT])
        four = (P, 2, NT)
        sg, av, y, q = two("decay_sig", four), two("a_gate", four), two("log_mid", four), two("log_prev", four)
        lc, half, dec = c.sb("log_sum", list(four)), two("half", (P, 2, NT // CHUNK)), two("half_decay", (P, 2, NT // CHUNK))
        ea, er, eb, kd, kka = two("exp_a", four), two("exp_r", four), two("exp_b", four), two("k_dir", four), two("kk_a", four)
        ops = [[c.sb(f"ops{b}{d}", [P, NT // CHUNK, OPW]) for d in range(2)] for b in range(2)]
        argw = [c.ps(f"arg_w{d}", [P, NT]) for d in range(2)]
        arga = [c.ps(f"arg_a{d}", [P, NT]) for d in range(2)]
        ssum = c.ps("kk_sum", [P, NT])
        k_in, r_in, stored = ([c.sem(f"{x}{b}") for b in range(2)] for x in ("k_in", "r_in", "ops_stored"))
        names = ("zeroed", "const_in", "low_in", "tanh_ok", "args_ok", "sig_ok", "sum_mm", "ks_ok", "sq_ok", "root_ok", "scan_ok", "half_ok", "mid_ok",
                 "prev_ok", "exp_ok", "floor_ok", "inv_ok", "kk_ok", "kd_part", "kd_ok", "kka_ok", "ops_ok")
        (zeroed, const_in, low_in, tanh_ok, args_ok, sig_ok, sum_mm, ks_ok, sq_ok, root_ok, scan_ok, half_ok, mid_ok, prev_ok, exp_ok,
         floor_ok, inv_ok, kk_ok, kd_part, kd_ok, kka_ok, ops_ok) = (c.sem(n) for n in names)
        block = ctx.enter_context(nc.Block())

        def steps(eng, body):
            def fixed(n):
                return lambda x: (n + x, (n + x) % PAIRS, (n + x) // 2, (n + x) // PAIRS, NT if n + x >= PAIRS else CTX) if 0 <= n + x < N else None
            for n in range(-2, PAIRS):
                body(fixed(n))
            with eng.Fori(0, SEGS - 1) as i:
                for p in range(PAIRS):
                    body(lambda x: (i * PAIRS + (PAIRS + p + x), (p + x) % PAIRS, i * (PAIRS // 2) + (PAIRS + p + x) // 2, i + (PAIRS + p + x) // PAIRS, NT))
            for n in range(N - PAIRS, N):
                body(fixed(n))

        def wait(eng, sem, value):
            if not (isinstance(value, int) and value <= 0):
                eng.wait_ge(sem, value)

        def col_of(seg, nt):
            return slice(0, CTX) if nt == CTX else ds(seg * NT + (CTX - NT), NT)

        @block.sync
        def _(sp):
            for dst, tile in ((th, 3 * PAIRS), (ad, 3 * PAIRS + 1)):
                sp.dma_start(dst[:, :], ZA[tile]).then_inc(low_in, 16)
            sp.wait_ge(zeroed, 2)
            for d in range(2):
                for dst, src in ((wu, "rwkv_w_up"), (au, "rwkv_a_up")):
                    sp.dma_start(dst[HEAD * d:HEAD * d + HEAD, d, :], a[src][0, d]).then_inc(const_in, 16)

            def step(at):
                if at(0):
                    n, p, m, seg, nt = at(0)
                    nch = nt // CHUNK
                    chunk = slice(0, NCTX) if nt == CTX else ds(seg * nch + (NCTX - nch), nch)
                    sp.wait_ge(ops_ok, n * 10 + 10)
                    for d in range(2):
                        sp.dma_start(OPS[chunk, p + PAIRS * d, :, :].rearrange("s p w -> p s w"), ops[p % 2][d][:, 0:nch, :]).then_inc(stored[p % 2], 16)
                if at(2):
                    n, p, m, seg, nt = at(2)
                    sp.dma_start(r[p % 2][:, 0:nt], ZA[p, :, col_of(seg, nt)]).then_inc(r_in[p % 2], 16)
            steps(sp, step)
            for b in range(2):
                sp.wait_ge(stored[b], 32 * (N // 2))

        @block.tensor
        def _(pe):
            pe.wait_ge(const_in, 64)
            pe.wait_ge(low_in, 32)
            pe.wait_ge(tanh_ok, 1)

            def arguments(n, p, m, seg, nt):
                wait(pe, sig_ok, n * 4)
                cols = slice(p * P, (p + 1) * P)
                for d in range(2):
                    pe.matmul(argw[d][:, 0:nt], wu[:, d, cols], th[:, col_of(seg, nt)], start=True, stop=True)
                    mm = pe.matmul(arga[d][:, 0:nt], au[:, d, cols], ad[:, col_of(seg, nt)], start=True, stop=True)
                mm.then_inc(args_ok, 1)

            def step(at):
                if at(3):
                    arguments(*at(3))
                if at(2):
                    n, p, m, seg, nt = at(2)
                    pe.wait_ge(sq_ok, n + 1)
                    wait(pe, root_ok, n)
                    pe.matmul(ssum[:, 0:nt], keep.heads[:, :], sq[:, 0:nt], start=True, stop=True).then_inc(sum_mm, 1)
            arguments(0, 0, 0, 0, CTX)
            steps(pe, step)

        @block.scalar
        def _(act):
            act.wait_ge(low_in, 32)
            act.activation(th[:, :], th[:, :], ACT.Tanh).then_inc(tanh_ok, 1)

            def sigmoids(n, p, m, seg, nt):
                b = p % 2
                act.wait_ge(args_ok, n + 1)
                wait(act, prev_ok, n * 2 - 2)
                wait(act, kka_ok, n * 2 - 2)
                for d in range(2):
                    for dst, arg, name in ((sg, argw, "rwkv_w0"), (av, arga, "rwkv_a0")):
                        at_ = PC[name] + PAIRS * d + p
                        act.activation(dst[b][:, d, 0:nt], arg[d][:, 0:nt], ACT.Sigmoid, bias=keep.par[:, at_:at_ + 1]).then_inc(sig_ok, 1)

            def exponentials(n, p, m, seg, nt):
                b = p % 2
                wait(act, ops_ok, n * 10 - 10)
                act.wait_ge(sig_ok, n * 4 + 4)
                for d in range(2):
                    act.activation(kd[b][:, d, 0:nt], av[b][:, d, 0:nt], ACT.Identity, scale=keep.par[:, PC["rwkv_k_a"] + p:PC["rwkv_k_a"] + p + 1],
                                   bias=keep.ka_rest[:, p:p + 1]).then_inc(kd_part, 1)
                for d in range(2):
                    act.wait_ge(prev_ok, n * 2 + (d + 1))
                    y_, q_ = y[b][:, d, 0:nt], q[b][:, d, 0:nt]
                    table = ((er, y_, -1), (ea, q_, -1), (eb, y_, 1)) if d == 0 else ((ea, y_, 1), (er, q_, 1), (eb, q_, -1))
                    for dst, src, sign in table:
                        act.activation(dst[b][:, d, 0:nt], src, ACT.Exp, scale=sign * KAPPA).then_inc(exp_ok, 1)
                    nch = nt // CHUNK
                    act.activation(dec[b][:, d, 0:nch], half[b][:, d, 0:nch], ACT.Exp, scale=-KAPPA).then_inc(exp_ok, 1)

            def root(n, p, m, seg, nt):
                b = p % 2
                act.wait_ge(ks_ok, n + 1)
                wait(act, sum_mm, n)
                act.activation(sq[:, 0:nt], ks[b][:, 0:nt], ACT.Square).then_inc(sq_ok, 1)
                act.wait_ge(sum_mm, n + 1)
                wait(act, kk_ok, n - 1)
                act.activation(nrm[b][:, 0:nt], ssum[:, 0:nt], ACT.Sqrt).then_inc(root_ok, 1)

            def step(at):
                if at(2):
                    sigmoids(*at(2))
                if at(1):
                    exponentials(*at(1))
                if at(2):
                    root(*at(2))
            steps(act, step)

        @block.gpsimd
        def _(pool):
            def key(n, p, m, seg, nt):
                wait(pool, ks_ok, n - 1)
                wait(pool, kd_ok, n * 2 - 2)
                pool.dma_start(k[p % 2][:, 0:nt], ZA[p + PAIRS, :, col_of(seg, nt)]).then_inc(k_in[p % 2], 16)

            def step(at):
                if at(1):
                    n, p, m, seg, nt = at(1)
                    b = p % 2
                    wait(pool, exp_ok, n * 8 - 8)
                    for d in range(2):
                        pool.wait_ge(mid_ok, n * 2 + (d + 1))
                        pool.tensor_tensor(q[b][:, d, 0:nt], y[b][:, d, 0:nt], sg[b][:, d, 0:nt], ALU.subtract).then_inc(prev_ok, 1)
                    pool.wait_ge(k_in[b], m * 16 + 16)
                    for d in range(2):
                        pool.wait_ge(kd_part, n * 2 + (d + 1))
                        pool.tensor_tensor(kd[b][:, d, 0:nt], kd[b][:, d, 0:nt], k[b][:, 0:nt], ALU.mult).then_inc(kd_ok, 1)
                if at(3):
                    key(*at(3))
                if at(1):
                    pool.wait_ge(kk_ok, n + 1)
                    pool.wait_ge(sig_ok, n * 4 + 4)
                    wait(pool, ops_ok, n * 10 - 10)
                    for d in range(2):
                        pool.tensor_tensor(kka[b][:, d, 0:nt], kk[b][:, 0:nt], av[b][:, d, 0:nt], ALU.mult).then_inc(kka_ok, 1)
            for dst in (wu, au):
                pool.memset(dst[:, :, :], 0.0).then_inc(zeroed, 1)
            key(0, 0, 0, 0, CTX)
            steps(pool, step)

        @block.vector
        def _(dve):
            by_chunk = lambda x: x.rearrange("p (c t) -> p c t", t=CHUNK)

            def logs(n, p, m, seg, nt):
                b, nch = p % 2, nt // CHUNK
                dve.wait_ge(sig_ok, n * 4 + 4)
                wait(dve, prev_ok, n * 2 - 2)
                wait(dve, mid_ok, n * 2)
                for d in range(2):
                    dve.tensor_tensor_scan(lc[:, d, 0:nt], keep.restart[:, 0:nt], sg[b][:, d, 0:nt], 0.0, ALU.mult,
                                           ALU.add).then_inc(scan_ok, 1)
                wait(dve, exp_ok, n * 8 - 8)
                for d in range(2):
                    dve.wait_ge(scan_ok, n * 2 + (d + 1))
                    dve.tensor_scalar(half[b][:, d, 0:nch], by_chunk(lc[:, d, 0:nt])[:, :, CHUNK - 1], 0.5, None,
                                      ALU.mult).then_inc(half_ok, 1)
                for d in range(2):
                    dve.wait_ge(half_ok, n * 2 + (d + 1))
                    dve.tensor_tensor(by_chunk(y[b][:, d, 0:nt]), by_chunk(lc[:, d, 0:nt]),
                                      half[b][:, d, 0:nch, None].to_broadcast([P, nch, CHUNK]), ALU.subtract).then_inc(mid_ok, 1)

            def direction(n, p, m, seg, nt):
                b = p % 2
                dve.wait_ge(root_ok, n + 1)
                dve.tensor_scalar(nrm[b][:, 0:nt], nrm[b][:, 0:nt], 1e-12, None, ALU.max).then_inc(floor_ok, 1)
                dve.wait_ge(floor_ok, n + 1)
                dve.reciprocal(nrm[b][:, 0:nt], nrm[b][:, 0:nt]).then_inc(inv_ok, 1)
                dve.wait_ge(inv_ok, n + 1)
                wait(dve, kka_ok, n * 2 - 2)
                wait(dve, ops_ok, n * 10 - 10)
                dve.tensor_tensor(kk[b][:, 0:nt], ks[b][:, 0:nt], nrm[b][:, 0:nt], ALU.mult).then_inc(kk_ok, 1)

            def scaled_key(n, p, m, seg, nt):
                b = p % 2
                dve.wait_ge(k_in[b], m * 16 + 16)
                wait(dve, kk_ok, n - 1)
                wait(dve, sq_ok, n - 1)
                dve.tensor_scalar(ks[b][:, 0:nt], k[b][:, 0:nt], keep.par[:, PC["rwkv_k_k"] + p:PC["rwkv_k_k"] + p + 1], None,
                                  ALU.mult).then_inc(ks_ok, 1)

            def operands(n, p, m, seg, nt):
                b, nch = p % 2, nt // CHUNK
                dve.wait_ge(kk_ok, n + 1)
                dve.wait_ge(r_in[b], m * 16 + 16)
                dve.wait_ge(kd_ok, n * 2 + 2)
                dve.wait_ge(kka_ok, n * 2 + 2)
                wait(dve, stored[b], m * 32)
                for d in range(2):
                    dve.wait_ge(exp_ok, n * 8 + 4 * (d + 1))
                    dve.tensor_copy(ops[b][d][:, 0:nch, 0], dec[b][:, d, 0:nch]).then_inc(ops_ok, 1)
                    for s, (x, e) in enumerate(((kk[b][:, 0:nt], ea), (r[b][:, 0:nt], er), (kka[b][:, d, 0:nt], eb),
                                                (kd[b][:, d, 0:nt], eb))):
                        dve.tensor_tensor(ops[b][d][:, 0:nch, 1 + s * CHUNK:1 + (s + 1) * CHUNK], by_chunk(x),
                                          by_chunk(e[b][:, d, 0:nt]), ALU.mult).then_inc(ops_ok, 1)

            def step(at):
                if at(1):
                    logs(*at(1))
                if at(2):
                    scaled_key(*at(2))
                if at(1):
                    direction(*at(1))
                if at(0):
                    operands(*at(0))
            steps(dve, step)


LEVELS = 5
N_MASKS = 4 + 1 + LEVELS


def scan_masks():
    s, t = np.arange(P)[:, None], np.arange(P)[None, :]
    same = s // CHUNK == t // CHUNK
    out = np.zeros((P, 2, N_MASKS, P), np.float32)
    for d in range(2):
        a, b = (s, t) if d == 0 else (t, s)
        for j in range(4):
            out[:, d, j] = same & ((a < b) if j % 2 == 0 else (a <= b))
        for lv in range(LEVELS + 1):
            w = 1 << lv
            out[:, d, 4 + lv] = (a // (2 * w) == b // (2 * w)) & (a // w < b // w)
        out[:, d, 4] *= -1
    return out


def scan(nc, a, keep, ZA, OPS, Y):
    with ExitStack() as ctx:
        c = Core(nc, ctx, "scan")
        U4 = PAIRS
        BD = U4 + 1
        masks = c.sb("masks", [P, 2, N_MASKS, P])

        def g2(name, shape):
            return [c.sb(f"{name}{g}", shape) for g in range(2)]

        def g2b(name, shape):
            return [[c.sb(f"{name}{g}{b}", shape) for b in range(2)] for g in range(2)]
        st, bd, yo, dh = g2b("staged", [P, U4, OPW + CHUNK]), g2b("diag", [P, U4, 5, P]), g2b("y_out", [P, U4, CHUNK]), g2b("decay", [P, U4])
        gm, tm, lv = g2("products", [P, U4, 4, P]), g2("by_token", [P, U4, 3, P]), g2("level_parts", [P, U4, LEVELS, P])
        T, TT, Z = g2("inv", [P, U4, P]), g2("inv_turned", [P, U4, P]), g2("level_prod", [P, U4, P])
        ru, uu, sp_, sn = g2("u_rhs", [P, U4, P]), g2("u", [P, U4, P]), g2b("state_mid", [P, U4, P]), g2("state", [P, U4, P])
        d2 = g2("decay_two", [P, U4])
        bank = [[c.ps(f"bank{g}{j}", [P, 512]) for j in range(4)] for g in range(2)]

        def s2(name):
            return [c.sem(f"{name}{g}") for g in range(2)]
        ops_in = [[c.sem(f"ops_in{g}{b}") for b in range(2)] for g in range(2)]
        y_stored = [[c.sem(f"y_stored{g}{b}") for b in range(2)] for g in range(2)]
        masks_in, zeroed = c.sem("masks_in"), c.sem("diag_zeroed")
        bd_ok, decay_ok, mid_ok, lv_ok = s2("diag_ok"), s2("decay_ok"), s2("state_mid_ok"), s2("levels_ok")
        tr_mm, g_mm, ru_mm, t0_mm, z_mm, p_mm = s2("turned"), s2("products_mm"), s2("u_rhs_mm"), s2("inv0_mm"), s2("z_mm"), s2("p_mm")
        tt_mm = s2("inv_turned_mm")
        u_mm, s_mm, y_mm = s2("u_mm"), s2("state_mm"), s2("y_mm")
        tm_ok, ru_ok, z_ok, u_ok, y_ok = s2("by_token_ok"), s2("u_rhs_ok"), s2("z_ok"), s2("u_ok"), s2("y_ok")
        gm_ok, pair_ok, tt0_ok, t0_ok, t_ok, tt_ok, sn_ok = (s2("products_ok"), s2("pairs_ok"), s2("inv0_turned_ok"), s2("inv0_ok"),
                                                             s2("inv_ok"), s2("inv_turned_ok"), s2("state_ok"))
        block = ctx.enter_context(nc.Block())

        def steps(eng, body):
            with eng.Fori(0, NCTX // 2) as i:
                for b in range(2):
                    body(i * 2 + b, i, b, (i * 2 + b, i * (-2) + (NCTX - 1 - b)))
            with eng.Fori(0, NLAT // 2) as i:
                for b in range(2):
                    body(i * 2 + (NCTX + b), i + NCTX // 2, b, (i * 2 + (NCTX + b), i * (-2) + (STEPS - 1 - b)))

        @block.sync
        def _(sp):
            sp.dma_start(masks[:, :, :, :], a["scan_masks"]).then_inc(masks_in, 16)

            def body(n, m, b, chunk):
                for g in range(2):
                    sp.wait_ge(bd_ok[g], n * BD + BD)
                    sp.dma_start(st[g][b][:, :, 0:OPW],
                                 OPS[ds(chunk[g], 1), U4 * g:U4 * g + U4, :, :].rearrange("c u p w -> p (c u) w")).then_inc(ops_in[g][b], 16)
                    sp.dma_start(st[g][b][:, :, OPW:OPW + CHUNK],
                                 ZA[2 * PAIRS:3 * PAIRS, :, ds(chunk[g] * CHUNK, CHUNK)].rearrange("u p t -> p u t")).then_inc(ops_in[g][b], 16)
            steps(sp, body)

        @block.gpsimd
        def _(pool):
            for g in range(2):
                pool.sem_inc(bd_ok[g], 2 * BD)
                pool.memset(sn[g][:, :, :], 0.0).then_inc(zeroed, 1)
                pool.memset(dh[g][1][:, :], 1.0).then_inc(zeroed, 1)
            pool.wait_ge(zeroed, 4)
            pool.wait_ge(masks_in, 16)

            def body(n, m, b, chunk):
                for g in range(2):
                    pool.wait_ge(ops_in[g][b], m * 32 + 32)
                    pool.wait_ge(y_mm[g], n + 1)
                    for u in range(U4):
                        pool.tensor_tensor(bd[g][b][:, u, :, :].rearrange("p o (h t) -> p o h t", h=2),
                                           st[g][b][:, u, 1:1 + 5 * CHUNK].rearrange("p (o x t) -> p o x t", o=5, x=1).to_broadcast([P, 5, 2, CHUNK]),
                                           keep.head_of[:, None, :, None].to_broadcast([P, 5, 2, CHUNK]), ALU.mult).then_inc(bd_ok[g], 1)
                    pool.tensor_tensor(dh[g][b][:, :], st[g][b][:, :, 0], keep.ones[:, 0:U4], ALU.mult).then_inc(bd_ok[g], 1)
                for g in range(2):
                    pool.wait_ge(bd_ok[g], n * BD + 3 * BD)
                    pool.tensor_tensor(d2[g][:, :], dh[g][b][:, :], dh[g][1 - b][:, :], ALU.mult).then_inc(decay_ok[g], 1)
                    pool.wait_ge(decay_ok[g], n + 1)
                    pool.wait_ge(sn_ok[g], n + 1)
                    pool.tensor_tensor(sp_[g][b][:, :, :], sn[g][:, :, :], d2[g][:, :, None].to_broadcast([P, U4, P]),
                                       ALU.mult).then_inc(mid_ok[g], 1)
                for l in range(LEVELS):
                    for g in range(2):
                        pool.wait_ge(gm_ok[g], n * 4 + 4)
                        pool.tensor_tensor(lv[g][:, :, l, :], gm[g][:, :, 0, :], masks[:, g:g + 1, 5 + l, :].to_broadcast([P, U4, P]),
                                           ALU.mult).then_inc(lv_ok[g], 1)
            steps(pool, body)

        @block.tensor
        def _(pe):
            for g in range(2):
                pe.sem_inc(y_mm[g], 2)

            def body(n, m, b, chunk):
                def mm(g, j, u, lhsT, rhs, start=True, stop=True, w=P):
                    return pe.matmul(bank[g][j][:, u * w:(u + 1) * w], lhsT, rhs, start=start, stop=stop)
                for g in range(2):
                    pe.wait_ge(bd_ok[g], n * BD + 3 * BD)
                    for e in (u_ok, sn_ok, ru_ok):
                        pe.wait_ge(e[g], n + 1)
                    pe.wait_ge(y_ok[g], n * 2 + 2)
                    for u in range(U4):
                        for j in range(3):
                            x = pe.transpose(bank[g][u][:, j * P:(j + 1) * P], bd[g][b][:, u, 2 + j, :], keep.ident[:, :])
                        x.then_inc(tr_mm[g], 1)
                for g in range(2):
                    for u in range(U4):
                        pe.wait_ge(tm_ok[g], n * 4 + (u + 1))
                        ar = bd[g][b][:, u, 0:2, :]
                        for j in range(2):
                            x = pe.matmul(bank[g][u][:, j * 256:(j + 1) * 256], bd[g][b][:, u, 2 + j, :], ar, start=True, stop=True)
                        x.then_inc(g_mm[g], 1)
                for g in range(2):
                    pe.wait_ge(mid_ok[g], n + 1)
                    pe.wait_ge(gm_ok[g], n * 4 + 4)
                    for u in range(U4):
                        mm(g, 3, u, bd[g][b][:, u, 0, :], sp_[g][b][:, u, :], stop=False)
                        x = mm(g, 3, u, gm[g][:, u, 2, :], tm[g][:, u, 2, :], start=False)
                    x.then_inc(ru_mm[g], 1)
                for g in range(2):
                    pe.wait_ge(tt0_ok[g], n + 1)
                    for u in range(U4):
                        x = pe.transpose(bank[g][0][:, u * P:(u + 1) * P], TT[g][:, u, :], keep.ident[:, :])
                    x.then_inc(t0_mm[g], 1)
                for l in range(1, LEVELS + 1):
                    for g in range(2):
                        pe.wait_ge(lv_ok[g], n * LEVELS + l)
                        if l == 1:
                            pe.wait_ge(t0_ok[g], n + 1)
                        else:
                            pe.wait_ge(t_ok[g], n * (LEVELS - 1) + (l - 1))
                        for u in range(U4):
                            x = mm(g, 0, u, lv[g][:, u, l - 1, :], T[g][:, u, :])
                        x.then_inc(z_mm[g], 1)
                        if l > 1:
                            for u in range(U4):
                                x = pe.transpose(bank[g][2][:, u * P:(u + 1) * P], T[g][:, u, :], keep.ident[:, :])
                            x.then_inc(tt_mm[g], 1)
                    for g in range(2):
                        pe.wait_ge(z_ok[g], n * LEVELS + l)
                        if l > 1:
                            pe.wait_ge(tt_ok[g], n * LEVELS + (l - 1))
                        for u in range(U4):
                            if l < LEVELS:
                                x = mm(g, 1, u, TT[g][:, u, :], Z[g][:, u, :])
                            else:
                                x = mm(g, 2, u, Z[g][:, u, :], TT[g][:, u, :])
                        x.then_inc(p_mm[g], 1)
                for g in range(2):
                    pe.wait_ge(tt_ok[g], n * LEVELS + LEVELS)
                    pe.wait_ge(ru_ok[g], n + 2)
                    for u in range(U4):
                        x = mm(g, 0, u, TT[g][:, u, :], ru[g][:, u, :])
                    x.then_inc(u_mm[g], 1)
                for g in range(2):
                    pe.wait_ge(u_ok[g], n + 2)
                    for u in range(U4):
                        mm(g, 1, u, tm[g][:, u, 0, :], uu[g][:, u, :], stop=False)
                        x = mm(g, 1, u, tm[g][:, u, 1, :], tm[g][:, u, 2, :], start=False)
                    x.then_inc(s_mm[g], 1)
                for g in range(2):
                    for u in range(U4):
                        mm(g, 2, u, sp_[g][b][:, u, :], bd[g][b][:, u, 1, :], stop=False)
                        mm(g, 2, u, uu[g][:, u, :], gm[g][:, u, 1, :], start=False, stop=False)
                        x = mm(g, 2, u, tm[g][:, u, 2, :], gm[g][:, u, 3, :], start=False)
                    x.then_inc(y_mm[g], 1)
            steps(pe, body)

        @block.scalar
        def _(act):
            for g in range(2):
                act.sem_inc(u_ok[g], 1)
                act.sem_inc(ru_ok[g], 1)
                act.sem_inc(y_ok[g], 2)
                for b in range(2):
                    act.sem_inc(y_stored[g][b], 16)
            flat = lambda x: x.rearrange("p u t -> p (u t)")

            def body(n, m, b, chunk):
                for g in range(2):
                    for u in range(U4):
                        act.wait_ge(tr_mm[g], n * 4 + (u + 1))
                        act.activation(tm[g][:, u, :, :].rearrange("p o t -> p (o t)"), bank[g][u][:, 0:3 * P],
                                       ACT.Copy).then_inc(tm_ok[g], 1)
                for g in range(2):
                    act.wait_ge(ru_mm[g], n + 1)
                    act.activation(flat(ru[g][:, :, :]), bank[g][3][:, :], ACT.Copy).then_inc(ru_ok[g], 1)
                for l in range(1, LEVELS + 1):
                    for g in range(2):
                        act.wait_ge(z_mm[g], n * LEVELS + l)
                        act.activation(flat(Z[g][:, :, :]), bank[g][0][:, :], ACT.Copy).then_inc(z_ok[g], 1)
                for g in range(2):
                    act.wait_ge(u_mm[g], n + 1)
                    act.activation(flat(uu[g][:, :, :]), bank[g][0][:, :], ACT.Copy, scale=-1.0).then_inc(u_ok[g], 1)
                for g in range(2):
                    act.wait_ge(y_mm[g], n + 3)
                    act.wait_ge(y_stored[g][b], m * 16 + 16)
                    for h in range(2):
                        hp = slice(HEAD * h, HEAD * h + HEAD)
                        act.activation(yo[g][b][hp, :, :], bank[g][2][hp, :].rearrange("p (u t) -> p u t", t=P)[:, :, hp],
                                       ACT.Copy).then_inc(y_ok[g], 1)
                    act.wait_ge(y_ok[g], n * 2 + 4)
                    act.dma_start(Y[g, :, :, ds(chunk[g] * CHUNK, CHUNK)].rearrange("u p t -> p u t"),
                                  yo[g][b][:, :, :]).then_inc(y_stored[g][b], 16)
            steps(act, body)
            for g in range(2):
                for b in range(2):
                    act.wait_ge(y_stored[g][b], 16 + 16 * (STEPS // 2))

        @block.vector
        def _(dve):
            for g in range(2):
                dve.sem_inc(sn_ok[g], 1)
            dve.wait_ge(masks_in, 16)
            flat = lambda x: x.rearrange("p u t -> p (u t)")

            def body(n, m, b, chunk):
                for g in range(2):
                    for u in range(U4):
                        dve.wait_ge(g_mm[g], n * 4 + (u + 1))
                        dve.tensor_tensor(gm[g][:, u, :, :].rearrange("p o t -> p (o t)"), bank[g][u][:, :],
                                          masks[:, g, 0:4, :].rearrange("p o t -> p (o t)"), ALU.mult).then_inc(gm_ok[g], 1)
                    dve.wait_ge(gm_ok[g], n * 4 + 4)
                    dve.tensor_tensor(TT[g][:, :, :], gm[g][:, :, 0, :], masks[:, g, 4:5, :].to_broadcast([P, U4, P]),
                                      ALU.mult).then_inc(pair_ok[g], 1)
                    dve.wait_ge(pair_ok[g], n + 1)
                    dve.tensor_tensor(TT[g][:, :, :], TT[g][:, :, :], keep.ident[:, None, :].to_broadcast([P, U4, P]),
                                      ALU.add).then_inc(tt0_ok[g], 1)
                for g in range(2):
                    dve.wait_ge(t0_mm[g], n + 1)
                    dve.tensor_copy(flat(T[g][:, :, :]), bank[g][0][:, :]).then_inc(t0_ok[g], 1)
                for l in range(1, LEVELS + 1):
                    for g in range(2):
                        dve.wait_ge(p_mm[g], n * LEVELS + l)
                        if l < LEVELS:
                            dve.tensor_tensor(flat(T[g][:, :, :]), flat(T[g][:, :, :]), bank[g][1][:, :], ALU.subtract).then_inc(t_ok[g], 1)
                        else:
                            dve.tensor_tensor(flat(TT[g][:, :, :]), flat(TT[g][:, :, :]), bank[g][2][:, :], ALU.subtract).then_inc(tt_ok[g], 1)
                    if l < LEVELS:
                        for g in range(2):
                            dve.wait_ge(tt_mm[g], n * (LEVELS - 1) + l)
                            dve.tensor_copy(flat(TT[g][:, :, :]), bank[g][2][:, :]).then_inc(tt_ok[g], 1)
                for g in range(2):
                    dve.wait_ge(s_mm[g], n + 1)
                    dve.tensor_tensor(flat(sn[g][:, :, :]), flat(sp_[g][b][:, :, :]), bank[g][1][:, :], ALU.add).then_inc(sn_ok[g], 1)
            steps(dve, body)


def branches(nc, a, keep, ZA, Y, YB, GT, merged):
    with ExitStack() as ctx:
        c = Core(nc, ctx, "branches")
        NT, K4, QP = 512, D_RWKV // P, KD // PAIRS
        SEGS = SEQ // NT
        N = SEGS * PAIRS

        def two(name, shape=(P, NT)):
            return [c.sb(f"{name}{b}", list(shape)) for b in range(2)]
        yf, yr, r, k, v, gd, gu, yc = two("y_fwd"), two("y_rev"), two("r"), two("k"), two("v"), two("gd"), two("g_up", (P, P)), two("y_mid")
        sq, rt, eps = c.sb("y_sq", [P, NT]), c.sb("y_root", [P, NT]), c.sb("gn_eps", [P, 1])
        wa, wb = c.sb("w_branch_a", [P, K4, D]), c.sb("w_branch_b", [P, K4, D])
        ya, yb, gates, t = two("ya", (P, K4, NT)), two("yb", (P, K4, NT)), two("gates", (P, 2, NT)), c.sb("gated", [P, 2, NT])
        mean, bonus, gate, var = c.ps("mean", [P, NT]), c.ps("bonus", [P, NT]), c.ps("gate", [P, NT]), c.ps("var", [P, NT])
        acc = [[c.ps(f"branch{j}{x}", [P, NT]) for x in range(2)] for j in range(2)]
        y_in, yb_in, g_in = ([c.sem(f"{x}{b}") for b in range(2)] for x in ("y_in", "yb_in", "gates_in"))
        names = ("w_branch_in", "y_sum", "rk_ok", "g_sig_ok", "sums_mm", "mid_ok", "sq_ok", "var_mm", "root_ok", "inv_ok", "norm_ok",
                 "affine_ok", "bonus_ok", "ya_ok", "eps_ok", "branch_mm", "gated_ok", "summed")
        (w_in_, y_sum, rk_ok, g_sig_ok, sums_mm, mid_ok, sq_ok, var_mm, root_ok, inv_ok, norm_ok, affine_ok, bonus_ok, ya_ok, eps_ok,
         branch_mm, gated, summed) = (c.sem(n) for n in names)
        block = ctx.enter_context(nc.Block())

        def tiles_at(n):
            return [q for q in range((n - PAIRS) * QP, (n - PAIRS + 1) * QP) if 0 <= q < SEGS * KD]

        @block.sync
        def _(sp):
            def load_instance(n):
                seg, p, b = n // PAIRS, n % PAIRS, n % 2
                if n >= 2:
                    sp.wait_ge(ya_ok, n - 1)
                cols = slice(CTX + seg * NT, CTX + (seg + 1) * NT)
                for d, dst in enumerate((yf, yr)):
                    sp.dma_start(dst[b][:, :], Y[d, p, :, cols]).then_inc(y_in[b], 16)
                for dst, tile in ((r, p), (k, p + PAIRS), (v, p + 2 * PAIRS), (gd, MA - 1)):
                    sp.dma_start(dst[b][:, :], ZA[tile, :, cols]).then_inc(y_in[b], 16)
                sp.dma_start(gu[b][:, :], a["rwkv_g_up"][0][:, p * P:(p + 1) * P]).then_inc(y_in[b], 16)

            def load_yb(seg):
                if seg >= 2:
                    sp.wait_ge(branch_mm, (seg - 1) * KD)
                sp.dma_start(yb[seg % 2][:, :, :], YB[:, :, seg * NT:(seg + 1) * NT].rearrange("m p t -> p m t")).then_inc(yb_in[seg % 2], 16)

            def load_gates(q):
                seg, m, j = q // KD, q % KD, q % 2
                if q >= 2:
                    sp.wait_ge(gated, 2 * q - 2)
                sp.dma_start(gates[j][:, :, :], GT.rearrange("(x m) p t -> m p x t", x=2)[m][:, :, seg * NT:(seg + 1) * NT]).then_inc(g_in[j], 16)
            load_instance(0)
            load_instance(1)
            sp.dma_start(wa[:, :, :], a["w_branch_a"][0].rearrange("(k p) n -> p k n", p=P)).then_inc(w_in_, 16)
            sp.dma_start(wb[:, :, :], a["w_branch_b"][0].rearrange("(k p) n -> p k n", p=P)).then_inc(w_in_, 16)
            for n in range(2, N + PAIRS + 1):
                if n < N:
                    load_instance(n)
                if n % PAIRS == 2 and n < N:
                    load_yb(n // PAIRS)
                for q in tiles_at(n - 1):
                    load_gates(q)

        @block.tensor
        def _(pe):
            def sums(n):
                b = n % 2
                pe.wait_ge(y_sum, n + 1)
                if n:
                    pe.wait_ge(ya_ok, n)
                pe.matmul(mean[:, :], keep.heads[:, :], yf[b][:, :], start=True, stop=True)
                pe.wait_ge(rk_ok, n + 1)
                pe.matmul(bonus[:, :], keep.heads[:, :], r[b][:, :], start=True, stop=True)
                pe.wait_ge(g_sig_ok, n + 1)
                pe.matmul(gate[:, :], gu[b][:, :], gd[b][:, :], start=True, stop=True).then_inc(sums_mm, 1)

            def variance(n):
                pe.wait_ge(sq_ok, n + 1)
                if n:
                    pe.wait_ge(root_ok, n)
                pe.matmul(var[:, :], keep.heads[:, :], sq[:, :], start=True, stop=True).then_inc(var_mm, 1)

            def product(q):
                seg, m, j = q // KD, q % KD, q % 2
                if q == 0:
                    pe.wait_ge(w_in_, 32)
                if m == 0:
                    pe.wait_ge(ya_ok, (seg + 1) * PAIRS)
                    pe.wait_ge(yb_in[seg % 2], 16 * (seg // 2 + 1))
                if q >= 2:
                    pe.wait_ge(gated, 2 * q - 2)
                for x, (w, y) in enumerate(((wa, ya), (wb, yb))):
                    for kk in range(K4):
                        mm = pe.matmul(acc[j][x][:, :], w[:, kk, m * P:(m + 1) * P], y[seg % 2][:, kk, :], start=kk == 0, stop=kk == K4 - 1)
                mm.then_inc(branch_mm, 1)
            for n in range(N + PAIRS):
                if n < N:
                    sums(n)
                for q in tiles_at(n)[:QP // 2]:
                    product(q)
                if n < N:
                    variance(n)
                for q in tiles_at(n)[QP // 2:]:
                    product(q)

        @block.scalar
        def _(act):
            act.wait_ge(eps_ok, 1)

            def gate_sigmoid(n):
                b = n % 2
                act.wait_ge(y_in[b], 112 * (n // 2 + 1))
                act.activation(gd[b][:, :], gd[b][:, :], ACT.Sigmoid).then_inc(g_sig_ok, 1)
            gate_sigmoid(0)
            for n in range(N):
                act.wait_ge(mid_ok, n + 1)
                if n:
                    act.wait_ge(var_mm, n)
                act.activation(sq[:, :], yc[n % 2][:, :], ACT.Square).then_inc(sq_ok, 1)
                if n + 1 < N:
                    gate_sigmoid(n + 1)
                act.wait_ge(var_mm, n + 1)
                if n:
                    act.wait_ge(norm_ok, n)
                act.activation(rt[:, :], var[:, :], ACT.Sqrt, bias=eps[:, :], scale=1.0 / HEAD).then_inc(root_ok, 1)

        @block.vector
        def _(dve):
            dve.memset(eps[:, :], GN_EPS).then_inc(eps_ok, 1)

            def par(name, p):
                return keep.par[:, PC[name] + p:PC[name] + p + 1]

            def inputs(n):
                p, b = n % PAIRS, n % 2
                dve.wait_ge(y_in[b], 112 * (n // 2 + 1))
                dve.tensor_tensor(yf[b][:, :], yf[b][:, :], yr[b][:, :], ALU.add).then_inc(y_sum, 1)
                dve.scalar_tensor_tensor(r[b][:, :], r[b][:, :], par("rwkv_r_k", p), k[b][:, :], ALU.mult, ALU.mult).then_inc(rk_ok, 1)

            def centre(n):
                b = n % 2
                dve.wait_ge(sums_mm, n + 1)
                dve.scalar_tensor_tensor(yc[b][:, :], mean[:, :], -1.0 / HEAD, yf[b][:, :], ALU.mult, ALU.add).then_inc(mid_ok, 1)
                dve.tensor_tensor(v[b][:, :], v[b][:, :], bonus[:, :], ALU.mult).then_inc(bonus_ok, 1)

            def normed(n):
                seg, p, b = n // PAIRS, n % PAIRS, n % 2
                dve.wait_ge(root_ok, n + 1)
                dve.reciprocal(rt[:, :], rt[:, :]).then_inc(inv_ok, 1)
                dve.wait_ge(inv_ok, n + 1)
                dve.tensor_tensor(yc[b][:, :], yc[b][:, :], rt[:, :], ALU.mult).then_inc(norm_ok, 1)
                dve.wait_ge(norm_ok, n + 1)
                dve.wait_ge(bonus_ok, n + 1)
                dve.scalar_tensor_tensor(yc[b][:, :], yc[b][:, :], par("rwkv_ln_w", p), v[b][:, :], ALU.mult, ALU.add).then_inc(affine_ok, 1)
                dve.wait_ge(affine_ok, n + 1)
                if seg >= 2:
                    dve.wait_ge(branch_mm, (seg - 1) * KD)
                dve.scalar_tensor_tensor(ya[seg % 2][:, p, :], yc[b][:, :], par("rwkv_ln_b", p), gate[:, :], ALU.add, ALU.mult).then_inc(ya_ok, 1)

            def gated_sum(q):
                seg, m, j = q // KD, q % KD, q % 2
                dve.wait_ge(branch_mm, q + 1)
                dve.wait_ge(g_in[j], 16 * (q // 2 + 1))
                if q:
                    dve.wait_ge(summed, q)
                for x in range(2):
                    dve.tensor_tensor(t[:, x, :], gates[j][:, x, :], acc[j][x][:, :], ALU.mult).then_inc(gated, 1)
                dve.wait_ge(gated, 2 * q + 2)
                dve.tensor_tensor(merged[:, m, seg * NT:(seg + 1) * NT], t[:, 0, :], t[:, 1, :], ALU.add).then_inc(summed, 1)
            inputs(0)
            for n in range(N + PAIRS):
                if n < N:
                    centre(n)
                for q in tiles_at(n - 1)[QP // 2:]:
                    gated_sum(q)
                if n + 1 < N:
                    inputs(n + 1)
                for q in tiles_at(n)[:QP // 2]:
                    gated_sum(q)
                if n < N:
                    normed(n)
            for q in tiles_at(N + PAIRS - 1)[QP // 2:]:
                gated_sum(q)


def row_of(MOD, row):
    return MOD[0:1, row * D:(row + 1) * D].to_broadcast([P, D])


def residual(nc, a, keep, MOD, merged, X2, H2):
    with ExitStack() as ctx:
        c = Core(nc, ctx, "residual")
        NR = N_GRP + N_EXP

        def two(name, shape):
            return [c.sb(f"{name}{b}", list(shape)) for b in range(2)]
        wo, wr = c.sb("w_out", [P, KD, D]), c.sb("w_router", [P, KD, NR])
        br, gt, sc, sh = c.sb("b_router", [P, NR]), c.sb("gt1_all", [P, D]), c.sb("scale2_all", [P, D]), c.sb("shift2_all", [P, D])
        ms, xt, x2, h2, hT = two("merged_tile", (P, KD, P)), two("x_tile", (P, D)), two("x2", (P, D)), two("h2", (P, D)), two("h2_turned", (P, KD, P))
        sq = c.sb("x2_sq", [P, D])
        ss, rt, rs, eps = c.sb("sum_sq", [P, 2]), c.sb("root", [P, 2]), c.sb("rstd", [P, 2]), c.sb("eps", [P, 1])
        acc = [[c.ps(f"out{b}{h}", [P, 512]) for h in range(2)] for b in range(2)]
        turn = [c.ps(f"h2_turn{h}", [P, 512]) for h in range(2)]
        lg = c.ps("logits", [P, NR])
        const_in, x_in = c.sem("const_in"), [c.sem(f"x_in{b}") for b in range(2)]
        r_in = c.sem("router_in")
        st = [c.sem(f"rows_stored{b}") for b in range(2)]
        names = ("scale_ok", "copied", "out_mm", "gated", "x2_ok", "sq_ok", "root_ok", "rstd_ok", "normed", "scaled", "h2_ok",
                 "turn_mm", "turn_ok", "lg_mm", "lg_ok", "eps_ok")
        (scale_ok, copied, out_mm, gated, x2_ok, sq_ok, root_ok, rstd_ok, normed, scaled, h2_ok, turn_mm, turn_ok, lg_mm, lg_ok,
         eps_ok) = (c.sem(n) for n in names)
        block = ctx.enter_context(nc.Block())

        @block.sync
        def _(sp):
            sp.dma_start(wo[:, :, :], a["w_out"][0].rearrange("(k p) n -> p k n", p=P)).then_inc(const_in, 16)
            for row, dst in ((2, gt), (4, sc), (3, sh)):
                sp.dma_start(dst[:, :], row_of(MOD, row)).then_inc(const_in, 16)
            sp.dma_start(wr[:, :, 0:N_GRP], a["moe_grp_w"][0].rearrange("(k p) n -> p k n", p=P)).then_inc(const_in, 16)
            sp.dma_start(wr[:, :, N_GRP:NR], a["moe_exp_w"][0].rearrange("(k p) n -> p k n", p=P)).then_inc(const_in, 16)
            sp.dma_start(br[:, 0:N_GRP], a["moe_grp_b"].to_broadcast([P, N_GRP])).then_inc(const_in, 16)
            sp.dma_start(br[:, N_GRP:NR], a["moe_exp_b"].to_broadcast([P, N_EXP])).then_inc(const_in, 16)
            sp.dma_start(sq[:, :], a["norm2_g"].to_broadcast([P, D])).then_inc(const_in, 16)
            for b in range(2):
                sp.sem_inc(st[b], 32)
            with sp.Fori(0, TILES // 2) as i:
                for b in range(2):
                    rows = ds(i * (2 * P) + b * P, P)
                    n = i * 2 + b
                    sp.wait_ge(x2_ok, n * 2 + 2)
                    sp.dma_start(xt[b][:, :], a["x"][0][rows, :]).then_inc(x_in[b], 16)
                    sp.wait_ge(x2_ok, n * 2 + 6)
                    sp.dma_start(X2[rows, :], x2[b][:, :]).then_inc(st[b], 16)
                    sp.wait_ge(h2_ok, n + 1)
                    sp.dma_start(H2[rows, :], h2[b][:, :]).then_inc(st[b], 16)
            for b in range(2):
                sp.wait_ge(st[b], 32 + 32 * (TILES // 2))

        @block.gpsimd
        def _(pool):
            with pool.Fori(0, TILES // 2) as i:
                for b in range(2):
                    pool.wait_ge(out_mm, i * 2 + b + 1)
                    pool.tensor_copy(ms[b][:, :, :], merged[:, :, ds(i * (2 * P) + b * P, P)]).then_inc(copied, 1)

        @block.tensor
        def _(pe):
            pe.sem_inc(out_mm, 2)
            pe.wait_ge(const_in, 144)

            def out(n, b, h):
                if h == 0:
                    pe.wait_ge(copied, n + 1)
                    pe.wait_ge(gated, n * 2 + 2)
                for k in range(KD):
                    mm = pe.matmul(acc[b][h][:, :], ms[b][:, k, :], wo[:, k, h * 512:(h + 1) * 512], start=k == 0, stop=k == KD - 1)
                if h == 1:
                    mm.then_inc(out_mm, 1)

            def turn_rows(n, b):
                pe.wait_ge(h2_ok, n + 1)
                pe.wait_ge(turn_ok, n * 2 + 2)
                for k in range(KD):
                    mm = pe.transpose(turn[k // 4][:, (k % 4) * P:(k % 4 + 1) * P], h2[b][:, k * P:(k + 1) * P], keep.ident[:, :])
                mm.then_inc(turn_mm, 1)

            def router(n, b):
                pe.wait_ge(turn_ok, n * 2 + 4)
                pe.wait_ge(lg_ok, n + 1)
                for k in range(KD):
                    mm = pe.matmul(lg[:, :], hT[b][:, k, :], wr[:, k, :], start=k == 0, stop=k == KD - 1)
                mm.then_inc(lg_mm, 1)
            for b in range(2):
                for h in range(2):
                    out(b, b, h)
            turn_rows(0, 0)
            with pe.Fori(0, TILES // 2 - 1) as i:
                for b in range(2):
                    out(i * 2 + (b + 2), b, 0)
                    router(i * 2 + b, b)
                    out(i * 2 + (b + 2), b, 1)
                    turn_rows(i * 2 + (b + 1), 1 - b)
            router(TILES - 2, 0)
            turn_rows(TILES - 1, 1)
            router(TILES - 1, 1)

        @block.scalar
        def _(act):
            act.sem_inc(turn_ok, 2)
            act.wait_ge(eps_ok, 1)
            act.wait_ge(scale_ok, 1)
            with act.Fori(0, TILES // 2) as i:
                for b in range(2):
                    n = i * 2 + b
                    act.wait_ge(x2_ok, n * 2 + 6)
                    act.activation(sq[:, :], x2[b][:, :], ACT.Square, accum_out=ss[:, b:b + 1]).then_inc(sq_ok, 1)
                    act.wait_ge(sq_ok, n + 1)
                    act.activation(rt[:, b:b + 1], ss[:, b:b + 1], ACT.Sqrt, bias=eps[:, :], scale=1.0 / D).then_inc(root_ok, 1)
                    act.wait_ge(rstd_ok, n + 1)
                    act.wait_ge(st[b], i * 32 + 32)
                    act.wait_ge(turn_mm, n + 1)
                    act.activation(h2[b][:, :], x2[b][:, :], ACT.Copy, scale=rs[:, b:b + 1]).then_inc(normed, 1)
                    act.wait_ge(turn_mm, n + 3)
                    for h in range(2):
                        act.activation(hT[b][:, 4 * h:4 * h + 4, :].rearrange("p k t -> p (k t)"), turn[h][:, :], ACT.Copy).then_inc(turn_ok, 1)

        @block.vector
        def _(dve):
            dve.memset(eps[:, :], NORM_EPS).then_inc(eps_ok, 1)
            dve.sem_inc(gated, 4)
            dve.sem_inc(x2_ok, 4)
            dve.sem_inc(lg_ok, 1)
            dve.sem_inc(turn_mm, 2)
            dve.wait_ge(const_in, 144)
            dve.scalar_tensor_tensor(sc[:, :], sc[:, :], 1.0, sq[:, :], ALU.add, ALU.mult).then_inc(scale_ok, 1)
            dve.wait_ge(scale_ok, 1)

            def first(n, i, b):
                dve.wait_ge(out_mm, n + 3)
                dve.wait_ge(x_in[b], i * 16 + 16)
                dve.wait_ge(st[b], i * 32 + 32)
                for h in range(2):
                    cols = slice(h * 512, (h + 1) * 512)
                    dve.tensor_tensor(x2[b][:, cols], acc[b][h][:, :], gt[:, cols], ALU.mult).then_inc(gated, 1)
                for h in range(2):
                    cols = slice(h * 512, (h + 1) * 512)
                    dve.wait_ge(gated, n * 2 + (5 + h))
                    dve.tensor_tensor(x2[b][:, cols], x2[b][:, cols], xt[b][:, cols], ALU.add).then_inc(x2_ok, 1)
                dve.wait_ge(root_ok, n + 1)
                dve.reciprocal(rs[:, b:b + 1], rt[:, b:b + 1]).then_inc(rstd_ok, 1)
                dve.wait_ge(normed, n + 1)
                dve.tensor_tensor(h2[b][:, :], h2[b][:, :], sc[:, :], ALU.mult).then_inc(scaled, 1)
                dve.wait_ge(scaled, n + 1)
                dve.tensor_tensor(h2[b][:, :], h2[b][:, :], sh[:, :], ALU.add).then_inc(h2_ok, 1)

            def second(n):
                dve.wait_ge(lg_mm, n + 1)
                dve.tensor_tensor(keep.logits[:, ds(n, 1), :].rearrange("p n e -> p (n e)"), lg[:, :], br[:, :], ALU.add).then_inc(lg_ok, 1)
            for b in range(2):
                first(b, 0, b)
            with dve.Fori(0, TILES // 2 - 1) as i:
                for b in range(2):
                    second(i * 2 + b)
                    first(i * 2 + (b + 2), i + 1, b)
            second(TILES - 2)
            second(TILES - 1)


def routing(nc, a, keep, ROWTOK):
    with ExitStack() as ctx:
        c = Core(nc, ctx, "routing")
        G, E, N, T16 = N_GRP, PER_GRP, N_EXP, TILES
        BIG = 1e30

        g3, gm, gi, goh = c.sb("grp_tmp", [P, T16, G]), c.sb("grp_max", [P, T16]), c.sb("grp_first", [P, T16]), c.sb("grp_hot", [P, T16, G])
        ge, pg = c.sb("grp_exp", [P, T16, G]), c.sb("p_grp", [P, T16])
        mix, sel, s3 = c.sb("grp_logits", [P, T16, G, E]), c.sb("selected", [P, T16, E]), c.sb("sel_tmp", [P, T16, E])
        v = [c.sb(f"top{j}", [P, T16]) for j in range(2)]
        vi = c.sb("top_first", [P, T16])
        hot = [c.sb(f"hot{j}", [P, T16, E]) for j in range(2)]
        M = [c.sb(f"mask{j}", [P, T16, G, E]) for j in range(3)]
        big4, big8 = c.sb("iota_grp", [P, G]), c.sb("iota_exp", [P, E])
        iota16, iota64, tok = c.sb("iota_blocks", [P, TILES]), c.sb("iota_all_blocks", [P, N_BLOCKS]), c.sb("token", [P, T16])
        tri = c.sb("before", [P, P])
        dv, e1 = c.sb("v_diff", [P, T16]), c.sb("v_exp", [P, T16])
        base, tot, slot = c.sb("tile_base", [P, T16, N]), c.sb("tile_total", [P, T16, N]), c.sb("slot_of", [P, T16, N])
        cnt, cmp1, nb, pend, pst = (c.sb("count", [P, N]), c.sb("count_cmp", [P, N, TILES]), c.sb("n_blocks", [P, N]), c.sb("end_block", [P, N]),
                                    c.sb("first_slot", [P, N]))
        used, rank, eo, endq = (c.sb(x, [P, N]) for x in ("used", "rank", "rank_tmp", "rank_end"))
        cmp2, be, pr = c.sb("block_cmp", [P, N_BLOCKS, N]), c.sb("block_exp", [P, N_BLOCKS]), c.sb("prod", [P, T16, N])
        dest = [c.sb(f"dest{j}", [P, T16]) for j in range(2)]
        zero, rows = c.sb("zero_rows", [N_BLOCKS, P]), c.sb("slot_rows", [N_BLOCKS, P])
        cum, total, turn = c.ps("cum", [P, T16 * N]), c.ps("total", [P, T16 * N]), c.ps("slot_turn", [P, N_BLOCKS])
        iota_ok, chain, act_ok, hot_mm, dest_ok = c.sem("iota_ok"), c.sem("chain"), c.sem("act_ok"), c.sem("hot_mm"), c.sem("dest_ok")
        tri0, zero_out, scattered, rows_in, turned, split_ok = (c.sem("tri0"), c.sem("zero_out"), c.sem("scattered"), c.sem("rows_in"),
                                                               c.sem("turned"), c.sem("hot_ok"))
        masks_ok = c.sem("masks_ok")
        block = ctx.enter_context(nc.Block())
        LG, LE = keep.logits[:, :, 0:G], keep.logits[:, :, G:G + N].rearrange("p t (g e) -> p t g e", g=G)
        flat = lambda x: x.rearrange("p t g e -> p (t g e)")
        by_exp = lambda x: x.rearrange("p t g e -> p t (g e)")

        @block.gpsimd
        def _(pool):
            pool.memset(tri[:, :], 1.0).then_inc(tri0, 1)
            pool.memset(zero[:, :], 0.0).then_inc(tri0, 1)
            pool.iota(big4[:, :], pattern=[[1, G]], base=0, channel_multiplier=0, allow_small_or_imprecise_dtypes=True).then_inc(iota_ok, 1)
            pool.iota(big8[:, :], pattern=[[1, E]], base=0, channel_multiplier=0, allow_small_or_imprecise_dtypes=True).then_inc(iota_ok, 1)
            pool.iota(iota16[:, :], pattern=[[SLOTS_BLOCK, TILES]], base=0, channel_multiplier=0,
                      allow_small_or_imprecise_dtypes=True).then_inc(iota_ok, 1)
            pool.iota(iota64[:, :], pattern=[[1, N_BLOCKS]], base=0, channel_multiplier=0,
                      allow_small_or_imprecise_dtypes=True).then_inc(iota_ok, 1)
            pool.iota(tok[:, :], pattern=[[P, T16]], base=0, channel_multiplier=1, allow_small_or_imprecise_dtypes=True).then_inc(iota_ok, 1)
            pool.wait_ge(tri0, 2)
            pool.affine_select(out=tri[:, :], in_=tri[:, :], compare_op=ALU.is_gt, fill=0.0, base=0, pattern=[[1, P]],
                               channel_multiplier=-1).then_inc(iota_ok, 1)
            pool.dma_start(ROWTOK.rearrange("(b p) o -> b (p o)", p=P), zero[:, :]).then_inc(zero_out, 16)
            pool.wait_ge(zero_out, 16)
            pool.wait_ge(dest_ok, 2)
            for j in range(2):
                for t in range(T16):
                    pool.indirect_dma_start(out=ROWTOK, out_offset=bass.IndirectOffsetOnAxis(ap=keep.dest[j][:, t:t + 1], axis=0),
                                            in_=tok[:, t:t + 1], in_offset=None).then_inc(scattered, 16)
            pool.wait_ge(scattered, 16 * 2 * T16)
            pool.dma_start(rows[:, :], ROWTOK.rearrange("(b p) o -> b (p o)", p=P)).then_inc(rows_in, 16)

        @block.scalar
        def _(act):
            act.wait_ge(split_ok, 1)
            act.activation(ge[:, :, :], g3[:, :, :], ACT.Exp).then_inc(act_ok, 1)
            act.wait_ge(split_ok, 2)
            act.activation(e1[:, :], dv[:, :], ACT.Exp).then_inc(act_ok, 1)

        @block.tensor
        def _(pe):
            pe.wait_ge(iota_ok, 6)
            pe.wait_ge(masks_ok, 1)
            pe.matmul(cum[:, :], tri[:, :], flat(M[2][:, :, :, :]), start=True, stop=True)
            pe.matmul(total[:, :], keep.ones[:, 0:P], flat(M[2][:, :, :, :]), start=True, stop=True).then_inc(hot_mm, 1)
            pe.wait_ge(rows_in, 16)
            pe.transpose(turn[:, :], rows[:, :], keep.ident[0:N_BLOCKS, 0:N_BLOCKS]).then_inc(turned, 1)

        @block.vector
        def _(dve):
            done = [0]

            def link(ins):
                done[0] += 1
                ins.then_inc(chain, 1)
                dve.wait_ge(chain, done[0])

            bt = lambda x, n: x[:, :, None].to_broadcast([P, T16, n])

            def first_of(dst_hot, vals, top, iota, first, tmp, n):
                link(dve.tensor_tensor(tmp, vals, bt(top, n), ALU.is_lt))
                link(dve.scalar_tensor_tensor(tmp, tmp, BIG, iota[:, None, :].to_broadcast([P, T16, n]), ALU.mult, ALU.add))
                link(dve.tensor_reduce(first, tmp, AX.X, ALU.min))
                link(dve.tensor_tensor(dst_hot, iota[:, None, :].to_broadcast([P, T16, n]), bt(first, n), ALU.is_equal))

            dve.wait_ge(iota_ok, 6)
            link(dve.tensor_reduce(gm[:, :], LG, AX.X, ALU.max))
            dve.tensor_tensor(g3[:, :, :], LG, bt(gm, G), ALU.subtract).then_inc(split_ok, 1)
            dve.wait_ge(act_ok, 1)
            link(dve.tensor_reduce(pg[:, :], ge[:, :, :], AX.X, ALU.add))
            link(dve.reciprocal(pg[:, :], pg[:, :]))
            first_of(goh[:, :, :], LG, gm, big4, gi[:, :], g3[:, :, :], G)
            link(dve.tensor_tensor(mix[:, :, :, :], LE, goh[:, :, :, None].to_broadcast([P, T16, G, E]), ALU.mult))
            link(dve.tensor_reduce(sel[:, :, :], mix[:, :, :, :].rearrange("p t g e -> p t e g"), AX.X, ALU.add))
            for j in range(2):
                link(dve.tensor_reduce(v[j][:, :], sel[:, :, :], AX.X, ALU.max))
                first_of(hot[j][:, :, :], sel[:, :, :], v[j], big8, vi[:, :], s3[:, :, :], E)
                if j == 0:
                    link(dve.scalar_tensor_tensor(sel[:, :, :], hot[0][:, :, :], -BIG, sel[:, :, :], ALU.mult, ALU.add))
                link(dve.tensor_tensor(M[j][:, :, :, :], goh[:, :, :, None].to_broadcast([P, T16, G, E]),
                                       hot[j][:, :, None, :].to_broadcast([P, T16, G, E]), ALU.mult))
            dve.tensor_tensor(flat(M[2][:, :, :, :]), flat(M[0][:, :, :, :]), flat(M[1][:, :, :, :]), ALU.add).then_inc(masks_ok, 1)
            dve.tensor_tensor(dv[:, :], v[1][:, :], v[0][:, :], ALU.subtract).then_inc(split_ok, 1)
            dve.wait_ge(act_ok, 2)
            link(dve.tensor_scalar(dv[:, :], e1[:, :], 1.0, None, ALU.add))
            link(dve.reciprocal(dv[:, :], dv[:, :]))
            link(dve.tensor_tensor(keep.weights[:, 0, :], dv[:, :], pg[:, :], ALU.mult))
            link(dve.tensor_tensor(keep.weights[:, 1, :], keep.weights[:, 0, :], e1[:, :], ALU.mult))
            dve.wait_ge(hot_mm, 1)
            link(dve.tensor_copy(tot[:, :, :].rearrange("p t e -> p (t e)"), total[:, :]))
            link(dve.memset(base[:, 0, :], 0.0))
            for t in range(1, T16):
                link(dve.tensor_tensor(base[:, t, :], base[:, t - 1, :], tot[:, t - 1, :], ALU.add))
            link(dve.tensor_tensor(cnt[:, :], base[:, T16 - 1, :], tot[:, T16 - 1, :], ALU.add))
            link(dve.tensor_tensor(cmp1[:, :, :], cnt[:, :, None].to_broadcast([P, N, TILES]),
                                   iota16[:, None, :].to_broadcast([P, N, TILES]), ALU.is_gt))
            link(dve.tensor_reduce(nb[:, :], cmp1[:, :, :], AX.X, ALU.add))
            link(dve.tensor_tensor_scan(pend[:, :], keep.ones[:, 0:N], nb[:, :], 0.0, ALU.mult, ALU.add))
            link(dve.tensor_tensor(pst[:, :], pend[:, :], nb[:, :], ALU.subtract))
            link(dve.tensor_scalar(pst[:, :], pst[:, :], float(SLOTS_BLOCK), None, ALU.mult))
            link(dve.tensor_tensor(slot[:, :, :].rearrange("p t e -> p (t e)"), cum[:, :], base[:, :, :].rearrange("p t e -> p (t e)"), ALU.add))
            link(dve.tensor_tensor(slot[:, :, :], slot[:, :, :], pst[:, None, :].to_broadcast([P, T16, N]), ALU.add))
            for j in range(2):
                link(dve.tensor_tensor(pr[:, :, :], slot[:, :, :], by_exp(M[j][:, :, :, :]), ALU.mult))
                link(dve.tensor_reduce(dest[j][:, :], pr[:, :, :], AX.X, ALU.add))
                dve.tensor_copy(keep.dest[j][:, :], dest[j][:, :]).then_inc(dest_ok, 1)
            allq = iota64[:, 0:N]
            link(dve.tensor_scalar(used[:, :], nb[:, :], 0.0, None, ALU.is_gt))
            link(dve.tensor_tensor_scan(rank[:, :], keep.ones[:, 0:N], used[:, :], 0.0, ALU.mult, ALU.add))
            link(dve.tensor_tensor(cmp2[:, 0:N, :], allq[:, :, None].to_broadcast([P, N, N]), rank[:, None, :].to_broadcast([P, N, N]), ALU.is_ge))
            link(dve.tensor_reduce(eo[:, :], cmp2[:, 0:N, :], AX.X, ALU.add))
            link(dve.tensor_scalar(eo[:, :], eo[:, :], float(N_EXP - 1), None, ALU.min))
            link(dve.tensor_copy(keep.rank_expert[:, :], eo[:, :]))
            link(dve.tensor_scalar(eo[:, :], rank[:, :], -1.0, None, ALU.add))
            link(dve.tensor_tensor(cmp2[:, 0:N, :], allq[:, :, None].to_broadcast([P, N, N]), eo[:, None, :].to_broadcast([P, N, N]), ALU.is_ge))
            link(dve.tensor_tensor(cmp2[:, 0:N, :], cmp2[:, 0:N, :], nb[:, None, :].to_broadcast([P, N, N]), ALU.mult))
            link(dve.tensor_reduce(endq[:, :], cmp2[:, 0:N, :], AX.X, ALU.add))
            link(dve.tensor_copy(keep.end_block[:, :], endq[:, :]))
            link(dve.tensor_tensor(cmp2[:, :, :], iota64[:, :, None].to_broadcast([P, N_BLOCKS, N]),
                                   endq[:, None, :].to_broadcast([P, N_BLOCKS, N]), ALU.is_ge))
            link(dve.tensor_reduce(be[:, :], cmp2[:, :, :], AX.X, ALU.add))
            link(dve.tensor_scalar(eo[:, 0:1], rank[:, N - 1:N], -1.0, None, ALU.add))
            link(dve.tensor_scalar(be[:, :], be[:, :], eo[:, 0:1], None, ALU.min))
            link(dve.tensor_copy(keep.block_rank[:, :], be[:, :]))
            link(dve.tensor_scalar(keep.block_place[:, :], keep.block_rank[:, :], 1, None, ALU.bitwise_and))
            link(dve.tensor_scalar(keep.block_even[:, :], keep.block_rank[:, :], N_EXP - 2, None, ALU.bitwise_and))
            link(dve.tensor_scalar(eo[:, 0:1], pend[:, N - 1:N], 0.5, None, ALU.mult))
            link(dve.tensor_scalar(be[:, 0:N_BLOCKS // 2 - 1], iota64[:, 1:N_BLOCKS // 2], eo[:, 0:1], None, ALU.is_lt))
            link(dve.tensor_reduce(eo[:, 1:2], be[:, 0:N_BLOCKS // 2 - 1], AX.X, ALU.add))
            link(dve.tensor_copy(keep.pairs_less_one[:, :], eo[:, 1:2]))
            dve.wait_ge(turned, 1)
            link(dve.tensor_copy(keep.slot_token[:, :], turn[:, :]))


def experts(nc, a, keep, H2, YG):
    with ExitStack() as ctx:
        c = Core(nc, ctx, "experts")
        KE = D_EXP // P
        wg, wu, wd = c.sb("w_gate", [P, 2, KD, D_EXP]), c.sb("w_up", [P, 2, KD, D_EXP]), c.sb("w_down", [P, 2, KE, D])

        def two(name, shape, dt=F32):
            return [c.sb(f"{name}{b}", list(shape), dt) for b in range(2)]
        idx, xg, xT, sg, hh, hT, yo = (two("slot_token", (P, 1), I32), two("rows", (P, D)), two("rows_turned", (P, KD, P)), two("silu", (P, D_EXP)),
                                       two("hidden", (P, D_EXP)), two("hidden_turned", (P, KE, P)), two("y_rows", (P, D)))
        xp = [c.ps(f"row_turn{h}", [P, 512]) for h in range(2)]
        gp, up, hp = c.ps("gate", [P, D_EXP]), c.ps("up", [P, D_EXP]), c.ps("hidden_turn", [P, 512])
        yp = [c.ps(f"down{h}", [P, 512]) for h in range(2)]
        gu_in, d_in = [c.sem(f"gate_up_in{b}") for b in range(2)], [c.sem(f"down_in{b}") for b in range(2)]
        x_in = [c.sem(f"x_in{b}") for b in range(2)]
        gather_go = c.sem("gather_go")
        all_stored, zero_ok, zero_out = c.sem("all_stored"), c.sem("zero_ok"), c.sem("zero_out")
        zero_rows = c.sb("zero_rows", [P, D])
        y_out = [c.sem(f"y_out{b}") for b in range(2)]
        names = ("idx_ok", "xturn_mm", "xturn_ok", "gate_mm", "up_mm", "silu_ok", "hid_ok", "hturn_mm", "hturn_ok",
                 "down_mm", "y_ok")
        (idx_ok, xturn_mm, xturn_ok, gate_mm, up_mm, silu_ok, hid_ok, hturn_mm, hturn_ok, down_mm,
         y_ok) = (c.sem(n) for n in names)
        block = ctx.enter_context(nc.Block())
        PAIRS_MAX = N_BLOCKS // 2

        def all_pairs(eng, body, last):
            less_one = eng.value_load(keep.pairs_less_one[0:1, 0:1], min_val=0, max_val=PAIRS_MAX - 1)
            with eng.Fori(0, PAIRS_MAX - 1) as i:
                with eng.If(i < less_one):
                    body(i)
            last(less_one)

        @block.sync
        def _(sp):
            sp.sem_inc(gu_in[1], 32)
            sp.sem_inc(d_in[1], 16)

            def expert(q):
                return sp.value_load(keep.rank_expert[0:1, ds(q, 1)], min_val=0, max_val=N_EXP - 1)

            def gate_up(e, s):
                for dst, src in ((wg, "moe_w_gate"), (wu, "moe_w_up")):
                    sp.dma_start(dst[:, s, :, :], a[src][0, ds(e, 1), :, :].rearrange("e (k p) n -> p (e k) n", p=P)).then_inc(gu_in[s], 16)

            def down(e, s):
                sp.dma_start(wd[:, s, :, :], a["moe_w_down"][0, ds(e, 1), :, :].rearrange("e (k p) n -> p (e k) n", p=P)).then_inc(d_in[s], 16)
            for s in range(2):
                e = expert(s)
                gate_up(e, s)
                down(e, s)
            with sp.Fori(0, N_EXP // 2 - 1) as i:
                for s in range(2):
                    e = expert(i * 2 + (2 + s))
                    end = sp.value_load(keep.end_block[0:1, ds(i * 2 + s, 1)], min_val=1, max_val=N_BLOCKS)
                    sp.wait_ge(up_mm, end)
                    gate_up(e, s)
                    sp.wait_ge(down_mm, end + 1)
                    down(e, s)
            for s in range(2):
                sp.wait_ge(gu_in[s], 32 * (N_EXP // 2 + s))
                sp.wait_ge(d_in[s], 16 * (N_EXP // 2 + s))
            less_one = sp.value_load(keep.pairs_less_one[0:1, 0:1], min_val=0, max_val=PAIRS_MAX - 1)
            sp.wait_ge(zero_ok, 1)
            with sp.Fori(0, PAIRS_MAX) as i:
                with sp.If(i > less_one):
                    for b in range(2):
                        sp.dma_start(YG[ds(i * 2 * P + b * P, P), :], zero_rows[:, :]).then_inc(zero_out, 16)
                with sp.If(i <= less_one):
                    sp.sem_inc(zero_out, 32)
            sp.wait_ge(zero_out, PAIRS_MAX * 32)

        @block.gpsimd
        def _(pool):
            pool.memset(zero_rows[:, :], 0.0).then_inc(zero_ok, 1)

            def gathers(i):
                for b in range(2):
                    pool.wait_ge(idx_ok, i * 2 + b + 1)
                    pool.wait_ge(xturn_mm, i * 2 + b + 1)
                    pool.sem_inc(gather_go, 1)
                    pool.indirect_dma_start(out=xg[b][:, :], out_offset=None, in_=H2,
                                            in_offset=bass.IndirectOffsetOnAxis(ap=idx[b][:, :], axis=0)).then_inc(x_in[b], 16)
            all_pairs(pool, gathers, gathers)

        @block.tensor
        def _(pe):
            pe.sem_inc(xturn_mm, 2)
            pe.sem_inc(down_mm, 1)

            def turn(n, i, b):
                pe.wait_ge(x_in[b], i * 16 + 16)
                pe.wait_ge(xturn_ok, n * 2 + 2)
                for k in range(KD):
                    mm = pe.transpose(xp[k // 4][:, (k % 4) * P:(k % 4 + 1) * P], xg[b][:, k * P:(k + 1) * P], keep.ident[:, :])
                mm.then_inc(xturn_mm, 1)

            def even_place(n):
                return (pe.value_load(keep.block_even[0:1, ds(n, 1)], min_val=0, max_val=N_EXP - 2),
                        pe.value_load(keep.block_place[0:1, ds(n, 1)], min_val=0, max_val=1))

            def hidden(n, b):
                even, s = even_place(n)
                pe.wait_ge(gu_in[0], even * 16 + 32)
                pe.wait_ge(gu_in[1], (even + s * 2) * 16 + 32)
                pe.wait_ge(xturn_ok, n * 2 + 4)
                pe.wait_ge(silu_ok, n + 1)
                for k in range(KD):
                    mm = pe.matmul(gp[:, :], xT[b][:, k, :], wg[:, ds(s, 1), k, :].rearrange("p s n -> p (s n)"), start=k == 0, stop=k == KD - 1)
                mm.then_inc(gate_mm, 1)
                pe.wait_ge(hid_ok, n + 1)
                for k in range(KD):
                    mm = pe.matmul(up[:, :], xT[b][:, k, :], wu[:, ds(s, 1), k, :].rearrange("p s n -> p (s n)"), start=k == 0, stop=k == KD - 1)
                mm.then_inc(up_mm, 1)

            def turn_hidden(n, b):
                pe.wait_ge(hid_ok, n + 2)
                pe.wait_ge(hturn_ok, n + 1)
                for k in range(KE):
                    mm = pe.transpose(hp[:, k * P:(k + 1) * P], hh[b][:, k * P:(k + 1) * P], keep.ident[:, :])
                mm.then_inc(hturn_mm, 1)

            def down(n, b):
                even, s = even_place(n)
                pe.wait_ge(d_in[0], even * 8 + 16)
                pe.wait_ge(d_in[1], (even + s * 2) * 8 + 16)
                pe.wait_ge(hturn_ok, n + 2)
                pe.wait_ge(y_ok, n * 2 + 2)
                for h in range(2):
                    for k in range(KE):
                        mm = pe.matmul(yp[h][:, :], hT[b][:, k, :], wd[:, ds(s, 1), k, h * 512:(h + 1) * 512].rearrange("p s n -> p (s n)"),
                                       start=k == 0, stop=k == KE - 1)
                mm.then_inc(down_mm, 1)

            def pair(i):
                hidden(i * 2 + 1, 1)
                turn_hidden(i * 2, 0)
                turn(i * 2 + 2, i + 1, 0)
                down(i * 2, 0)
                hidden(i * 2 + 2, 0)
                turn_hidden(i * 2 + 1, 1)
                turn(i * 2 + 3, i + 1, 1)
                down(i * 2 + 1, 1)

            def last_pair(i):
                hidden(i * 2 + 1, 1)
                turn_hidden(i * 2, 0)
                down(i * 2, 0)
                turn_hidden(i * 2 + 1, 1)
                down(i * 2 + 1, 1)
            turn(0, 0, 0)
            hidden(0, 0)
            turn(1, 0, 1)
            all_pairs(pe, pair, last_pair)

        @block.scalar
        def _(act):
            act.sem_inc(xturn_ok, 2)
            act.sem_inc(silu_ok, 1)
            act.sem_inc(hturn_ok, 1)
            for b in range(2):
                act.sem_inc(y_out[b], 16)

            def turned(n, b):
                act.wait_ge(xturn_mm, n + 3)
                for h in range(2):
                    act.activation(xT[b][:, 4 * h:4 * h + 4, :].rearrange("p k t -> p (k t)"), xp[h][:, :], ACT.Copy).then_inc(xturn_ok, 1)

            def silu(n, b):
                act.wait_ge(gate_mm, n + 1)
                act.activation(sg[b][:, :], gp[:, :], ACT.Silu).then_inc(silu_ok, 1)

            def hidden_turned(n, b):
                act.wait_ge(hturn_mm, n + 1)
                act.activation(hT[b][:, :, :].rearrange("p k t -> p (k t)"), hp[:, :], ACT.Copy).then_inc(hturn_ok, 1)

            def store(n, b):
                act.wait_ge(y_ok, n * 2 + 4)
                act.dma_start(YG[ds(n * P, P), :], yo[b][:, :]).then_inc(y_out[b], 16)

            def pair(i):
                silu(i * 2 + 1, 1)
                hidden_turned(i * 2, 0)
                turned(i * 2 + 2, 0)
                silu(i * 2 + 2, 0)
                store(i * 2, 0)
                hidden_turned(i * 2 + 1, 1)
                turned(i * 2 + 3, 1)
                store(i * 2 + 1, 1)

            def last_pair(i):
                silu(i * 2 + 1, 1)
                hidden_turned(i * 2, 0)
                store(i * 2, 0)
                hidden_turned(i * 2 + 1, 1)
                store(i * 2 + 1, 1)
                for b in range(2):
                    act.wait_ge(y_out[b], i * 16 + 32)
                act.sem_inc(all_stored, 1)
            turned(0, 0)
            silu(0, 0)
            turned(1, 1)
            all_pairs(act, pair, last_pair)

        @block.vector
        def _(dve):
            dve.sem_inc(hid_ok, 1)
            dve.sem_inc(y_ok, 2)

            def index(n, b):
                dve.tensor_scalar(idx[b][:, :], keep.slot_token[:, ds(n, 1)], 0.0, None, ALU.add).then_inc(idx_ok, 1)
            for b in range(2):
                index(b, b)

            def product(n, b):
                dve.wait_ge(up_mm, n + 1)
                dve.wait_ge(silu_ok, n + 2)
                dve.tensor_tensor(hh[b][:, :], sg[b][:, :], up[:, :], ALU.mult).then_inc(hid_ok, 1)

            def rows(n, i, b):
                dve.wait_ge(down_mm, n + 2)
                dve.wait_ge(y_out[b], i * 16 + 16)
                for h in range(2):
                    dve.tensor_copy(yo[b][:, h * 512:(h + 1) * 512], yp[h][:, :]).then_inc(y_ok, 1)

            def pair(i):
                for b in range(2):
                    index(i * 2 + (b + 2), b)
                    product(i * 2 + b + 1, 1 - b)
                    rows(i * 2 + b, i, b)

            def last_pair(i):
                product(i * 2 + 1, 1)
                for b in range(2):
                    rows(i * 2 + b, i, b)
            product(0, 0)
            all_pairs(dve, pair, last_pair)


def combine(nc, a, keep, MOD, X2, YG, out):
    with ExitStack() as ctx:
        c = Core(nc, ctx, "combine")

        def two(name, shape, dt=F32):
            return [c.sb(f"{name}{b}", list(shape), dt) for b in range(2)]
        gt, gf = c.sb("gt2_all", [P, D]), c.sb("final_g_all", [P, D])
        y0, y1, xt, ot, wt = two("y_first", (P, D)), two("y_second", (P, D)), two("x2", (P, D)), two("out", (P, D)), two("weights", (P, 2))
        idxs = [[c.sb(f"slot{j}{b}", [P, 1], I32) for j in range(2)] for b in range(2)]
        sq, ss, rt, rs, eps = c.sb("sq", [P, D]), c.sb("sum_sq", [P, 2]), c.sb("root", [P, 2]), c.sb("rstd", [P, 2]), c.sb("eps", [P, 1])
        gather_go = c.sem("gather_go")
        y_in, x_in, o_out = ([c.sem(f"{x}{b}") for b in range(2)] for x in ("y_in", "x_in", "o_out"))
        names = ("const_in", "cols_ok", "first_ok", "both_ok", "gated", "x3_ok", "sq_ok", "root_ok", "rstd_ok", "out_ok",
                 "eps_ok")
        (const_in, cols_ok, first_ok, both_ok, gated, x3_ok, sq_ok, root_ok, rstd_ok, out_ok,
         eps_ok) = (c.sem(n) for n in names)
        block = ctx.enter_context(nc.Block())

        @block.sync
        def _(sp):
            sp.dma_start(gf[:, :], a["final_norm_g"].rearrange("(o n) -> o n", o=1).to_broadcast([P, D])).then_inc(const_in, 16)
            sp.dma_start(gt[:, :], row_of(MOD, 5)).then_inc(const_in, 16)
            for b in range(2):
                sp.sem_inc(o_out[b], 16)
            for b in range(2):
                sp.dma_start(xt[b][:, :], X2[b * P:(b + 1) * P, :]).then_inc(x_in[b], 16)

            def store(n, b, row):
                sp.wait_ge(out_ok, n + 1)
                sp.dma_start(out[0][ds(row, P), :], ot[b][:, :]).then_inc(o_out[b], 16)
            with sp.Fori(0, TILES // 2 - 1) as i:
                for b in range(2):
                    store(i * 2 + b, b, i * (2 * P) + b * P)
                    sp.dma_start(xt[b][:, :], X2[ds(i * (2 * P) + (2 + b) * P, P), :]).then_inc(x_in[b], 16)
            for b in range(2):
                store(TILES - 2 + b, b, (TILES - 2 + b) * P)
            for b in range(2):
                sp.wait_ge(o_out[b], 16 + 16 * (TILES // 2))

        @block.gpsimd
        def _(pool):
            with pool.Fori(0, TILES // 2) as i:
                for b in range(2):
                    n = i * 2 + b
                    pool.wait_ge(cols_ok, n * 3 + 3)
                    pool.wait_ge(x3_ok, n + 1)
                    pool.sem_inc(gather_go, 1)
                    for j, y in enumerate((y0, y1)):
                        pool.indirect_dma_start(out=y[b][:, :], out_offset=None, in_=YG,
                                                in_offset=bass.IndirectOffsetOnAxis(ap=idxs[b][j][:, :], axis=0)).then_inc(y_in[b], 16)

        @block.scalar
        def _(act):
            act.wait_ge(eps_ok, 1)
            with act.Fori(0, TILES // 2) as i:
                for b in range(2):
                    n = i * 2 + b
                    act.wait_ge(y_in[b], i * 32 + 32)
                    act.activation(y0[b][:, :], y0[b][:, :], ACT.Copy, scale=wt[b][:, 0:1]).then_inc(first_ok, 1)
                    act.wait_ge(x3_ok, n + 3)
                    act.activation(sq[:, :], xt[b][:, :], ACT.Square, accum_out=ss[:, b:b + 1]).then_inc(sq_ok, 1)
                    act.wait_ge(sq_ok, n + 1)
                    act.activation(rt[:, b:b + 1], ss[:, b:b + 1], ACT.Sqrt, bias=eps[:, :], scale=1.0 / D).then_inc(root_ok, 1)

        @block.vector
        def _(dve):
            dve.memset(eps[:, :], NORM_EPS).then_inc(eps_ok, 1)
            dve.sem_inc(both_ok, 2)
            dve.sem_inc(x3_ok, 2)
            dve.wait_ge(const_in, 32)

            def columns(n, b):
                for j in range(2):
                    dve.tensor_scalar(idxs[b][j][:, :], keep.dest[j][:, ds(n, 1)], 0.0, None, ALU.add).then_inc(cols_ok, 1)
                w = keep.weights[:, :, ds(n, 1)].rearrange("p j n -> p (j n)")
                dve.tensor_scalar(wt[b][:, :], w, 1.0, None, ALU.mult).then_inc(cols_ok, 1)

            def tile(n, i, b, more):
                dve.wait_ge(first_ok, n + 1)
                dve.scalar_tensor_tensor(y0[b][:, :], y1[b][:, :], wt[b][:, 1:2], y0[b][:, :], ALU.mult, ALU.add).then_inc(both_ok, 1)
                dve.wait_ge(both_ok, n + 3)
                dve.tensor_tensor(y1[b][:, :], y0[b][:, :], gt[:, :], ALU.mult).then_inc(gated, 1)
                dve.wait_ge(gated, n + 1)
                dve.wait_ge(x_in[b], i * 16 + 16)
                dve.tensor_tensor(xt[b][:, :], xt[b][:, :], y1[b][:, :], ALU.add).then_inc(x3_ok, 1)
                dve.wait_ge(root_ok, n + 1)
                dve.reciprocal(rs[:, b:b + 1], rt[:, b:b + 1]).then_inc(rstd_ok, 1)
                dve.wait_ge(rstd_ok, n + 1)
                dve.wait_ge(o_out[b], i * 16 + 16)
                dve.scalar_tensor_tensor(ot[b][:, :], xt[b][:, :], rs[:, b:b + 1], gf[:, :], ALU.mult, ALU.mult).then_inc(out_ok, 1)
                if more:
                    columns(n + 2, b)
            for b in range(2):
                columns(b, b)
            with dve.Fori(0, TILES // 2 - 1) as i:
                for b in range(2):
                    tile(i * 2 + b, i, b, True)
            for b in range(2):
                tile(TILES - 2 + b, TILES // 2 - 1, b, False)


class Keep:

    def __init__(self, nc, ctx):
        c = Core(nc, ctx, "keep")
        self.ident = c.sb("ident", [P, P])
        self.ones = c.sb("ones", [P, 512])
        self.quarter = c.sb("quarter", [P, 4, 32])
        self.dirq = c.sb("dirq", [P, 4])
        self.modc = c.sb("mod_cols", [P, 48, 2])
        self.par = c.sb("par_cols", [P, N_PC])
        self.scale1 = c.sb("scale1", [P, 2, KD])
        self.mu_rest = c.sb("mu_rest", [P, MA])
        self.mu_dir = c.sb("mu_dir", [P, 6, MA])
        self.ka_rest = c.sb("ka_rest", [P, PAIRS])
        self.heads = c.sb("head_blocks", [P, P])
        self.restart = c.sb("chunk_restart", [P, 512])
        self.head_of = c.sb("head_of", [P, 2])
        self.logits = c.sb("router_logits", [P, TILES, N_GRP + N_EXP])
        self.weights = c.sb("expert_weights", [P, 2, TILES])
        self.dest = [c.sb(f"slot_of_choice{j}", [P, TILES], I32) for j in range(2)]
        self.rank_expert = c.sb("rank_expert", [P, N_EXP], I32)
        self.block_rank = c.sb("block_rank", [P, N_BLOCKS], I32)
        self.block_even = c.sb("block_even", [P, N_BLOCKS], I32)
        self.block_place = c.sb("block_place", [P, N_BLOCKS], I32)
        self.pairs_less_one = c.sb("pairs_less_one", [P, 1], I32)
        self.end_block = c.sb("end_block", [P, N_EXP], I32)
        self.slot_token = c.sb("slot_token", [P, N_BLOCKS])


def build(nc, a, out):
    def scratch(name, shape):
        return nc.dram_tensor(name, shape, F32, kind="Internal").ap()
    ZA, UU, GT = scratch("z_shifted", (MA, P, ALL)), scratch("u_gelu", (GROUPS_SG, P, SEQ)), scratch("gates", (2 * KD, P, SEQ))
    YB, OPS, Y = scratch("y_b", (GROUPS_SG, P, SEQ)), scratch("scan_operands", (STEPS, UNITS, P, OPW)), scratch("y_scan", (2, PAIRS, P, ALL))
    X2, H2 = scratch("x2", (SEQ, D)), scratch("h2", (SEQ, D))
    ROWTOK, YG = scratch("slot_to_token", (N_BLOCKS * SLOTS_BLOCK, 1)), scratch("expert_rows", (N_BLOCKS * SLOTS_BLOCK, D))
    MOD = scratch("modulation_rows", (2, 6 * D))
    with ExitStack() as ctx:
        keep = Keep(nc, ctx)
        modulation(nc, a, keep, MOD)
        with ExitStack() as rows:
            lat = [rows.enter_context(nc.sbuf_tensor(f"latents_{x}", [P, KD, SEQ], F32)) for x in ("high", "low")]
            with ExitStack() as context_rows:
                con = [context_rows.enter_context(nc.sbuf_tensor(f"context_{x}", [P, KD, CTX], F32)) for x in ("high", "low")]
                normalise(nc, a, keep, lat, con)
                project(nc, a, keep, lat, con, ZA, UU, GT)
            spatial_gate(nc, a, keep, lat, UU, YB)
        prepare(nc, a, keep, ZA, OPS)
        scan(nc, a, keep, ZA, OPS, Y)
        with nc.sbuf_tensor("merged", [P, KD, SEQ], F32) as merged:
            branches(nc, a, keep, ZA, Y, YB, GT, merged)
            residual(nc, a, keep, MOD, merged, X2, H2)
        routing(nc, a, keep, ROWTOK)
        experts(nc, a, keep, H2, YG)
        combine(nc, a, keep, MOD, X2, YG, out)


_INS = ("x", "c", "ctx", "c_ctx", "ada_w", "ada_b", "norm1_g", "norm2_g", "w_in", "shift_mu", "rwkv_w0", "rwkv_w_up", "rwkv_a0",
        "rwkv_a_up", "rwkv_g_up", "rwkv_k_k", "rwkv_k_a", "rwkv_r_k", "rwkv_ln_w", "rwkv_ln_b", "w_branch_a", "sg_ln_w", "sg_ln_b",
        "sg_w", "sg_b", "w_branch_b", "w_out", "moe_grp_w", "moe_grp_b", "moe_exp_w", "moe_exp_b", "moe_w_gate", "moe_w_up",
        "moe_w_down", "final_norm_g")


def kernel(**inputs):
    import concourse.bacc as bacc
    from concourse.bass_utils import run_bass_kernel_spmd

    nc = bacc.Bacc("TRN2", target_bir_lowering=False, num_devices=1)
    arrays = {f"in_{n}": np.ascontiguousarray(inputs[n]) for n in _INS}
    arrays["in_scan_masks"] = scan_masks()
    a = {n[3:]: nc.dram_tensor(n, v.shape, mybir.dt.from_np(v.dtype), kind="ExternalInput").ap() for n, v in arrays.items()}
    out = nc.dram_tensor("out", (1, SEQ, D), F32, kind="ExternalOutput").ap()
    build(nc, a, out)
    return run_bass_kernel_spmd(nc, [arrays], core_ids=[0]).results[0]["out"]
```
